# Optimizing a Trainium2 kernel written in Bass

```python
import math
import jax, jax.numpy as jnp
from jax import lax
import numpy as np

D_MODEL = 1024
BATCH = 1
SEQ = 256
DEPTH = 2
DEC_BATCH = 8
DEC_SEQ = 4
PAST_LEN = 1024
PAGE_SIZE = 128

N_SSM_LAYERS = (DEPTH + 1) // 2
N_ATTN_LAYERS = DEPTH // 2
SSM_P = 16
SSM_GROUPS = D_MODEL // SSM_P
SSM_N = 64
SSM_DT_MIN = 1e-3
SSM_DT_MAX = 1e-1
N_HEADS = 8
HEAD_DIM = 64
WINDOWS = (128, 512, 2048)
DILATIONS = (1, 4, 16)
N_GROUPS = len(WINDOWS)
ROPE_DIM = HEAD_DIM // 4
ROPE_THETA = 500000.0
PEER_HEADS = 8
PEER_N_KEYS = 128
PEER_N_EXPERTS = PEER_N_KEYS * PEER_N_KEYS
PEER_D_KEY = 128
PEER_TOPK = 16
PEER_TOKEN_BLOCK = 128
EPS = 1e-6
NEG_INF = -1e30

kernel_name = 'hybrid_s5_dilated_attn_peer_step'

def rms_norm(x, gain=None):
    x32 = x.astype(jnp.float32)
    y = x32 * lax.rsqrt(jnp.mean(x32 * x32, axis=-1, keepdims=True) + EPS)
    if gain is not None:
        y = y * gain.astype(jnp.float32)
    return y.astype(x.dtype)

def adaln_params(c, w, b):
    return jnp.split(jax.nn.silu(c) @ w + b, 6, axis=-1)

def modulate(x, gain, shift, scale):
    return rms_norm(x, gain) * (1.0 + scale[:, None, :]) + shift[:, None, :]

def rope_partial(x, pos):
    half = ROPE_DIM // 2
    inv = ROPE_THETA ** (-jnp.arange(half, dtype=jnp.float32) / half)
    ang = pos.astype(jnp.float32)[:, None] * inv[None, :]
    shp = (1, pos.shape[0]) + (1,) * (x.ndim - 3) + (half,)
    cos, sin = jnp.cos(ang).reshape(shp), jnp.sin(ang).reshape(shp)
    x32 = x.astype(jnp.float32)
    x1, x2 = x32[..., :half], x32[..., half:ROPE_DIM]
    out = jnp.concatenate([x1 * cos - x2 * sin, x1 * sin + x2 * cos, x32[..., ROPE_DIM:]], axis=-1)
    return out.astype(x.dtype)

def softmax_lse(s):
    m = jnp.max(s, axis=-1, keepdims=True)
    p = jnp.exp(s - m)
    den = jnp.sum(p, axis=-1, keepdims=True)
    return p / den, (m + jnp.log(den))[..., 0]

def _linear_recurrence_combine(e1, e2):
    a1, b1 = e1
    a2, b2 = e2
    return a1 * a2, a2 * b1 + b2

def s5_mixer(h, h0, lam_re, lam_im, log_dt, b_re, b_im, c_re, c_im, d_skip, w_glu):
    f32 = jnp.float32
    Bt, S, D = h.shape
    lam = lax.complex(lam_re.astype(f32), lam_im.astype(f32))
    dt = jnp.exp(log_dt.astype(f32))[:, None]
    a_bar = jnp.exp(lam * dt)
    b_bar = ((a_bar - 1.0) / lam)[..., None] * lax.complex(b_re.astype(f32), b_im.astype(f32))
    c_mat = lax.complex(c_re.astype(f32), c_im.astype(f32))
    u = h.astype(f32).reshape(Bt, S, SSM_GROUPS, SSM_P)
    bu = jnp.einsum('bsgp,gnp->bsgn', u.astype(jnp.complex64), b_bar)
    bu = bu.at[:, 0].add(a_bar[None] * h0)
    a = jnp.broadcast_to(a_bar[None, None], (1, S, SSM_GROUPS, SSM_N))
    _, states = lax.associative_scan(_linear_recurrence_combine, (a, bu), axis=1)
    y = jnp.real(jnp.einsum('bsgn,gpn->bsgp', states, c_mat)) \
        + d_skip.astype(f32).reshape(SSM_GROUPS, SSM_P) * u
    z = y.reshape(Bt, S, D).astype(h.dtype) @ w_glu
    out = z[..., :D] * jax.nn.sigmoid(z[..., D:])
    last = states[:, -1]
    return out, jnp.stack([jnp.real(last), jnp.imag(last)], axis=1).astype(h.dtype)

def qkv_heads(h, pos, w_qkv, q_gain, k_gain):
    Bt, S, _ = h.shape
    qkv = (h @ w_qkv).reshape(Bt, S, N_GROUPS, 3, N_HEADS, HEAD_DIM)
    q = rope_partial(rms_norm(qkv[:, :, :, 0], q_gain), pos)
    k = rope_partial(rms_norm(qkv[:, :, :, 1], k_gain), pos)
    return q, k, qkv[:, :, :, 2]

def band_attention(q, k, v, dil, n_back):
    Bt, S, H, E = q.shape
    L = S // dil
    nb = -(-L // n_back)
    Lp = nb * n_back

    def sub(t):
        t = t.reshape(Bt, L, dil, H, E).transpose(0, 2, 1, 3, 4)
        return jnp.pad(t, ((0, 0), (0, 0), (0, Lp - L), (0, 0), (0, 0)))

    def band(t):
        t = jnp.pad(sub(t), ((0, 0), (0, 0), (n_back, 0), (0, 0), (0, 0)))
        t = t.reshape(Bt, dil, nb + 1, n_back, H, E)
        return jnp.concatenate([t[:, :, :-1], t[:, :, 1:]], axis=3)

    qs = sub(q).reshape(Bt, dil, nb, n_back, H, E)
    kb, vb = band(k), band(v)
    s = jnp.einsum('brnqhe,brnkhe->brnhqk', qs, kb, preferred_element_type=jnp.float32) * (E ** -0.5)
    iq = jnp.arange(n_back)[:, None]
    ik = jnp.arange(2 * n_back)[None, :]
    dist = iq + n_back - ik
    key_sub = jnp.arange(nb)[:, None, None] * n_back + ik - n_back
    mask = (dist >= 0) & (dist <= n_back) & (key_sub >= 0)
    s = jnp.where(mask[None, None, :, None], s, NEG_INF)
    p, lse = softmax_lse(s)
    o = jnp.einsum('brnhqk,brnkhe->brnqhe', p, vb.astype(jnp.float32))
    o = o.reshape(Bt, dil, Lp, H, E)[:, :, :L].transpose(0, 2, 1, 3, 4).reshape(Bt, S, H, E)
    lse = lse.transpose(0, 1, 2, 4, 3).reshape(Bt, dil, Lp, H)[:, :, :L]
    lse = lse.transpose(0, 2, 1, 3).reshape(Bt, S, H)
    return o, lse

def strided_gather_attention(q, k_new, v_new, k_buf, v_buf, dil, n_back):
    W, T, E = k_buf.shape[1], q.shape[1], q.shape[-1]
    k_ext = jnp.concatenate([k_buf, k_new.astype(k_buf.dtype)], axis=1)
    v_ext = jnp.concatenate([v_buf, v_new.astype(v_buf.dtype)], axis=1)
    idx = W + jnp.arange(T)[:, None] - dil * jnp.arange(n_back + 1)[None, :]
    valid = idx >= 0
    idx = jnp.maximum(idx, 0)
    kg, vg = k_ext[:, idx], v_ext[:, idx]
    s = jnp.einsum('bthe,btjhe->bhtj', q, kg.astype(q.dtype), preferred_element_type=jnp.float32) * (E ** -0.5)
    s = jnp.where(valid[None, None], s, NEG_INF)
    p, lse = softmax_lse(s)
    o = jnp.einsum('bhtj,btjhe->bthe', p, vg.astype(jnp.float32))
    return o, lse.transpose(0, 2, 1)

def merge_groups(outs, lses, w_o, dtype):
    wts = jax.nn.softmax(jnp.stack(lses, axis=0), axis=0)
    o = jnp.sum(wts[..., None] * jnp.stack(outs, axis=0), axis=0)
    Bt, S = o.shape[:2]
    return o.reshape(Bt, S, N_HEADS * HEAD_DIM).astype(dtype) @ w_o

def dilated_attn_prompt(h, pos, w_qkv, q_gain, k_gain, w_o):
    S = h.shape[1]
    q, k, v = qkv_heads(h, pos, w_qkv, q_gain, k_gain)
    outs, lses, kv_rows = [], [], []
    for g in range(N_GROUPS):
        o, l = band_attention(q[:, :, g], k[:, :, g], v[:, :, g], DILATIONS[g], WINDOWS[g] // DILATIONS[g])
        outs.append(o)
        lses.append(l)
        keep = min(WINDOWS[g], S)
        kv_rows.append(jnp.stack([k[:, S - keep:, g], v[:, S - keep:, g]], axis=1))
    return merge_groups(outs, lses, w_o, h.dtype), kv_rows

def dilated_attn_sample(h, pos, bufs, w_qkv, q_gain, k_gain, w_o):
    q, k, v = qkv_heads(h, pos, w_qkv, q_gain, k_gain)
    outs, lses, kv_rows = [], [], []
    for g in range(N_GROUPS):
        buf = bufs[g]
        o, l = strided_gather_attention(q[:, :, g], k[:, :, g], v[:, :, g], buf[:, 0], buf[:, 1],
                                        DILATIONS[g], WINDOWS[g] // DILATIONS[g])
        outs.append(o)
        lses.append(l)
        kv_rows.append(jnp.stack([k[:, :, g], v[:, :, g]], axis=1))
    return merge_groups(outs, lses, w_o, h.dtype), kv_rows

def peer_ffn(h, w_q, sub_keys, u_tab, v_tab):
    Bt, S, D = h.shape
    t = h.reshape(Bt * S, D)
    n = t.shape[0]
    q = rms_norm((t @ w_q).reshape(n, PEER_HEADS, 2, PEER_D_KEY // 2))
    s = jnp.einsum('thcd,hckd->thck', q, sub_keys, preferred_element_type=jnp.float32)
    v1, i1 = lax.top_k(s[:, :, 0], PEER_TOPK)
    v2, i2 = lax.top_k(s[:, :, 1], PEER_TOPK)
    cand = (v1[..., :, None] + v2[..., None, :]).reshape(n, PEER_HEADS, PEER_TOPK * PEER_TOPK)
    cidx = (i1[..., :, None] * PEER_N_KEYS + i2[..., None, :]).reshape(n, PEER_HEADS, PEER_TOPK * PEER_TOPK)
    best, sel = lax.top_k(cand, PEER_TOPK)
    eidx = jnp.take_along_axis(cidx, sel, axis=-1)
    gates = jax.nn.softmax(best, axis=-1)
    nb = -(-n // PEER_TOKEN_BLOCK)
    pad = nb * PEER_TOKEN_BLOCK - n
    tp = jnp.pad(t, ((0, pad), (0, 0))).reshape(nb, PEER_TOKEN_BLOCK, D)
    ep = jnp.pad(eidx, ((0, pad), (0, 0), (0, 0))).reshape(nb, PEER_TOKEN_BLOCK, PEER_HEADS, PEER_TOPK)
    gp = jnp.pad(gates, ((0, pad), (0, 0), (0, 0))).reshape(nb, PEER_TOKEN_BLOCK, PEER_HEADS, PEER_TOPK)

    def block(args):
        tb, eb, gb = args
        act = jax.nn.gelu(jnp.einsum('td,thkd->thk', tb, u_tab[eb], preferred_element_type=jnp.float32),
                          approximate=False)
        return jnp.einsum('thk,thkd->td', (gb * act).astype(tb.dtype), v_tab[eb])

    y = lax.map(block, (tp, ep, gp)).reshape(nb * PEER_TOKEN_BLOCK, D)[:n]
    return y.reshape(Bt, S, D)

def setup_inputs(seed: int = 0) -> dict:
    key = jax.random.key(seed)
    keys = iter(jax.random.split(key, 40))
    f32 = jnp.float32
    D = D_MODEL
    A = N_HEADS * HEAD_DIM

    def nrm(shape, scale=1.0):
        return jax.random.normal(next(keys), shape, f32) * scale

    n_buf = [min(w, PAST_LEN) for w in WINDOWS]
    lam_im0 = jnp.pi * jnp.arange(SSM_N, dtype=f32)
    kv_shape = lambda w: (N_ATTN_LAYERS, DEC_BATCH, 2, w, N_HEADS, HEAD_DIM)
    return {
        'x_prompt': nrm((BATCH, SEQ, D)),
        'x_sample': nrm((DEC_BATCH, DEC_SEQ, D)),
        'c_prompt': nrm((BATCH, D)),
        'c_sample': nrm((DEC_BATCH, D)),
        'state_ssm': nrm((N_SSM_LAYERS, DEC_BATCH, 2, SSM_GROUPS, SSM_N), 0.1),
        'cache_kv_w128': nrm(kv_shape(n_buf[0])),
        'cache_kv_w512': nrm(kv_shape(n_buf[1])),
        'cache_kv_w2048': nrm(kv_shape(n_buf[2])),
        'norm_mix': 1.0 + nrm((DEPTH, D), 0.05),
        'norm_ffn': 1.0 + nrm((DEPTH, D), 0.05),
        'ada_w': nrm((DEPTH, D, 6 * D), 0.5 * D ** -0.5),
        'ada_b': nrm((DEPTH, 6 * D), 0.02),
        'ssm_lam_re': -0.5 + nrm((N_SSM_LAYERS, SSM_GROUPS, SSM_N), 0.01),
        'ssm_lam_im': lam_im0 + nrm((N_SSM_LAYERS, SSM_GROUPS, SSM_N), 0.01),
        'ssm_log_dt': jax.random.uniform(next(keys), (N_SSM_LAYERS, SSM_GROUPS), f32,
                                         math.log(SSM_DT_MIN), math.log(SSM_DT_MAX)),
        'ssm_b_re': nrm((N_SSM_LAYERS, SSM_GROUPS, SSM_N, SSM_P), (2 * SSM_P) ** -0.5),
        'ssm_b_im': nrm((N_SSM_LAYERS, SSM_GROUPS, SSM_N, SSM_P), (2 * SSM_P) ** -0.5),
        'ssm_c_re': nrm((N_SSM_LAYERS, SSM_GROUPS, SSM_P, SSM_N), (2 * SSM_N) ** -0.5),
        'ssm_c_im': nrm((N_SSM_LAYERS, SSM_GROUPS, SSM_P, SSM_N), (2 * SSM_N) ** -0.5),
        'ssm_d': nrm((N_SSM_LAYERS, D)),
        'ssm_w_glu': nrm((N_SSM_LAYERS, D, 2 * D), D ** -0.5),
        'attn_w_qkv': nrm((N_ATTN_LAYERS, D, N_GROUPS * 3 * A), D ** -0.5),
        'attn_q_norm': 1.0 + nrm((N_ATTN_LAYERS, HEAD_DIM), 0.05),
        'attn_k_norm': 1.0 + nrm((N_ATTN_LAYERS, HEAD_DIM), 0.05),
        'attn_w_o': nrm((N_ATTN_LAYERS, A, D), A ** -0.5),
        'peer_w_q': nrm((DEPTH, D, PEER_HEADS * PEER_D_KEY), D ** -0.5),
        'peer_sub_keys': nrm((DEPTH, PEER_HEADS, 2, PEER_N_KEYS, PEER_D_KEY // 2), (PEER_D_KEY // 2) ** -0.5),
        'peer_u': nrm((DEPTH, PEER_N_EXPERTS, D), D ** -0.5),
        'peer_v': nrm((DEPTH, PEER_N_EXPERTS, D), 0.5),
    }

def reference(x_prompt, x_sample, c_prompt, c_sample, state_ssm, cache_kv_w128, cache_kv_w512,
              cache_kv_w2048, norm_mix, norm_ffn, ada_w, ada_b, ssm_lam_re, ssm_lam_im, ssm_log_dt,
              ssm_b_re, ssm_b_im, ssm_c_re, ssm_c_im, ssm_d, ssm_w_glu, attn_w_qkv, attn_q_norm,
              attn_k_norm, attn_w_o, peer_w_q, peer_sub_keys, peer_u, peer_v):
    f32 = jnp.float32
    S, T = x_prompt.shape[1], x_sample.shape[1]
    pos_p = jnp.arange(S, dtype=jnp.int32)
    pos_s = PAST_LEN + jnp.arange(T, dtype=jnp.int32)
    sample_bufs = (cache_kv_w128, cache_kv_w512, cache_kv_w2048)
    h0_p = jnp.zeros((x_prompt.shape[0], SSM_GROUPS, SSM_N), jnp.complex64)
    xp, xs = x_prompt, x_sample
    ssm_new_p, ssm_new_s = [], []
    kv_new_p = [[] for _ in range(N_GROUPS)]
    kv_new_s = [[] for _ in range(N_GROUPS)]
    for i in range(DEPTH):
        j = i // 2
        mp = adaln_params(c_prompt, ada_w[i], ada_b[i])
        ms = adaln_params(c_sample, ada_w[i], ada_b[i])
        hp = modulate(xp, norm_mix[i], mp[0], mp[1])
        hs = modulate(xs, norm_mix[i], ms[0], ms[1])
        if i % 2 == 0:
            sw = (ssm_lam_re[j], ssm_lam_im[j], ssm_log_dt[j], ssm_b_re[j], ssm_b_im[j],
                  ssm_c_re[j], ssm_c_im[j], ssm_d[j], ssm_w_glu[j])
            h0_s = lax.complex(state_ssm[j, :, 0].astype(f32), state_ssm[j, :, 1].astype(f32))
            op, st_p = s5_mixer(hp, h0_p, *sw)
            os_, st_s = s5_mixer(hs, h0_s, *sw)
            ssm_new_p.append(st_p)
            ssm_new_s.append(st_s)
        else:
            aw = (attn_w_qkv[j], attn_q_norm[j], attn_k_norm[j], attn_w_o[j])
            op, kv_p = dilated_attn_prompt(hp, pos_p, *aw)
            os_, kv_s = dilated_attn_sample(hs, pos_s, [b[j] for b in sample_bufs], *aw)
            for g in range(N_GROUPS):
                kv_new_p[g].append(kv_p[g])
                kv_new_s[g].append(kv_s[g])
        xp = xp + mp[2][:, None, :] * op
        xs = xs + ms[2][:, None, :] * os_
        pw = (peer_w_q[i], peer_sub_keys[i], peer_u[i], peer_v[i])
        xp = xp + mp[5][:, None, :] * peer_ffn(modulate(xp, norm_ffn[i], mp[3], mp[4]), *pw)
        xs = xs + ms[5][:, None, :] * peer_ffn(modulate(xs, norm_ffn[i], ms[3], ms[4]), *pw)
    return (xp, xs,
            jnp.stack(ssm_new_p), jnp.stack(kv_new_p[0]), jnp.stack(kv_new_p[1]), jnp.stack(kv_new_p[2]),
            jnp.stack(ssm_new_s), jnp.stack(kv_new_s[0]), jnp.stack(kv_new_s[1]), jnp.stack(kv_new_s[2]))


_drawn_inputs = setup_inputs


def setup_inputs(seed=0):
    import zlib

    import numpy as np

    out = dict(_drawn_inputs(seed))
    spreads = {}
    factors = {'cache_kv_w128': 2.892,
     'cache_kv_w512': 2.846,
     'cache_kv_w2048': 3.813,
     'ssm_lam_re': 4.882,
     'ssm_c_re': 3.132,
     'ssm_c_im': 3.062,
     'attn_q_norm': 8.0}
    for name, (base, spread) in spreads.items():
        noise = np.random.default_rng([zlib.crc32(name.encode()), seed]).standard_normal(out[name].shape)
        drawn = base * np.exp(spread * noise) if base else spread * noise
        out[name] = __import__('jax').numpy.asarray(drawn.astype(out[name].dtype))
    for name, factor in factors.items():
        out[name] = (out[name] * factor).astype(out[name].dtype)
    return out
```

```python
from contextlib import ExitStack

import concourse.bass as bass
from concourse import mybir

P = 128
D = 1024
NC = D // P
SP_, SB, ST = 256, 8, 4
T = SP_ + SB * ST
ROWS = 1 + SB
L = 2
G64, SN = 64, 64
PAIRS = G64 // 2
H, E = 8, 64
HP = H // 2
NG = 3
WIN, DIL, PAST = (128, 512, 2048), (1, 4, 16), 1024
NK = (128, 512, 256)
KOFF = (512, 0, 640)
CK = sum(NK)
NEWC = CK
SW = CK + NG * 32
PH, NKEYS, TOPK = 8, 128, 16
UNITS = 18
EPS = 1e-6
RING = 4

ADA, GLU, PQ = 0, 96, (112, 416)
UT, VT = (120, 424), (248, 552)
QK, VP, WO, TILES = 376, 400, 412, 680
NB0 = 48

F32 = mybir.dt.float32
U32 = mybir.dt.uint32
ALU = mybir.AluOpType
ACT = mybir.ActivationFunctionType
X = mybir.AxisListType.X
TWO_PI = 6.283185307179586
C1 = 6.28125
C2 = 0.0019350051879882812
C3 = 3.019916050e-07
MAGIC = 12582912.0
PI_LO = 3.1415925


class Count:

    def __init__(self, eng, sem):
        self.eng, self.sem, self.n = eng, sem, 0

    def __call__(self, ins):
        self.n += 1
        ins.then_inc(self.sem, 1)

    def settle(self):
        self.eng.wait_ge(self.sem, self.n)


def build(nc, I, O):
    ctx = ExitStack()
    with ctx:
        def sb(name, words, dt=F32):
            return ctx.enter_context(nc.sbuf_tensor(name, [P, words], dt))

        def sem(name):
            return ctx.enter_context(nc.semaphore(name))

        big = sb("big", 128 * T)
        ring = ctx.enter_context(nc.sbuf_tensor("ring", [P, RING, 1024], F32))
        xT_t, hT_t = sb("xT", NC * T), sb("hT", NC * T)
        xT = xT_t[:, :].rearrange("p (c t) -> p c t", c=NC)
        hT = hT_t[:, :].rearrange("p (c t) -> p c t", c=NC)
        ada_t = sb("ada", L * 48 * ROWS)
        ada = ada_t[:, :].rearrange("p (l j c r) -> p l j c r", l=L, j=6, c=NC)
        consts = sb("consts", 5 * 128 + 10)
        ones = consts[:, 0:128]
        blk64 = consts[:, 128:256]
        ident = consts[:, 256:384]
        rotm = consts[:, 384:512]
        iota = consts[:, 512:640]
        gmask = consts[:, 640:648]
        qg, kg = consts[:, 648:649], consts[:, 649:650]
        ccol = sb("ccol", NC * ROWS)
        bias_t = sb("bias", L * 48)
        gain_t = sb("gain", 2 * L * NC)
        eps_c = sb("eps_c", 1)
        rstd = sb("rstd", T)
        idx_t = sb("idx", 3 * T)
        idx = idx_t[:, :].rearrange("p (q t) -> p q t", q=3)
        gtmp = sb("gtmp", 2 * T)
        oh_t = sb("oh", 4 * 512)
        oh = oh_t[:, :].rearrange("p (w b t k) -> p w b t k", w=2, b=2, t=4)
        smask = sb("smask", T)
        small = sb("small", 600)
        r_col = small[:, 0:PAIRS]
        h0 = small[:, 32:544].rearrange("p (z k b) -> p z k b", z=2, k=PAIRS)
        dskip = small[:, 544:552]
        st_t = idx_t[:, 0:2 * PAIRS * ROWS]
        st = st_t.rearrange("p (z k r) -> p z k r", z=2, k=PAIRS)
        ps = ctx.enter_context(nc.psum_tensor("ps", [P, 8, 512], F32))

        class Region:

            def __init__(self, at=0):
                self.at = at

            def take(self, words):
                a = big[:, self.at:self.at + words]
                self.at += words
                assert self.at <= 128 * T, self.at
                return a

        W = big[:, :].rearrange("p (j t) -> p j t", j=128)
        rg = Region(NB0 * T)
        s_sb = rg.take(UNITS * 256)
        cand = rg.take(UNITS * 256)
        eq = rg.take(UNITS * 256)
        s_two = eq
        qraw_t = cand
        qraw = qraw_t[:, 0:NC * T].rearrange("p (c t) -> p c t", c=NC)
        qsq_t = eq
        qsq = qsq_t[:, 0:NC * T].rearrange("p (c t) -> p c t", c=NC)
        qrs = eq[:, NC * T:2 * NC * T].rearrange("p (c t) -> p c t", c=NC)
        v16 = rg.take(2 * UNITS * 16).rearrange("p (u z a) -> p u z a", u=UNITS, z=2)
        i16f = rg.take(2 * UNITS * 16).rearrange("p (u z a) -> p u z a", u=UNITS, z=2)
        i16u_f = rg.take(2 * UNITS * 16)
        i16u = i16u_f.bitcast(U32).rearrange("p (u z a) -> p u z a", u=UNITS, z=2)
        best = rg.take(UNITS * 16).rearrange("p (u k) -> p u k", u=UNITS)
        selu = rg.take(UNITS * 16).bitcast(U32).rearrange("p (u k) -> p u k", u=UNITS)
        selabu = rg.take(2 * UNITS * 16).bitcast(U32).rearrange("p (z u k) -> p z u k", z=2, u=UNITS)
        selab = rg.take(2 * UNITS * 16).rearrange("p (z u k) -> p z u k", z=2, u=UNITS)
        sel3 = rg.take(3 * UNITS * 16).rearrange("p (q u k) -> p q u k", q=3, u=UNITS)
        selz = rg.take(3 * 128).rearrange("p (q s) -> p q s", q=3)
        gsum = rg.take(2 * UNITS)
        hqm = rg.take(4)
        jsel = rg.take(32)
        subk_t = rg.take(PH * NKEYS)
        subk = subk_t.rearrange("p (h k) -> p h k", h=PH)
        modsq = big[:, 128 * T - NC * T:128 * T].rearrange("p (c t) -> p c t", c=NC)

        rs = Region()
        tcos = rs.take(PAIRS * T).rearrange("p (k t) -> p k t", k=PAIRS)
        tsin = rs.take(PAIRS * T).rearrange("p (k t) -> p k t", k=PAIRS)
        bb_re = rs.take(4096).rearrange("p (c g n) -> p c g n", c=NC, g=8)
        bb_im_f = rs.take(4096)
        bb_im = bb_im_f.rearrange("p (c g n) -> p c g n", c=NC, g=8)
        cb = rs.take(3 * 1024).rearrange("p (z k m) -> p z k m", z=3, k=PAIRS)
        ring5 = rs.at
        LW = 512 + PAIRS
        lre, lim, ldt = rs.take(LW), rs.take(LW), rs.take(LW)
        sth, sq1, ssin, scos, sr, st1 = (rs.take(LW) for _ in range(6))
        sbre, sbim = rs.take(512), rs.take(512)
        assert rs.at <= 128 * T
        r5 = Region(ring5)
        m5 = [r5.take(4 * T).rearrange("p (q t) -> p q t", q=4) for _ in range(2)]
        zin = [r5.take(2 * T).rearrange("p (q t) -> p q t", q=2) for _ in range(2)]
        z5 = zin
        o5 = [r5.take(4 * T).rearrange("p (q t) -> p q t", q=4) for _ in range(2)]
        rm5 = [r5.take(T) for _ in range(2)]

        hr5 = [small[:, 552 + 16 * n:568 + 16 * n].rearrange("p (z b) -> p z b", z=2) for n in range(2)]

        ra = Region()
        qk = ra.take(24 * T).rearrange("p (m t) -> p m t", m=24)
        v_sb = ra.take(9 * 512).rearrange("p (a g n) -> p a g n", a=3, g=NG)
        rope = ra.take(2 * T).rearrange("p (z t) -> p z t", z=2)
        pmask = ra.take(384 + 768)
        smaskv = ra.take(SW + 96)
        qz_t = ra.take(NG * SB * HP * 32)
        qz = qz_t.rearrange("p (g b q h t) -> p g b q h t", g=NG, b=SB, q=HP, h=H)
        o_tok = ra.take(512)
        oT = ra.take(HP * T).rearrange("p (q t) -> p q t", q=HP)
        sst = ra.take(64)
        tmp0 = ra.at
        asq = ra.take(4 * T).rearrange("p (m t) -> p m t", m=4)
        ars = ra.take(4 * T).rearrange("p (m t) -> p m t", m=4)
        rb = Region(tmp0)
        p_sb = [rb.take(768) for _ in range(2)]
        pt_sb = rb.take(768)
        ps_s = rb.take(SW)
        pts = rb.take(7 * 128).rearrange("p (k r) -> p k r", k=7)
        ptn = rb.take(3 * 128).rearrange("p (g r) -> p g r", g=3)
        kv_buf = [rb.take(4 * CK) for _ in range(3)]

        S = {n: sem(n) for n in (
            "tile_done in_setup in_s5 in_att in_kv0 in_kv1 in_kv2 kv_used v_own a_own p_own silu_c "
            "ada_done sq_ready ms_ready std_ready h_ready s5_trig s5_thr s5_bb s5_tab s5_bu s5_rot s5_rm s5_zin s5_z "
            "s5_op s5_cs s5_ymm s5_hy glu_sig glu_used st_ready x_ready q_copied qsq_ready qms_ready qsd_ready "
            "qn_ready sc_mm sc_copied gate_in gate_exp sel_ready sel_t idx_ready gb_o1 gb_df gb_sq gb_o2 gb_mm gb_mul gb_cp "
            "gelu_done w_done aq_copied aq_sq aq_ms aq_sd aq_qn aq_rot aq_done v_copied qz_ready "
            "us_mm us_max us_exp us_t us_cpa us_cpv us_pv us_o ot_mm ot_cp ss_mm ss_max ss_exp ss_t ss_cp "
            "ss_norm ss_pv oT_ready out_done st_out kv_out glu_used_v").split()}
        tile_in = [sem(f"tile_in{s}") for s in range(RING)]

        def tile_wait(eng, n, i=0):
            eng.wait_ge(tile_in[n % RING], 16 * i + 16 * (n // RING + 1))

        block = ctx.enter_context(nc.Block())

        @block.sync
        def _(sp):
            stream = I["stream"]
            for s in range(RING):
                sp.dma_start(ring[:, s, :], stream[s]).then_inc(tile_in[s], 16)
            with sp.Fori(1, TILES // RING) as i:
                for s in range(RING):
                    sp.wait_ge(S["tile_done"], RING * i + (s + 1 - RING))
                    sp.dma_start(ring[:, s, :], stream[bass.ds(RING * i + s, 1)].rearrange("a p n -> (a p) n"))\
                      .then_inc(tile_in[s], 16)
            sp.wait_ge(S["x_ready"], 3)
            sp.dma_start(O["yT"], xT_t[:, :]).then_inc(S["out_done"], 16)
            sp.wait_ge(S["out_done"], 16)
            sp.wait_ge(S["st_out"], 16)
            sp.wait_ge(S["kv_out"], 48)

        def peer_act(act, l):
            act.dma_start(subk_t, I["subk"][l]).then_inc(S["gate_in"], 16)
            act.dma_start(hqm, I["hqm"]).then_inc(S["gate_in"], 16)
            act.dma_start(jsel, I["jsel"]).then_inc(S["gate_in"], 16)
            for m in range(8):
                act.wait_ge(S["tile_done"], PQ[l] + m + 1)
                nc.scalar.activation(qraw[:, m, :], ps[:, m % 4, 0:T], ACT.Copy).then_inc(S["q_copied"], 1)

            def gelus(j0, j1):
                with act.Fori(j0 // 4, j1 // 4) as i:
                    for s in range(4):
                        act.wait_ge(S["tile_done"], 4 * i + (UT[l] + s + 1))
                        dst = W[:, bass.ds(4 * i + s, 1), :].rearrange("p a t -> p (a t)")
                        nc.scalar.activation(dst, ps[:, 6 + s % 2, 0:T], ACT.Gelu).then_inc(S["gelu_done"], 1)

            def q_root(n):
                act.wait_ge(S["qms_ready"], 2 * l + n + 1)
                nc.scalar.activation(qrs[:, 4 * n:4 * n + 4, :], ps[:, 0:4, 0:T], ACT.Sqrt, bias=eps_c[:, :],
                                     scale=1.0 / 64).then_inc(S["qsd_ready"], 1)

            def scores_out(n):
                act.wait_ge(S["sc_mm"], 3 * l + n + 1)
                u0, u1 = ((0, 8), (16, 18), (8, 16))[n]
                dst = s_sb.rearrange("p (u z k) -> p z u k", u=UNITS, z=2)[:, :, u0:u1, :]
                if n == 1:
                    src = ps[:, 4:6, 0:256].rearrange("p z (u k) -> p z u k", u=2)
                else:
                    src = ps[:, 0:4, :].rearrange("p (z a) (b k) -> p z (a b) k", z=2, b=4)
                nc.scalar.activation(dst, src, ACT.Copy).then_inc(S["sc_copied"], 1)

            gelus(0, 8)
            q_root(0)
            gelus(8, 12)
            q_root(1)
            gelus(12, 16)
            scores_out(0)
            scores_out(1)
            gelus(16, 20)
            scores_out(2)
            gelus(20, NB0)
            act.wait_ge(S["gate_exp"], 2 * l + 1)
            nc.scalar.activation(best, best, ACT.Exp).then_inc(S["gate_exp"], 1)
            for n in range(2):
                act.wait_ge(S["sel_t"], 3 * l + n + 1)
                nc.scalar.activation(idx[:, :, n * 128:(n + 1) * 128],
                                     ps[:, n, 0:384].rearrange("p (q t) -> p q t", q=3), ACT.Copy)\
                   .then_inc(S["idx_ready"], 1)
            act.wait_ge(S["sel_t"], 3 * l + 3)
            nc.scalar.activation(idx[:, :, 256:T], ps[:, 2, 0:96].rearrange("p (q t) -> p q t", q=3), ACT.Copy)\
               .then_inc(S["idx_ready"], 1)
            def onehot1(i, b):
                act.wait_ge(S["gb_sq"], 2 * i + (b + 1 + 72 * l))
                nc.scalar.activation(oh[:, 0, b], oh[:, 0, b], ACT.Relu, bias=1.0, scale=-1.0).then_inc(S["gb_o1"], 1)

            def gate_high(i, b):
                act.wait_ge(S["gb_mul"], 2 * i + (b + 1 + 72 * l))
                nc.scalar.activation(W[:, NB0:128, bass.ds(8 * i + 4 * b, 4)],
                                     ps[:, b, :].rearrange("p (t j) -> p j t", t=4)[:, NB0:128, :], ACT.Copy)\
                    .then_inc(S["gb_cp"], 1)

            onehot1(0, 0)
            onehot1(0, 1)
            gate_high(0, 0)
            with act.Fori(1, T // 8) as i:
                onehot1(i, 0)
                gate_high(i - 1, 1)
                onehot1(i, 1)
                gate_high(i, 0)
            gate_high(T // 8 - 1, 1)
            for s in range(4):
                act.wait_ge(S["tile_done"], UT[l] + NB0 + s + 1)
                if s >= 2:
                    act.wait_ge(S["w_done"], (128 - NB0) * l + s - 1)
                nc.scalar.activation(gtmp[:, (s % 2) * T:(s % 2 + 1) * T], ps[:, 6 + s % 2, 0:T], ACT.Gelu)\
                   .then_inc(S["gelu_done"], 1)
            with act.Fori(NB0 // 4 + 1, 32) as i:
                for s in range(4):
                    act.wait_ge(S["tile_done"], 4 * i + (UT[l] + s + 1))
                    act.wait_ge(S["w_done"], 4 * i + (s - 1 - NB0 + (128 - NB0) * l))
                    nc.scalar.activation(gtmp[:, (s % 2) * T:(s % 2 + 1) * T], ps[:, 6 + s % 2, 0:T], ACT.Gelu)\
                       .then_inc(S["gelu_done"], 1)

        def attention_act(act, own):
            act.wait_ge(S["tile_done"], VT[0] + 128)
            for dst, name in [(rope.rearrange("p z t -> p (z t)"), "rope"), (pmask, "pmask"), (smaskv, "smaskv")]:
                act.dma_start(dst, I[name]).then_inc(S["in_att"], 16)

            def load_kv(n):
                half, v, b = n // 8, n % 8 // 4, n // 8 * 4 + n % 4
                if n >= 3:
                    act.wait_ge(S["kv_used"], n - 2)
                act.dma_start(kv_buf[n % 3], I["vc" if v else "kc"][b]).then_inc(S[f"in_kv{n % 3}"], 16)

            for gs in range(6):
                act.wait_ge(S["tile_done"], QK + 4 * gs + 4)
                nc.scalar.activation(qk[:, 4 * gs:4 * gs + 4, :], ps[:, 0:4, 0:T], ACT.Copy)\
                   .then_inc(S["aq_copied"], 1)
                act.wait_ge(S["aq_ms"], gs + 1)
                nc.scalar.activation(ars, ps[:, 4:8, 0:T], ACT.Sqrt, bias=eps_c[:, :], scale=1.0 / E)\
                   .then_inc(S["aq_sd"], 1)
            for g in range(NG):
                act.wait_ge(S["tile_done"], VP + 4 * g + 4)
                nc.scalar.activation(v_sb[:, 0:2, g, :], ps[:, 0:2, :], ACT.Copy)
                nc.scalar.activation(v_sb[0:32, 2, g, :], ps[0:32, 2, :], ACT.Copy).then_inc(S["v_copied"], 1)
            act.wait_ge(S["aq_done"], 6)
            act.wait_ge(S["v_copied"], NG)
            act.dma_start(O["qk"], qk).then_inc(S["kv_out"], 16)
            act.dma_start(O["v"], v_sb[:, 0:2]).then_inc(S["kv_out"], 16)
            act.dma_start(O["v_s"], v_sb[0:32, 2]).then_inc(S["kv_out"], 16)
            for n in range(3):
                load_kv(n)
            nkv = [3]

            def more(n):
                while nkv[0] < n:
                    load_kv(nkv[0])
                    nkv[0] += 1

            def sample_exp(hf):
                act.wait_ge(S["ss_max"], hf + 1)
                nc.scalar.activation(ps_s, ps_s, ACT.Exp, bias=sst[:, 0:1], accum_out=sst[:, 1:2])\
                   .then_inc(S["ss_exp"], 1)

            def sample_t(hf):
                act.wait_ge(S["ss_t"], hf + 1)
                nc.scalar.activation(pts, ps[:, 2:4, :].rearrange("p b n -> p (b n)")[:, 0:CK]
                                     .rearrange("p (k r) -> p k r", k=7), ACT.Copy)
                nc.scalar.activation(ptn[0:32], ps[0:32, 5, 0:384].rearrange("p (g r) -> p g r", g=3), ACT.Copy)\
                   .then_inc(S["ss_cp"], 1)

            def unit_exp(u):
                qt = u // H
                w = 384 * (qt + 1)
                act.wait_ge(S["us_max"], u + 1)
                nc.scalar.activation(p_sb[u % 2][:, 0:w], p_sb[u % 2][:, 0:w], ACT.Exp, bias=sst[:, 4 + 3 * (u % 2):5 + 3 * (u % 2)],
                                     accum_out=sst[:, 5 + 3 * (u % 2):6 + 3 * (u % 2)]).then_inc(S["us_exp"], 1)

            def unit_t(u):
                qt = u // H
                act.wait_ge(S["us_t"], u + 1)
                if u:
                    act.wait_ge(S["us_pv"], u)
                w = 384 * (qt + 1)
                nc.scalar.activation(pt_sb[:, 0:w], ps[:, 2:4, :].rearrange("p b n -> p (b n)")[:, 0:w], ACT.Copy)\
                   .then_inc(S["us_cpa"], 1)

            for hf in range(2):
                more(8 * hf + 7)
                sample_exp(hf)
                unit_exp(8 * hf)
                for u in range(8 * hf, 8 * hf + 8):
                    if u % 8 < 7:
                        unit_exp(u + 1)
                    unit_t(u)
                sample_t(hf)
                more(min(8 * hf + 11, 16))

        @block.scalar
        def _(act):
            own = Count(act, S["a_own"])
            setup = [(ccol[:, :], "ccol"), (consts[:, :], "consts"), (gain_t[:, :], "gain"),
                     (bias_t[:, :], "bias"), (xT_t[:, :], "xT"), (smask[:, :], "smask"),
                     (small[:, 32:552], "h0d")]
            for dst, name in setup:
                act.dma_start(dst, I[name]).then_inc(S["in_setup"], 16)
            for dst, name in [(lre, "lre"), (lim, "lim"), (ldt, "ldt"), (sbre, "sbre"), (sbim, "sbim")]:
                act.dma_start(dst, I[name]).then_inc(S["in_s5"], 16)
            act.dma_start(cb[:, 0:2], I["cri"].rearrange("p (z k m) -> p z k m", z=2, k=PAIRS))\
               .then_inc(S["in_s5"], 16)
            act.wait_ge(S["in_setup"], 16 * 7)
            nc.scalar.activation(ccol[:, :], ccol[:, :], ACT.Silu).then_inc(S["silu_c"], 1)
            act.wait_ge(S["in_s5"], 16 * 6)
            nc.scalar.activation(ldt, ldt, ACT.Exp).then_inc(S["s5_trig"], 1)
            act.wait_ge(S["s5_thr"], 1)
            nc.scalar.activation(ssin, sth, ACT.Sin)
            nc.scalar.activation(scos, sth, ACT.Sin, scale=0.5).then_inc(S["s5_trig"], 1)
            act.wait_ge(S["s5_thr"], 2)
            nc.scalar.activation(sr, sr, ACT.Exp).then_inc(S["s5_trig"], 1)
            act.wait_ge(S["s5_tab"], 1)
            for z, (src, dst) in enumerate(((sbre, bb_re), (sbim, bb_im))):
                for gl in range(8):
                    ins = nc.scalar.activation(dst[:, :, gl, :], src.rearrange("p (c n) -> p c n", c=NC),
                                               ACT.Copy, scale=gmask[:, gl:gl + 1])
            ins.then_inc(S["s5_bb"], 1)

            def root_mean(q, bank=7):
                act.wait_ge(S["ms_ready"], q + 1)
                nc.scalar.activation(rstd[:, :], ps[:, bank, 0:T], ACT.Sqrt, bias=eps_c[:, :], scale=1.0 / D)\
                   .then_inc(S["std_ready"], 1)

            root_mean(0)
            act.wait_ge(S["s5_rm"], PAIRS)
            act.dma_start(O["st"], st_t).then_inc(S["st_out"], 16)
            def sigmoids(i, first):
                for m in range(2):
                    act.wait_ge(S["tile_done"], 4 * i + (GLU + 2 * m + 2))
                    if not first:
                        act.wait_ge(S["glu_used"], 2 * i + (m - 1))
                    nc.scalar.activation(gtmp[:, m * T:(m + 1) * T], ps[:, 2 * m + 1, 0:T], ACT.Sigmoid)\
                       .then_inc(S["glu_sig"], 1)

            sigmoids(0, True)
            with act.Fori(1, 4) as i:
                sigmoids(i, False)
            root_mean(1)
            act.wait_ge(S["st_out"], 16)
            peer_act(act, 0)
            root_mean(2)
            attention_act(act, own)
            root_mean(3)
            act.wait_ge(S["kv_out"], 48)
            peer_act(act, 1)

        def attention_pe(pe, wide):
            mm = nc.tensor.matmul
            pe.wait_ge(S["h_ready"], 3)

            def norm(gs):
                pe.wait_ge(S["aq_sq"], gs + 1)
                if gs:
                    pe.wait_ge(S["aq_done"], gs)
                for m in range(4):
                    ins = mm(ps[:, 4 + m, 0:T], blk64, asq[:, m, :], start=True, stop=True)
                ins.then_inc(S["aq_ms"], 1)

            def rotate(gs):
                pe.wait_ge(S["aq_qn"], gs + 1)
                for m in range(4):
                    ins = mm(ps[:, 4 + m, 0:T], rotm, qk[:, 4 * gs + m, :], start=True, stop=True)
                ins.then_inc(S["aq_rot"], 1)

            for gs in range(6):
                if gs:
                    pe.wait_ge(S["aq_copied"], gs)
                for m in range(4):
                    if m == 2 and gs:
                        rotate(gs - 1)
                    wide(QK + 4 * gs + m, m, ps[:, m, 0:T], hT).then_inc(S["tile_done"], 1)
                norm(gs)
            pe.wait_ge(S["aq_copied"], 6)
            for g in range(NG):
                if g:
                    pe.wait_ge(S["v_copied"], g)
                for s in range(4):
                    tile_wait(pe, VP + 4 * g + s)
                    for z in range(2):
                        c = 2 * s + z
                        for a, n in ((0, 128), (1, 128), (2, 32)):
                            ins = mm(ps[0:n, a, :], hT[:, c, 128 * a:128 * a + n], ring[:, s, z * 512:(z + 1) * 512],
                                     start=(c == 0), stop=(c == NC - 1))
                    ins.then_inc(S["tile_done"], 1)
                if g == 0:
                    rotate(5)
            pe.wait_ge(S["aq_done"], 6)
            pe.wait_ge(S["v_copied"], NG)
            pe.wait_ge(S["qz_ready"], 1)

            def kv(n):
                pe.wait_ge(S[f"in_kv{n % 3}"], 16 * (n // 3 + 1))
                return kv_buf[n % 3]

            def sample_scores(hf):
                if hf:
                    pe.wait_ge(S["ss_cp"], hf)
                for bb in range(4):
                    b = 4 * hf + bb
                    kb = kv(8 * hf + bb).rearrange("p (q k) -> p q k", q=HP)
                    rows = slice(32 * bb, 32 * bb + 32)
                    for g in range(NG):
                        bank, c0 = (5, 0) if g == 1 else (6, KOFF[g] - 512)
                        for q in range(HP):
                            ins = mm(ps[rows, bank, c0:c0 + NK[g]], qz[:, g, b, q, :, :].rearrange("p h t -> p (h t)"),
                                     kb[:, q, KOFF[g]:KOFF[g] + NK[g]], start=(q == 0), stop=(q == HP - 1))
                    ins.then_inc(S["kv_used"], 1)
                    for g in range(NG):
                        c0 = NEWC - 512 + 32 * g
                        for q in range(HP):
                            ins = mm(ps[rows, 6, c0:c0 + 32], qz[:, g, b, q, :, :].rearrange("p h t -> p (h t)"),
                                     qk[:, 8 * g + 4 + q, 256:T], start=(q == 0), stop=(q == HP - 1))
                ins.then_inc(S["ss_mm"], 1)

            def sample_pv(hf):
                pe.wait_ge(S["ss_norm"], hf + 1)
                for k in range(7):
                    nc.tensor.transpose(ps[:, 2 + k // 4, (k % 4) * 128:(k % 4 + 1) * 128],
                                        ps_s[:, 128 * k:128 * k + 128], ident)
                for g in range(NG):
                    ins = nc.tensor.transpose(ps[0:32, 5, g * 128:(g + 1) * 128],
                                              ps_s[:, NEWC + 32 * g:NEWC + 32 * g + 32], ident)
                ins.then_inc(S["ss_t"], 1)
                pe.wait_ge(S["ss_cp"], hf + 1)
                for bb in range(4):
                    vb = kv(8 * hf + 4 + bb).rearrange("p (k n) -> p k n", k=7)
                    for q in range(HP):
                        c0 = (bb * HP + q) * 8
                        r0 = 32 * bb + 8 * q
                        for k in range(7):
                            ins = mm(ps[:, 7, c0:c0 + 8], vb[:, k, q * 128:(q + 1) * 128], pts[:, k, r0:r0 + 8],
                                     start=(k == 0), stop=False, skip_group_check=True)
                        if q == HP - 1:
                            ins.then_inc(S["kv_used"], 1)
                        for g in range(NG):
                            ins = mm(ps[:, 7, c0:c0 + 8], v_sb[0:32, 2, g, q * 128:(q + 1) * 128],
                                     ptn[0:32, g, r0:r0 + 8], start=False, stop=(g == NG - 1), skip_group_check=True)
                ins.then_inc(S["ss_pv"], 1)

            def unit_scores(u):
                qt, h = u // H, u % H
                r = slice(64 * (h % 2), 64 * (h % 2) + 64)
                if u:
                    pe.wait_ge(S["us_max"], u)
                w = 128 * (qt + 1)
                for g in range(NG):
                    bank, c0 = (0, g * w) if g * w < 512 else (1, 0)
                    ins = mm(ps[:, bank, c0:c0 + w], qk[r, 8 * g + h // 2, 128 * qt:128 * qt + 128],
                             qk[r, 8 * g + 4 + h // 2, 0:w], start=True, stop=True)
                ins.then_inc(S["us_mm"], 1)

            def unit_pv(u):
                qt, h = u // H, u % H
                pe.wait_ge(S["us_exp"], u + 1)
                if u:
                    pe.wait_ge(S["us_cpa"], u)
                if u % 8 == 0 and u:
                    pe.wait_ge(S["ss_cp"], u // 8)
                n = NG * (qt + 1)
                for k in range(n):
                    ins = nc.tensor.transpose(ps[:, 2 + k // 4, (k % 4) * 128:(k % 4 + 1) * 128],
                                              p_sb[u % 2][:, 128 * k:128 * k + 128], ident)
                ins.then_inc(S["us_t"], 1)
                if u < 15:
                    if u % 8 < 7:
                        unit_scores(u + 1)
                pe.wait_ge(S["us_cpa"], u + 1)
                if u >= 2:
                    pe.wait_ge(S["us_o"], u - 1)
                if u == 9:
                    pe.wait_ge(S["oT_ready"], 1)
                for k in range(n):
                    g, kt = k // (qt + 1), k % (qt + 1)
                    ins = mm(ps[:, 4 + 3 * (u % 2), 0:64], pt_sb[:, 128 * k:128 * k + 128],
                             v_sb[:, kt, g, 64 * h:64 * h + 64], start=(k == 0), stop=(k == n - 1))
                ins.then_inc(S["us_pv"], 1)

            for hf in range(2):
                sample_scores(hf)
                unit_scores(8 * hf)
                for u in range(8 * hf, 8 * hf + 8):
                    unit_pv(u)
                pe.wait_ge(S["us_o"], 8 * hf + 8)
                for q in range(HP):
                    ins = nc.tensor.transpose(ps[:, 0, 128 * q:128 * q + 128], o_tok[:, 128 * q:128 * q + 128], ident)
                ins.then_inc(S["ot_mm"], 1)
                sample_pv(hf)
                pe.wait_ge(S["ot_cp"], hf + 1)
            pe.wait_ge(S["oT_ready"], 2)
            for s in range(4):
                for z in range(2):
                    ins = wide(WO + s, s, ps[:, 2 * s + z, 0:T], oT, 0, HP, z * 512)
                ins.then_inc(S["tile_done"], 1)

        @block.tensor
        def _(pe):
            mm = nc.tensor.matmul

            def ada_tiles(l):
                with pe.Fori(0, 12) as i:
                    for s in range(4):
                        tile_wait(pe, ADA + 48 * l + s, i)
                        for c in range(NC):
                            ins = mm(ps[:, 5 + l, bass.ds((4 * i + s) * ROWS, ROWS)], ring[:, s, c * 128:(c + 1) * 128],
                                     ccol[:, c * ROWS:(c + 1) * ROWS], start=(c == 0), stop=(c == NC - 1))
                        ins.then_inc(S["tile_done"], 1)

            def mean_square(q):
                pe.wait_ge(S["sq_ready"], q + 1)
                for c in range(NC):
                    ins = mm(ps[:, 7, 0:T], ones, modsq[:, c, :] if q else hT[:, c, :], start=(c == 0), stop=(c == NC - 1))
                ins.then_inc(S["ms_ready"], 1)

            def wide(n, s, out, rhs, i=0, chunks=NC, off=0):
                tile_wait(pe, n, i)
                for c in range(chunks):
                    ins = mm(out, ring[:, s, off + c * 128:off + (c + 1) * 128], rhs[:, c, :], start=(c == 0),
                             stop=(c == chunks - 1))
                return ins

            pe.wait_ge(S["in_setup"], 16 * 7)
            pe.wait_ge(S["silu_c"], 1)
            ada_tiles(0)
            mean_square(0)
            ada_tiles(1)

            pe.wait_ge(S["s5_bb"], 1)
            pe.wait_ge(S["h_ready"], 1)
            pe.wait_ge(S["s5_cs"], 1)

            def s5_in(k):
                if k >= 2:
                    pe.wait_ge(S["s5_rot"], k - 1)
                c, gl = k // 4, 2 * (k % 4)
                for z, b in enumerate((bb_re, bb_im)):
                    ins = mm(ps[:, 2 * (k % 2) + z, 0:T], b[:, c, gl:gl + 2, :].rearrange("p g n -> p (g n)"),
                             hT[:, c, :], start=True, stop=True)
                ins.then_inc(S["s5_bu"], 1)

            def s5_out(k):
                c, kk = k // 4, k % 4
                pe.wait_ge(S["s5_op"], k + 1)
                if kk == 0 and c >= 2:
                    pe.wait_ge(S["s5_hy"], c - 1)
                if kk == 0:
                    pe.wait_ge(S["ada_done"], 2)
                o = o5[k % 2]
                for n, z in enumerate((0, 2, 1, 1)):
                    ins = mm(ps[32 * kk:32 * kk + 32, 4 + c % 2, 0:T], cb[:, z, k, :], o[:, n, :], start=(n == 0),
                             stop=(n == 3))
                ins.then_inc(S["s5_ymm"], 1)

            for k in range(PAIRS + 2):
                if k < PAIRS:
                    s5_in(k)
                if k >= 2:
                    s5_out(k - 2)

            pe.wait_ge(S["s5_hy"], NC)

            def glu(i, first):
                for m in range(2):
                    if not first:
                        pe.wait_ge(S["glu_used"], 2 * i + (m - 1))
                    for z in range(2):
                        s = 2 * m + z
                        wide(GLU + s, s, ps[:, s, 0:T], hT, i).then_inc(S["tile_done"], 1)

            glu(0, True)
            with pe.Fori(1, 4) as i:
                glu(i, False)

            def peer_pe(l):
                pe.wait_ge(S["h_ready"], 2 * l + 2)
                for m in range(8):
                    if m >= 4:
                        pe.wait_ge(S["q_copied"], 8 * l + m - 3)
                    wide(PQ[l] + m, m % 4, ps[:, m % 4, 0:T], hT).then_inc(S["tile_done"], 1)

                def experts(j0, j1):
                    with pe.Fori(j0 // 4, j1 // 4) as i:
                        for s in range(4):
                            pe.wait_ge(S["gelu_done"], 4 * i + (s - 1 + 128 * l))
                            wide(UT[l] + s, s, ps[:, 6 + s % 2, 0:T], hT, i).then_inc(S["tile_done"], 1)

                def q_norm(n):
                    pe.wait_ge(S["qsq_ready"], l + 1)
                    if n:
                        pe.wait_ge(S["qsd_ready"], 2 * l + 1)
                    for m in range(4):
                        ins = mm(ps[:, m, 0:T], blk64, qsq[:, 4 * n + m, :], start=True, stop=True)
                    ins.then_inc(S["qms_ready"], 1)

                def scores(n):
                    if n == 0:
                        pe.wait_ge(S["qn_ready"], l + 1)
                        pe.wait_ge(S["gate_in"], 48 * (l + 1))
                    if n == 2:
                        pe.wait_ge(S["sc_copied"], 3 * l + 1)
                    for h in range(PH):
                        for z in range(2):
                            r = slice(64 * z, 64 * z + 64)
                            if n != 1:
                                t0 = 128 * (n // 2)
                                out = ps[:, 2 * z + h // 4, (h % 4) * 128:(h % 4 + 1) * 128]
                                lhs = qraw[r, h, t0:t0 + 128]
                            else:
                                q = 32 * (h % 4)
                                out = ps[q:q + 32, 4 + z, (h // 4) * 128:(h // 4 + 1) * 128]
                                lhs = qraw[r, h, 256:T]
                            ins = mm(out, lhs, subk[r, h, :], start=True, stop=True)
                    ins.then_inc(S["sc_mm"], 1)

                for s in range(4):
                    if s >= 2:
                        pe.wait_ge(S["gelu_done"], 128 * l + s - 1)
                    wide(UT[l] + s, s, ps[:, 6 + s % 2, 0:T], hT).then_inc(S["tile_done"], 1)
                experts(4, 8)
                q_norm(0)
                experts(8, 12)
                q_norm(1)
                experts(12, 16)
                scores(0)
                scores(1)
                experts(16, 20)
                scores(2)
                experts(20, NB0)
                pe.wait_ge(S["sel_ready"], l + 1)
                pe.wait_ge(S["sc_copied"], 3 * l + 3)
                for n in range(2):
                    for q in range(3):
                        ins = nc.tensor.transpose(ps[:, n, 128 * q:128 * q + 128],
                                                  sel3[:, q, 8 * n:8 * n + 8, :].rearrange("p u k -> p (u k)"), ident)
                    ins.then_inc(S["sel_t"], 1)
                for q in range(3):
                    ins = mm(ps[:, 2, 32 * q:32 * q + 32], selz[:, q, :], jsel, start=True, stop=True)
                ins.then_inc(S["sel_t"], 1)
                pe.wait_ge(S["idx_ready"], 3 * l + 3)

                def gates(i, first):
                    for b in range(2):
                        pe.wait_ge(S["gb_o1"], 2 * i + (b + 1 + 72 * l))
                        pe.wait_ge(S["gb_o2"], 2 * i + (b + 1 + 72 * l))
                        if not first:
                            pe.wait_ge(S["gb_mul"], 2 * i + (b - 1 + 72 * l))
                            pe.wait_ge(S["gb_cp"], 2 * i + (b - 1 + 72 * l))
                        for t in range(4):
                            ins = mm(ps[:, b, 128 * t:128 * t + 128], oh[:, 0, b, t, :], oh[:, 1, b, t, :],
                                     start=True, stop=True)
                        ins.then_inc(S["gb_mm"], 1)

                gates(0, True)
                with pe.Fori(1, T // 8) as i:
                    gates(i, False)
                experts(NB0, 128)
                pe.wait_ge(S["w_done"], (128 - NB0) * (l + 1))
                pe.wait_ge(S["gb_mul"], 72 * (l + 1))

                def down(i, first, last=False):
                    for s in range(4):
                        tile_wait(pe, VT[l] + s, i)
                        for c in range(NC):
                            rhs = W[:, s, :] if first else W[:, bass.ds(4 * i + s, 1), :].rearrange("p a t -> p (a t)")
                            ins = mm(ps[:, c, 0:T], ring[:, s, c * 128:(c + 1) * 128], rhs,
                                     start=(first and s == 0), stop=(last and s == 3), skip_group_check=True)
                        ins.then_inc(S["tile_done"], 1)

                down(0, True)
                with pe.Fori(1, 31) as i:
                    down(i, False)
                down(31, False, True)

            mean_square(1)
            peer_pe(0)
            mean_square(2)
            attention_pe(pe, wide)
            mean_square(3)
            peer_pe(1)

        def attention_dve(v, own, residual):
            TT, TS, STT, CP = (nc.vector.tensor_tensor, nc.vector.tensor_scalar, nc.vector.scalar_tensor_tensor,
                               nc.vector.tensor_copy)
            v.wait_ge(S["in_att"], 48)

            def finish(gs):
                q = qk[:, 4 * gs:4 * gs + 4, :]
                v.wait_ge(S["aq_rot"], gs + 1)
                own(TT(asq, ps[:, 4:8, 0:T], rope[:, 1].unsqueeze(1).broadcast_to([P, 4, T]), ALU.mult))
                own(TT(q, q, rope[:, 0].unsqueeze(1).broadcast_to([P, 4, T]), ALU.mult))
                own.settle()
                TT(q, q, asq, ALU.add).then_inc(S["aq_done"], 1)

            for gs in range(6):
                q = qk[:, 4 * gs:4 * gs + 4, :]
                if gs:
                    finish(gs - 1)
                    v.wait_ge(S["aq_done"], gs)
                v.wait_ge(S["aq_copied"], gs + 1)
                TT(asq, q, q, ALU.mult).then_inc(S["aq_sq"], 1)
                v.wait_ge(S["aq_sd"], gs + 1)
                own(nc.vector.reciprocal(ars, ars))
                own.settle()
                STT(out=q, in0=q, scalar=(kg if gs % 2 else qg), in1=ars, op0=ALU.mult, op1=ALU.mult)\
                    .then_inc(S["aq_qn"], 1)
                v.wait_ge(S["aq_qn"], gs + 1)
            finish(5)

            def sample_max(hf):
                v.wait_ge(S["ss_mm"], hf + 1)
                own(STT(out=ps_s[:, 0:512], in0=ps[:, 5, :], scalar=E ** -0.5, in1=smaskv[:, 0:512],
                        op0=ALU.mult, op1=ALU.add))
                own(STT(out=ps_s[:, 512:CK], in0=ps[:, 6, 0:CK - 512], scalar=E ** -0.5, in1=smaskv[:, 512:CK],
                        op0=ALU.mult, op1=ALU.add))
                own(STT(out=ps_s[:, CK:SW], in0=ps[:, 6, CK - 512:SW - 512], scalar=E ** -0.5,
                        in1=smaskv[:, CK + 96 * hf:CK + 96 * hf + 96], op0=ALU.mult, op1=ALU.add))
                own.settle()
                own(nc.vector.tensor_reduce(sst[:, 2:3], ps_s, X, ALU.max))
                own.settle()
                TS(sst[:, 0:1], sst[:, 2:3], -1.0, None, ALU.mult).then_inc(S["ss_max"], 1)

            def sample_norm(hf):
                v.wait_ge(S["ss_exp"], hf + 1)
                own(nc.vector.reciprocal(sst[:, 3:4], sst[:, 1:2]))
                own.settle()
                TS(ps_s, ps_s, sst[:, 3:4], None, ALU.mult).then_inc(S["ss_norm"], 1)

            def sample_out(hf):
                v.wait_ge(S["ss_pv"], hf + 1)
                for h2 in range(2):
                    r = slice(64 * h2, 64 * h2 + 64)
                    src = ps[r, 7, 0:128].rearrange("p (b q n) -> p q b n", b=4, q=HP)[:, :, :, 4 * h2:4 * h2 + 4]
                    t0 = 256 + 16 * hf
                    ins = CP(oT[r, :, t0:t0 + 16].rearrange("p q (b t) -> p q b t", b=4), src)
                ins.then_inc(S["oT_ready"], 1)

            def unit_max(u):
                qt = u // H
                w = 384 * (qt + 1)
                c = 4 + 3 * (u % 2)
                v.wait_ge(S["us_mm"], u + 1)
                if u >= 2:
                    v.wait_ge(S["us_t"], u - 1)
                um = p_sb[u % 2]
                own(STT(out=um[:, 0:w], in0=ps[:, 0:2, :].rearrange("p b n -> p (b n)")[:, 0:w], scalar=E ** -0.5,
                        in1=pmask[:, 384 * qt:384 * qt + w], op0=ALU.mult, op1=ALU.add))
                own.settle()
                own(nc.vector.tensor_reduce(sst[:, c + 2:c + 3], um[:, 0:w], X, ALU.max))
                own.settle()
                TS(sst[:, c:c + 1], sst[:, c + 2:c + 3], -1.0, None, ALU.mult).then_inc(S["us_max"], 1)

            def unit_out(u):
                h = u % H
                c = 5 + 3 * (u % 2)
                v.wait_ge(S["us_pv"], u + 1)
                if u == 8:
                    v.wait_ge(S["ot_mm"], 1)
                TS(o_tok[:, 64 * h:64 * h + 64], ps[:, 4 + 3 * (u % 2), 0:64], rden[:, u:u + 1], None, ALU.mult)\
                    .then_inc(S["us_o"], 1)

            rden = sst[:, 16:32]

            def unit_den(u):
                c = 5 + 3 * (u % 2)
                v.wait_ge(S["us_exp"], u + 1)
                own(nc.vector.reciprocal(rden[:, u:u + 1], sst[:, c:c + 1]))
                own.settle()

            for hf in range(2):
                sample_max(hf)
                unit_max(8 * hf)
                sample_norm(hf)
                for u in range(8 * hf, 8 * hf + 8):
                    unit_den(u)
                    if u % 8 < 7:
                        unit_max(u + 1)
                    unit_out(u)
                v.wait_ge(S["ot_mm"], hf + 1)
                CP(oT[:, :, 128 * hf:128 * hf + 128], ps[:, 0, :].rearrange("p (q t) -> p q t", q=HP))\
                    .then_inc(S["ot_cp"], 1)
                sample_out(hf)
            v.wait_ge(S["tile_done"], WO + 4)
            residual(ada[:, 1, 2], ps[:, :, 0:T], 0, NC, gtmp[:, 0:256].rearrange("p (c t) -> p c t", c=NC), S["x_ready"])

        @block.vector
        def _(v):
            own = Count(v, S["v_own"])
            TT, TS, STT, CP = (nc.vector.tensor_tensor, nc.vector.tensor_scalar, nc.vector.scalar_tensor_tensor,
                               nc.vector.tensor_copy)
            own(nc.vector.memset(eps_c[:, :], EPS))
            v.wait_ge(S["in_setup"], 16 * 7)

            def square_x(q, dst):
                TT(dst, xT, xT, ALU.mult).then_inc(S["sq_ready"], 1)

            own.settle()
            square_x(0, hT)
            v.wait_ge(S["in_s5"], 16 * 6)
            v.wait_ge(S["s5_trig"], 1)
            own(TT(sth, lim, ldt, ALU.mult))
            own(TT(sr, lre, ldt, ALU.mult))
            own.settle()
            own(TS(sq1, sth, 1.0 / TWO_PI, MAGIC, ALU.mult, ALU.add))
            own.settle()
            own(TS(sq1, sq1, MAGIC, None, ALU.subtract))
            own.settle()
            for part in (C1, C2, C3):
                own(STT(out=sth, in0=sq1, scalar=-part, in1=sth, op0=ALU.mult, op1=ALU.add))
                own.settle()
            TS(sth, sth, PI_LO, -PI_LO, ALU.min, ALU.max).then_inc(S["s5_thr"], 1)
            v.wait_ge(S["s5_trig"], 2)
            own(TT(scos, scos, scos, ALU.mult))
            own.settle()
            TS(scos, scos, -2.0, 1.0, ALU.mult, ALU.add).then_inc(S["s5_thr"], 1)
            v.wait_ge(S["s5_trig"], 3)
            v.wait_ge(S["s5_thr"], 2)
            own(CP(r_col, sr[:, 512:LW]))
            a = slice(0, 512)
            are, aim, den, t1 = sq1[:, a], sth[:, a], ldt[:, a], st1[:, a]
            own(TT(are, sr[:, a], scos[:, a], ALU.mult))
            own(TT(aim, sr[:, a], ssin[:, a], ALU.mult))
            own(TT(den, lre[:, a], lre[:, a], ALU.mult))
            own(TT(t1, lim[:, a], lim[:, a], ALU.mult))
            own.settle()
            own(TS(are, are, 1.0, None, ALU.subtract))
            own(TT(den, den, t1, ALU.add))
            own.settle()
            own(nc.vector.reciprocal(den, den))
            own(TT(t1, are, lre[:, a], ALU.mult))
            own(TT(sr[:, a], aim, lim[:, a], ALU.mult))
            own.settle()
            own(TT(t1, t1, sr[:, a], ALU.add))
            own(TT(aim, aim, lre[:, a], ALU.mult))
            own(TT(are, are, lim[:, a], ALU.mult))
            own.settle()
            own(TT(aim, aim, are, ALU.subtract))
            own(TT(t1, t1, den, ALU.mult))
            own.settle()
            own(TT(aim, aim, den, ALU.mult))
            own.settle()
            own(TT(lre[:, a], t1, sbre, ALU.mult))
            own(TT(lim[:, a], aim, sbim, ALU.mult))
            own(TT(are, t1, sbim, ALU.mult))
            own(TT(den, aim, sbre, ALU.mult))
            own.settle()
            own(TT(sbre, lre[:, a], lim[:, a], ALU.subtract))
            own(TT(sbim, are, den, ALU.add))
            b = slice(512, LW)
            ec, es, tc, ts = scos[:, b], ssin[:, b], lre[:, b], lim[:, b]
            td = ldt[:, b]
            own(nc.vector.memset(tcos[:, :, 0:1], 1.0))
            own(nc.vector.memset(tsin[:, :, 0:1], 0.0))
            own.settle()
            n = 1
            scr = bb_im_f
            while n < 256:
                s1 = scr[:, 0:PAIRS * n].rearrange("p (k t) -> p k t", k=PAIRS)
                s2 = bb_re.rearrange("p c g n -> p (c g n)")[:, 0:PAIRS * n].rearrange("p (k t) -> p k t", k=PAIRS)
                cc, ss = (e.unsqueeze(2).broadcast_to([P, PAIRS, n]) for e in (ec, es))
                own(TT(tcos[:, :, n:2 * n], tcos[:, :, 0:n], cc, ALU.mult))
                own(TT(s1, tsin[:, :, 0:n], ss, ALU.mult))
                own(TT(tsin[:, :, n:2 * n], tsin[:, :, 0:n], cc, ALU.mult))
                own(TT(s2, tcos[:, :, 0:n], ss, ALU.mult))
                own(TT(tc, ec, ec, ALU.mult))
                own(TT(ts, es, es, ALU.mult))
                own(TT(td, ec, es, ALU.mult))
                own.settle()
                own(TT(tcos[:, :, n:2 * n], tcos[:, :, n:2 * n], s1, ALU.subtract))
                own(TT(tsin[:, :, n:2 * n], tsin[:, :, n:2 * n], s2, ALU.add))
                own(TT(ec, tc, ts, ALU.subtract))
                own(TS(es, td, 2.0, None, ALU.mult))
                own.settle()
                n *= 2
            for tab in (tcos, tsin):
                src = tab[:, :, 1:5].unsqueeze(2).broadcast_to([P, PAIRS, SB, ST])
                ins = CP(tab[:, :, 256:T].rearrange("p k (b t) -> p k b t", b=SB), src)
            ins.then_inc(S["s5_tab"], 1)

            def ada_finish(l):
                v.wait_ge(S["tile_done"], ADA + 48 * (l + 1))
                flat = ada_t[:, l * 48 * ROWS:(l + 1) * 48 * ROWS].rearrange("p (m r) -> p m r", r=ROWS)
                own(TT(flat, ps[:, 5 + l, 0:48 * ROWS].rearrange("p (m r) -> p m r", r=ROWS),
                       bias_t[:, 48 * l:48 * l + 48].unsqueeze(2).broadcast_to([P, 48, ROWS]), ALU.add))
                own.settle()
                for w in range(2):
                    sc = ada[:, l, 3 * w + 1]
                    g0 = (2 * l + w) * NC
                    ins = STT(out=sc, in0=sc, scalar=1.0,
                              in1=gain_t[:, g0:g0 + NC].unsqueeze(2).broadcast_to([P, NC, ROWS]),
                              op0=ALU.add, op1=ALU.mult)
                ins.then_inc(S["ada_done"], 1)

            def by_sample(row):
                return row.unsqueeze(3).broadcast_to([P, row.shape[1], SB, ST])

            def tokens4(x):
                return x.rearrange("p c (b t) -> p c b t", b=SB)

            def modulate(q):
                l, w = q // 2, q % 2
                v.wait_ge(S["std_ready"], q + 1)
                own(nc.vector.reciprocal(rstd[:, :], rstd[:, :]))
                own.settle()
                own(TT(hT, xT, rstd[:, :].unsqueeze(1).broadcast_to([P, NC, T]), ALU.mult))
                own.settle()
                sc, sh = ada[:, l, 3 * w + 1], ada[:, l, 3 * w]
                own(TT(tokens4(hT[:, :, 256:T]), tokens4(hT[:, :, 256:T]), by_sample(sc[:, :, 1:]), ALU.mult))
                for c in range(NC):
                    own(TS(hT[:, c, 0:256], hT[:, c, 0:256], sc[:, c, 0:1], sh[:, c, 0:1], ALU.mult, ALU.add))
                own.settle()
                TT(tokens4(hT[:, :, 256:T]), tokens4(hT[:, :, 256:T]), by_sample(sh[:, :, 1:]), ALU.add)\
                    .then_inc(S["h_ready"], 1)

            def residual(gate, src, m0, m1, tmp, done):
                own(TT(tokens4(tmp), tokens4(src[:, :, 256:T]), by_sample(gate[:, m0:m1, 1:]), ALU.mult))
                for m in range(m0, m1):
                    own(STT(out=xT[:, m, 0:256], in0=src[:, m - m0, 0:256], scalar=gate[:, m, 0:1],
                            in1=xT[:, m, 0:256], op0=ALU.mult, op1=ALU.add))
                own.settle()
                TT(xT[:, m0:m1, 256:T], xT[:, m0:m1, 256:T], tmp, ALU.add).then_inc(done, 1)

            ada_finish(0)
            v.wait_ge(S["ada_done"], 1)
            modulate(0)
            v.wait_ge(S["h_ready"], 1)
            v.wait_ge(S["s5_bb"], 1)

            def rot_in(k):
                v.wait_ge(S["s5_bu"], k + 1)
                if k >= 2:
                    v.wait_ge(S["s5_zin"], k - 1)
                re, im = ps[:, 2 * (k % 2), 0:T], ps[:, 2 * (k % 2) + 1, 0:T]
                m = m5[k % 2]
                TT(m[:, 0], tcos[:, k], re, ALU.mult)
                TT(m[:, 1], tsin[:, k], im, ALU.mult)
                TT(m[:, 2], tcos[:, k], im, ALU.mult)
                TT(m[:, 3], tsin[:, k], re, ALU.mult).then_inc(S["s5_rot"], 1)

            def scan(k):
                v.wait_ge(S["s5_zin"], k + 1)
                for z in range(2):
                    ins = nc.vector.tensor_tensor_scan(zin[k % 2][:, z], rm5[k % 2], zin[k % 2][:, z], 0.0,
                                                       ALU.mult, ALU.add)
                ins.then_inc(S["s5_z"], 1)
                v.wait_ge(S["s5_z"], k + 1)
                if k >= 2:
                    v.wait_ge(S["s5_ymm"], k - 1)
                    v.wait_ge(S["s5_rm"], k - 1)
                o, z = o5[k % 2], zin[k % 2]
                TT(o[:, 0], tcos[:, k], z[:, 0], ALU.mult)
                TT(o[:, 1], tsin[:, k], z[:, 1], ALU.mult)
                TT(o[:, 2], tsin[:, k], z[:, 0], ALU.mult)
                TT(o[:, 3], tcos[:, k], z[:, 1], ALU.mult).then_inc(S["s5_op"], 1)

            def chunk_y(c):
                v.wait_ge(S["s5_ymm"], 4 * c + 4)
                STT(out=hT[:, c], in0=hT[:, c], scalar=dskip[:, c:c + 1], in1=ps[:, 4 + c % 2, 0:T],
                    op0=ALU.mult, op1=ALU.add).then_inc(S["s5_hy"], 1)

            for k in range(PAIRS + 3):
                if k == 1:
                    ada_finish(1)
                if k < PAIRS:
                    rot_in(k)
                if 1 <= k <= PAIRS:
                    scan(k - 1)
                if k >= 6 and (k - 6) % 4 == 0:
                    chunk_y((k - 6) // 4)
            v.wait_ge(S["ada_done"], 2)
            for m in range(NC):
                v.wait_ge(S["glu_sig"], m + 1)
                g = gtmp[:, (m % 2) * T:(m % 2 + 1) * T]
                TT(g, ps[:, 2 * (m % 2), 0:T], g, ALU.mult).then_inc(S["glu_used_v"], 1)
                v.wait_ge(S["glu_used_v"], m + 1)
                residual(ada[:, 0, 2], g.unsqueeze(1), m, m + 1, rstd[:, 0:32].unsqueeze(1), S["glu_used"])
            v.wait_ge(S["glu_used"], NC)
            v.wait_ge(S["s5_rm"], PAIRS)
            square_x(1, modsq)

            def peer_dve(l):
                last = S["q_copied"]
                v.wait_ge(last, 8 * l + 8)
                TT(qsq, qraw, qraw, ALU.mult).then_inc(S["qsq_ready"], 1)
                v.wait_ge(S["qsd_ready"], 2 * l + 2)
                own(nc.vector.reciprocal(qrs, qrs))
                own.settle()
                TT(qraw, qraw, qrs, ALU.mult).then_inc(S["qn_ready"], 1)
                v.wait_ge(S["sc_copied"], 3 * l + 3)
                s4 = s_sb.rearrange("p (u z k) -> p u z k", u=UNITS, z=2)
                s24 = s_two.rearrange("p (u z k) -> p u z k", u=UNITS, z=2)
                uz = [(u, z) for u in range(UNITS) for z in range(2)]
                VM, VI, MR = nc.vector.max, nc.vector.max_index, nc.vector.match_replace
                for u, z in uz:
                    own(VM(v16[:, u, z, 0:8], s4[:, u, z]))
                own.settle()
                for u, z in uz:
                    own(VI(i16u[:, u, z, 0:8], v16[:, u, z, 0:8], s4[:, u, z]))
                    own(MR(s24[:, u, z], v16[:, u, z, 0:8], s4[:, u, z], -3.0e38))
                own.settle()
                for u, z in uz:
                    own(VM(v16[:, u, z, 8:16], s24[:, u, z]))
                own.settle()
                for u, z in uz:
                    own(VI(i16u[:, u, z, 8:16], v16[:, u, z, 8:16], s24[:, u, z]))
                c4 = cand.rearrange("p (u a b) -> p u a b", u=UNITS, a=16)
                own(TT(c4, v16[:, :, 0].unsqueeze(3).broadcast_to([P, UNITS, 16, 16]),
                       v16[:, :, 1].unsqueeze(2).broadcast_to([P, UNITS, 16, 16]), ALU.add))
                own.settle()
                own(CP(i16f, i16u))
                cu = cand.rearrange("p (u n) -> p u n", u=UNITS)
                c2 = s_sb.rearrange("p (u n) -> p u n", u=UNITS)
                for u in range(UNITS):
                    own(VM(best[:, u, 0:8], cu[:, u]))
                own.settle()
                for u in range(UNITS):
                    own(VI(selu[:, u, 0:8], best[:, u, 0:8], cu[:, u]))
                    own(MR(c2[:, u], best[:, u, 0:8], cu[:, u], -3.0e38))
                own.settle()
                for u in range(UNITS):
                    own(VM(best[:, u, 8:16], c2[:, u]))
                own.settle()
                for u in range(UNITS):
                    own(VI(selu[:, u, 8:16], best[:, u, 8:16], c2[:, u]))
                own(CP(gsum[:, 0:UNITS], best[:, :, 0]))
                own.settle()
                TT(best, best, gsum[:, 0:UNITS].unsqueeze(2).broadcast_to([P, UNITS, 16]), ALU.subtract)\
                    .then_inc(S["gate_exp"], 1)
                own(TS(selabu[:, 0], selu, 4, None, ALU.logical_shift_right))
                own(TS(selabu[:, 1], selu, 15, None, ALU.bitwise_and))
                own.settle()
                own(CP(selab, selabu))
                own.settle()
                e4 = eq.rearrange("p (u k a) -> p u k a", u=UNITS, k=16)
                for z in range(2):
                    own(TT(e4, selab[:, z].unsqueeze(3).broadcast_to([P, UNITS, 16, 16]),
                           iota[:, 0:16].unsqueeze(1).unsqueeze(1).broadcast_to([P, UNITS, 16, 16]), ALU.is_equal))
                    own.settle()
                    own(TT(e4, e4, i16f[:, :, z].unsqueeze(2).broadcast_to([P, UNITS, 16, 16]), ALU.mult))
                    own.settle()
                    own(nc.vector.tensor_reduce(sel3[:, z], e4, X, ALU.add))
                    own.settle()
                v.wait_ge(S["gate_exp"], 2 * l + 2)
                own(nc.vector.tensor_reduce(gsum[:, 0:UNITS], best, X, ALU.add))
                own.settle()
                own(nc.vector.reciprocal(gsum[:, 0:UNITS], gsum[:, 0:UNITS]))
                own.settle()
                own(TT(sel3[:, 2], best, gsum[:, 0:UNITS].unsqueeze(2).broadcast_to([P, UNITS, 16]), ALU.mult))
                own.settle()
                v.wait_ge(S["gate_in"], 48 * (l + 1))
                for q in range(3):
                    ins = TT(selz[:, q].rearrange("p (u h k) -> p u h k", u=2, h=4),
                             sel3[:, q, 16:18].unsqueeze(2).broadcast_to([P, 2, 4, 16]),
                             hqm.unsqueeze(1).unsqueeze(3).broadcast_to([P, 2, 4, 16]), ALU.mult)
                ins.then_inc(S["sel_ready"], 1)
                v.wait_ge(S["idx_ready"], 3 * l + 3)
                v.wait_ge(S["gelu_done"], 128 * l + NB0)

                def onehot2(i, b, first):
                    if not first:
                        v.wait_ge(S["gb_mm"], 2 * i + (b - 1 + 72 * l))
                    for t in range(4):
                        tok = 8 * i + 4 * b + t
                        ins = TS(oh[:, 1, b, t, :], iota, idx[:, 1, bass.ds(tok, 1)], idx[:, 2, bass.ds(tok, 1)],
                                 ALU.is_equal, ALU.mult)
                    ins.then_inc(S["gb_o2"], 1)

                def gate_low(i, b):
                    v.wait_ge(S["gb_mm"], 2 * i + (b + 1 + 72 * l))
                    w = W[:, 0:NB0, bass.ds(8 * i + 4 * b, 4)]
                    TT(w, w, ps[:, b, :].rearrange("p (t j) -> p j t", t=4)[:, 0:NB0, :], ALU.mult)\
                        .then_inc(S["gb_mul"], 1)

                onehot2(0, 0, True)
                onehot2(0, 1, True)
                gate_low(0, 0)
                with v.Fori(1, T // 8) as i:
                    onehot2(i, 0, False)
                    gate_low(i - 1, 1)
                    onehot2(i, 1, False)
                    gate_low(i, 0)
                gate_low(T // 8 - 1, 1)
                v.wait_ge(S["gb_cp"], 72 * (l + 1))
                with v.Fori(NB0 // 4, 32) as i:
                    for s in range(4):
                        v.wait_ge(S["gelu_done"], 4 * i + (s + 1 + 128 * l))
                        w = W[:, bass.ds(4 * i + s, 1), :].rearrange("p a t -> p (a t)")
                        TT(w, w, gtmp[:, (s % 2) * T:(s % 2 + 1) * T], ALU.mult).then_inc(S["w_done"], 1)
                v.wait_ge(S["tile_done"], VT[l] + 128)
                residual(ada[:, l, 5], ps[:, :, 0:T], 0, NC, gtmp[:, 0:256].rearrange("p (c t) -> p c t", c=NC),
                         S["x_ready"])

            modulate(1)
            peer_dve(0)
            v.wait_ge(S["x_ready"], 1)
            square_x(2, modsq)
            modulate(2)
            attention_dve(v, own, residual)
            v.wait_ge(S["x_ready"], 2)
            square_x(3, modsq)
            modulate(3)
            peer_dve(1)

        @block.gpsimd
        def _(pool):
            own = Count(pool, S["p_own"])
            TT, TS, CP = nc.gpsimd.tensor_tensor, nc.gpsimd.tensor_scalar, nc.gpsimd.tensor_copy
            pool.wait_ge(S["in_s5"], 16 * 6)
            TS(cb[:, 2], cb[:, 0], -1.0, None, ALU.mult)
            TS(cb[:, 1], cb[:, 1], -1.0, None, ALU.mult).then_inc(S["s5_cs"], 1)
            pool.wait_ge(S["s5_bb"], 1)
            pool.wait_ge(S["in_setup"], 16 * 7)

            def z_in(k):
                m, z = m5[k % 2], zin[k % 2]
                if k >= 2:
                    pool.wait_ge(S["s5_op"], k - 1)
                own(TS(rm5[k % 2], smask[:, :], r_col[:, k:k + 1], None, ALU.mult))
                own(TS(hr5[k % 2], h0[:, :, k, :], r_col[:, k:k + 1], None, ALU.mult))
                pool.wait_ge(S["s5_rot"], k + 1)
                own(TT(z[:, 0], m[:, 0], m[:, 1], ALU.add))
                own(TT(z[:, 1], m[:, 2], m[:, 3], ALU.subtract))
                own.settle()
                first = z[:, :, 256:T].rearrange("p z (b t) -> p z b t", t=ST)[:, :, :, 0]
                TT(first, first, hr5[k % 2], ALU.add).then_inc(S["s5_zin"], 1)

            def last_states(k):
                o = o5[k % 2]
                pool.wait_ge(S["s5_op"], k + 1)
                TT(st[:, 0, k, :], o[:, 0, 255:T:4], o[:, 1, 255:T:4], ALU.subtract)
                TT(st[:, 1, k, :], o[:, 2, 255:T:4], o[:, 3, 255:T:4], ALU.add).then_inc(S["s5_rm"], 1)

            for k in range(PAIRS + 1):
                if k < PAIRS:
                    z_in(k)
                if k >= 1:
                    last_states(k - 1)
            def onehot1(l):
                pool.wait_ge(S["idx_ready"], 3 * l + 3)

                def four(i, b, first):
                    if not first:
                        pool.wait_ge(S["gb_mm"], 2 * i + (b - 1 + 72 * l))
                    o = oh[:, 0, b]
                    TT(o, iota.unsqueeze(1).broadcast_to([P, 4, 128]),
                       idx[:, 0, bass.ds(8 * i + 4 * b, 4)].unsqueeze(2).broadcast_to([P, 4, 128]), ALU.subtract)\
                        .then_inc(S["gb_df"], 1)
                    pool.wait_ge(S["gb_df"], 2 * i + (b + 1 + 72 * l))
                    TT(o, o, o, ALU.mult).then_inc(S["gb_sq"], 1)

                four(0, 0, True)
                four(0, 1, True)
                with pool.Fori(1, T // 8) as i:
                    four(i, 0, False)
                    four(i, 1, False)

            onehot1(0)
            pool.wait_ge(S["tile_done"], VT[0] + 128)
            own(nc.gpsimd.memset(qz_t, 0.0))
            own.settle()
            pool.wait_ge(S["aq_done"], 6)
            for g in range(NG):
                for q in range(HP):
                    for h2 in range(2):
                        r = slice(64 * h2, 64 * h2 + 64)
                        ins = CP(qz[r, g, :, q, 2 * q + h2, :],
                                 qk[r, 8 * g + q, 256:T].rearrange("p (b t) -> p b t", b=SB))
            ins.then_inc(S["qz_ready"], 1)
            onehot1(1)


def kernel(**inp):
    import numpy as np
    import concourse.bacc as bacc
    from concourse import mybir as mb
    from concourse.bass_utils import run_bass_kernel_spmd

    a = {k: np.asarray(v) for k, v in inp.items()}
    f = np.float32
    ca = np.ascontiguousarray

    def cols(w, nt, kc=8):
        return w.reshape(kc, P, nt, P).transpose(2, 1, 0, 3).reshape(nt, P, kc * P)

    def u_tiles(u):
        return u.reshape(128, 128, 8, 128).transpose(1, 3, 2, 0).reshape(128, P, 1024)

    def v_tiles(w):
        return w.reshape(128, 128, 1024).transpose(1, 0, 2)

    glu = cols(a["ssm_w_glu"][0], 16).reshape(2, 8, P, 1024).transpose(1, 0, 2, 3).reshape(16, P, 1024)
    wq = a["attn_w_qkv"][0].reshape(D, 3, 3, 512)
    qkt = cols(ca(wq[:, :, 0:2].reshape(D, 3072)), 24)
    vpt = wq[:, :, 2].reshape(4, 2, P, 3, 512).transpose(3, 0, 2, 1, 4).reshape(12, P, 1024)
    wo = cols(a["attn_w_o"][0], 8, 4).reshape(4, 2, P, 512).transpose(0, 2, 1, 3).reshape(4, P, 1024)
    parts = [cols(a["ada_w"][0], 48), cols(a["ada_w"][1], 48), glu, cols(a["peer_w_q"][0], 8),
             u_tiles(a["peer_u"][0]), v_tiles(a["peer_v"][0]), qkt, vpt, wo, cols(a["peer_w_q"][1], 8),
             u_tiles(a["peer_u"][1]), v_tiles(a["peer_v"][1])]
    A = {"stream": np.concatenate(parts)}
    x = np.concatenate([a["x_prompt"][0], a["x_sample"].reshape(32, D)])
    A["xT"] = x.reshape(T, NC, P).transpose(2, 1, 0).reshape(P, NC * T)
    c = np.concatenate([a["c_prompt"], a["c_sample"]])
    A["ccol"] = c.reshape(ROWS, NC, P).transpose(2, 1, 0).reshape(P, -1)
    A["bias"] = a["ada_b"].reshape(L, 48, P).transpose(2, 0, 1).reshape(P, -1)
    gains = np.stack([a["norm_mix"], a["norm_ffn"]], 1)
    A["gain"] = gains.reshape(2 * L, NC, P).transpose(2, 0, 1).reshape(P, -1)
    ones = np.ones((P, P), f)
    blk = np.kron(np.eye(2), np.ones((64, 64))).astype(f)
    rot = np.zeros((P, P), f)
    for h in range(2):
        for i in range(8):
            rot[64 * h + 8 + i, 64 * h + i] = -1.0
            rot[64 * h + i, 64 * h + 8 + i] = 1.0
    iota = np.tile(np.arange(P, dtype=f), (P, 1))
    gm = (np.arange(P)[:, None] // 16 == np.arange(8)[None]).astype(f)
    qkg = np.stack([np.concatenate([a["attn_q_norm"][0]] * 2), np.concatenate([a["attn_k_norm"][0]] * 2)], 1)
    A["consts"] = np.concatenate([ones, blk, np.eye(P, dtype=f), rot, iota, gm, qkg], 1)
    t = np.arange(T)
    sm = np.tile(((t < 256) | ((t - 256) % 4 != 0)).astype(f), (P, 1))
    A["smask"] = sm
    h0 = a["state_ssm"][0].reshape(SB, 2, PAIRS, P).transpose(3, 1, 2, 0).reshape(P, -1)
    A["h0d"] = np.concatenate([h0, a["ssm_d"][0].reshape(NC, P).transpose(1, 0)], 1)

    def both(w):
        one = np.broadcast_to(w.reshape(8, 8, 1, 64), (8, 8, 16, 64)).transpose(1, 2, 0, 3).reshape(P, 512)
        return np.concatenate([one, w.reshape(PAIRS, P).transpose(1, 0)], 1)

    A["lre"], A["lim"] = both(a["ssm_lam_re"][0]), both(a["ssm_lam_im"][0])
    A["ldt"] = both(np.broadcast_to(a["ssm_log_dt"][0][:, None], (64, 64)))
    for n, k in (("sbre", "ssm_b_re"), ("sbim", "ssm_b_im")):
        A[n] = a[k][0].reshape(8, 8, 64, 16).transpose(1, 3, 0, 2).reshape(P, 512)
    cc = []
    for k in ("ssm_c_re", "ssm_c_im"):
        w = a[k][0].reshape(PAIRS, 2, 16, 64).transpose(1, 3, 0, 2)
        z = np.zeros((2, 64, PAIRS, 2, 16), f)
        z[0, :, :, 0], z[1, :, :, 1] = w[0], w[1]
        cc.append(z.reshape(P, 1024))
    A["cri"] = np.concatenate(cc, 1)
    A["subk"] = a["peer_sub_keys"].transpose(0, 2, 4, 1, 3).reshape(L, P, PH * NKEYS)
    A["hqm"] = (np.arange(P)[:, None] // 32 == np.arange(4)[None]).astype(f)
    A["jsel"] = (np.arange(P)[:, None] % 32 == np.arange(32)[None]).astype(f)
    pos = np.concatenate([np.arange(256), PAST + (t[256:] - 256) % 4]).astype(f)
    inv = (f(500000.0) ** (-np.arange(8, dtype=f) / f(8))).astype(f)
    ang = (pos[:, None] * inv[None]).astype(f)
    cs, sn = np.ones((64, T), f), np.zeros((64, T), f)
    cs[0:8] = cs[8:16] = np.cos(ang).T
    sn[0:8] = sn[8:16] = np.sin(ang).T
    A["rope"] = np.concatenate([np.tile(cs, (2, 1)), np.tile(sn, (2, 1))], 1)
    NEG = f(-1e30)
    pm = []
    for qt in range(2):
        q, k = 128 * qt + np.arange(128)[:, None], np.arange(128 * (qt + 1))[None]
        for g in range(NG):
            ok = (k <= q) & ((q - k) % DIL[g] == 0) & ((q - k) // DIL[g] <= WIN[g] // DIL[g])
            pm.append(np.where(ok, f(0), NEG).astype(f))
    A["pmask"] = np.concatenate(pm, 1)
    row = np.arange(P)
    bq, tq = row[:, None] // 32, row[:, None] % 4
    m1 = np.arange(512)[None] % 4 == tq
    m0 = np.arange(128)[None] >= tq
    m2 = np.arange(256)[None] % 4 == tq
    smk = [m1, m0, m2]
    nb, nt = np.arange(32)[None] // 4, np.arange(32)[None] % 4
    for hf in range(2):
        smk += [(nb == bq + 4 * hf) & (nt <= tq)] + [(nb == bq + 4 * hf) & (nt == tq)] * 2
    A["smaskv"] = np.where(np.concatenate(smk, 1), f(0), NEG).astype(f)
    kc, vc = [], []
    for g, name in ((1, "cache_kv_w512"), (0, "cache_kv_w128"), (2, "cache_kv_w2048")):
        cch = a[name][0]
        if g == 2:
            cch = cch.reshape(SB, 2, 64, 16, H, E)[:, :, :, 0:4].reshape(SB, 2, 256, H, E)
        kc.append(cch[:, 0].reshape(SB, -1, HP, P).transpose(0, 3, 2, 1))
        vc.append(cch[:, 1].reshape(SB, -1, P, 512).transpose(0, 2, 1, 3))
    A["kc"] = np.concatenate(kc, 3).reshape(SB, P, HP * CK)
    A["vc"] = np.concatenate(vc, 2).reshape(SB, P, 7 * 512)

    nc = bacc.Bacc("TRN2", target_bir_lowering=False, num_devices=1)
    arrays, I, O = {}, {}, {}
    for n, w in A.items():
        w = ca(w)
        arrays["in_" + n] = w
        I[n] = nc.dram_tensor("in_" + n, w.shape, mb.dt.from_np(w.dtype), kind="ExternalInput").ap()
    for n, shape in (("st", (P, 2 * PAIRS * ROWS)), ("yT", (P, NC * T)), ("qk", (P, 24, T)), ("v", (P, 2, 3, 512)), ("v_s", (32, 3, 512))):
        O[n] = nc.dram_tensor("out_" + n, shape, mb.dt.float32, kind="ExternalOutput").ap()
    build(nc, I, O)
    r = run_bass_kernel_spmd(nc, [arrays], core_ids=[0]).results[0]
    y = r["out_yT"].reshape(P, NC, T).transpose(2, 1, 0).reshape(T, D)
    s = r["out_st"].reshape(P, 2, PAIRS, ROWS).transpose(3, 1, 2, 0).reshape(ROWS, 2, G64, SN)
    k = r["out_qk"].reshape(P, NG, 2, HP, T)[:, :, 1].transpose(1, 3, 2, 0).reshape(NG, T, H, E)
    vv = np.concatenate([r["out_v"].transpose(2, 1, 0, 3).reshape(NG, 256, H, E),
                         r["out_v_s"].transpose(1, 0, 2).reshape(NG, 32, H, E)], 1)
    kvp, kvs = [], []
    for g in range(NG):
        keep = min(WIN[g], 256)
        kvp.append(ca(np.stack([k[g, 256 - keep:256], vv[g, 256 - keep:256]])[None, None]))
        kvs.append(ca(np.stack([k[g, 256:T].reshape(SB, ST, H, E), vv[g, 256:T].reshape(SB, ST, H, E)], 1)[None]))
    return (ca(y[0:256][None]), ca(y[256:].reshape(SB, ST, D)), ca(s[0:1][None]), *kvp, ca(s[1:][None]), *kvs)
```

```python
from contextlib import ExitStack

import concourse.bass as bass
from concourse import mybir

P = 128
D = 1024
NC = D // P
SP_, SB, ST = 256, 8, 4
T = SP_ + SB * ST
ROWS = 1 + SB
L = 2
G64, SN = 64, 64
PAIRS = G64 // 2
H, E = 8, 64
HP = H // 2
NG = 3
WIN, DIL, PAST = (128, 512, 2048), (1, 4, 16), 1024
NK = (128, 512, 256)
KOFF = (512, 0, 640)
CK = sum(NK)
NEWC = CK
SW = CK + NG * 32
PH, NKEYS, TOPK = 8, 128, 16
UNITS = 18
EPS = 1e-6
RING = 4

NB0 = 48
ADA, GLU, PQ = (0, 120), 48, (64, 416)
UT, UT2, VT = (72, 424), (120, 424), (248, 552)
QK, VP, WO, TILES = 376, 400, 412, 680
GROUPS, GPI = T // 4, 12

F32 = mybir.dt.float32
F32R = mybir.dt.float32r
U32 = mybir.dt.uint32
ALU = mybir.AluOpType
ACT = mybir.ActivationFunctionType
X = mybir.AxisListType.X
BU_BANK = (0, 2, 6)
TWO_PI = 6.283185307179586
C1 = 6.28125
C2 = 0.0019350051879882812
C3 = 3.019916050e-07
MAGIC = 12582912.0
PI_LO = 3.1415925


class Count:

    def __init__(self, eng, sem):
        self.eng, self.sem, self.n = eng, sem, 0

    def __call__(self, ins):
        self.n += 1
        ins.then_inc(self.sem, 1)

    def settle(self):
        self.eng.wait_ge(self.sem, self.n)


def build(nc, I, O):
    ctx = ExitStack()
    with ctx:
        def sb(name, words, dt=F32):
            return ctx.enter_context(nc.sbuf_tensor(name, [P, words], dt))

        def sem(name):
            return ctx.enter_context(nc.semaphore(name))

        big = sb("big", 128 * T)
        with nc.sbuf_tensor("ring", [P, RING, 1024], F32) as ring:
            pass
        ring_lo = ctx.enter_context(nc.sbuf_tensor("ring_lo", [P, RING, 1024], F32R))
        with nc.sbuf_tensor("oh", [P, 4 * 512], F32) as oh_t:
            pass
        wt_hi = ctx.enter_context(nc.sbuf_tensor("wt_hi", [P, 2, 1024], F32R))
        with nc.sbuf_tensor("hT", [P, NC * T], F32) as hT_t:
            pass
        split_t = ctx.enter_context(nc.sbuf_tensor("split", [P, 2 * NC * T], F32R))
        h_hi, h_lo = (split_t[:, z * NC * T:(z + 1) * NC * T].rearrange("p (c t) -> p c t", c=NC) for z in range(2))
        w_hi, w_lo = (split_t[:, 2 * z * T:2 * (z + 1) * T].rearrange("p (b t) -> p b t", b=2) for z in range(2))
        xT_t = sb("xT", NC * T)
        xT = xT_t[:, :].rearrange("p (c t) -> p c t", c=NC)
        hT = hT_t[:, :].rearrange("p (c t) -> p c t", c=NC)
        ada_t = sb("ada", L * 48 * ROWS)
        ada = ada_t[:, :].rearrange("p (l j c r) -> p l j c r", l=L, j=6, c=NC)
        consts = sb("consts", 4 * 128 + 10)
        ones = consts[:, 0:128]
        blk64 = consts[:, 128:256]
        ident = consts[:, 256:384]
        iota = consts[:, 384:512]
        gmask = consts[:, 512:520]
        qg, kg = consts[:, 520:521], consts[:, 521:522]
        ccol = sb("ccol", NC * ROWS)
        bias_t = sb("bias", L * 48)
        gain_t = sb("gain", 2 * L * NC)
        eps_c = sb("eps_c", 1)
        idx_t = sb("idx", 3 * T)
        idx = idx_t[:, :].rearrange("p (q t) -> p q t", q=3)
        gtmp = sb("gtmp", 2 * T)
        rstd = gtmp[:, T:2 * T]
        oh = oh_t[:, :].rearrange("p (w b t k) -> p w b t k", w=2, b=2, t=4)
        small = sb("small", 96)
        r_col = small[:, 0:PAIRS]
        st_t = idx_t[:, 0:2 * PAIRS * ROWS]
        st = st_t.rearrange("p (z k r) -> p z k r", z=2, k=PAIRS)
        ps = ctx.enter_context(nc.psum_tensor("ps", [P, 8, 512], F32))

        class Region:

            def __init__(self, at=0):
                self.at = at

            def take(self, words):
                a = big[:, self.at:self.at + words]
                self.at += words
                assert self.at <= 128 * T, self.at
                return a

        W = big[:, :].rearrange("p (j t) -> p j t", j=128)
        rg = Region(NB0 * T)
        s_sb = rg.take(UNITS * 256)
        cand = rg.take(UNITS * 256)
        eq = rg.take(UNITS * 256)
        s_two = eq
        qraw_t = cand
        qraw = qraw_t[:, 0:NC * T].rearrange("p (c t) -> p c t", c=NC)
        qsq_t = eq
        qsq = qsq_t[:, 0:NC * T].rearrange("p (c t) -> p c t", c=NC)
        qrs = eq[:, NC * T:2 * NC * T].rearrange("p (c t) -> p c t", c=NC)
        v16 = rg.take(2 * UNITS * 16).rearrange("p (u z a) -> p u z a", u=UNITS, z=2)
        i16f = rg.take(2 * UNITS * 16).rearrange("p (u z a) -> p u z a", u=UNITS, z=2)
        i16u_f = rg.take(2 * UNITS * 16)
        i16u = i16u_f.bitcast(U32).rearrange("p (u z a) -> p u z a", u=UNITS, z=2)
        best = rg.take(UNITS * 16).rearrange("p (u k) -> p u k", u=UNITS)
        selu = rg.take(UNITS * 16).bitcast(U32).rearrange("p (u k) -> p u k", u=UNITS)
        selabu = rg.take(2 * UNITS * 16).bitcast(U32).rearrange("p (z u k) -> p z u k", z=2, u=UNITS)
        selab = rg.take(2 * UNITS * 16).rearrange("p (z u k) -> p z u k", z=2, u=UNITS)
        sel3 = rg.take(3 * UNITS * 16).rearrange("p (q u k) -> p q u k", q=3, u=UNITS)
        selz = rg.take(3 * 128).rearrange("p (q s) -> p q s", q=3)
        gsum = rg.take(2 * UNITS)
        hqm = rg.take(4)
        jsel = rg.take(32)
        subk_t = rg.take(PH * NKEYS)
        subk = subk_t.rearrange("p (h k) -> p h k", h=PH)
        modsq = big[:, 128 * T - NC * T:128 * T].rearrange("p (c t) -> p c t", c=NC)

        rs = Region()
        tcos = rs.take(PAIRS * T).rearrange("p (k t) -> p k t", k=PAIRS)
        tsin = rs.take(PAIRS * T).rearrange("p (k t) -> p k t", k=PAIRS)
        bb_re = rs.take(4096).rearrange("p (c g n) -> p c g n", c=NC, g=8)
        bb_im_f = rs.take(4096)
        bb_im = bb_im_f.rearrange("p (c g n) -> p c g n", c=NC, g=8)
        cb = rs.take(3 * 1024).rearrange("p (z k m) -> p z k m", z=3, k=PAIRS)
        ring5 = rs.at
        LW = 512 + PAIRS
        lre, lim, ldt = rs.take(LW), rs.take(LW), rs.take(LW)
        sth, sq1, ssin, scos, sr, st1 = (rs.take(LW) for _ in range(6))
        sbre, sbim = rs.take(512), rs.take(512)
        assert rs.at <= 128 * T
        r5 = Region(ring5)
        m5 = [r5.take(4 * T).rearrange("p (q t) -> p q t", q=4) for _ in range(2)]
        zin = [r5.take(2 * T).rearrange("p (q t) -> p q t", q=2) for _ in range(2)]
        z5 = zin
        o5 = [r5.take(4 * T).rearrange("p (q t) -> p q t", q=4) for _ in range(2)]
        rm5 = [r5.take(T) for _ in range(2)]
        zl = gtmp[:, 0:2 * PAIRS * ROWS].rearrange("p (z k r) -> p z k r", z=2, k=PAIRS)

        smask = r5.take(T)
        h0d = r5.take(520)
        h0 = h0d[:, 0:512].rearrange("p (z k b) -> p z k b", z=2, k=PAIRS)
        dskip = h0d[:, 512:520]
        hr5 = [small[:, 32 + 16 * n:48 + 16 * n].rearrange("p (z b) -> p z b", z=2) for n in range(2)]

        ra = Region()
        qk = ra.take(24 * T).rearrange("p (m t) -> p m t", m=24)
        v_sb = ra.take(9 * 512).rearrange("p (a g n) -> p a g n", a=3, g=NG)
        rotm = ra.take(128)
        rope = ra.take(2 * T).rearrange("p (z t) -> p z t", z=2)
        pmask = ra.take(384 + 768)
        smaskv = ra.take(SW + 96)
        qz_t = ra.take(NG * SB * HP * 32)
        qz = qz_t.rearrange("p (g b q h t) -> p g b q h t", g=NG, b=SB, q=HP, h=H)
        oT = ra.take(HP * T).rearrange("p (q t) -> p q t", q=HP)
        sst = ra.take(4)
        ust = ra.take(48).rearrange("p (z u) -> p z u", z=3)
        tmp0 = ra.at
        asq = ra.take(4 * T).rearrange("p (m t) -> p m t", m=4)
        ars = ra.take(4 * T).rearrange("p (m t) -> p m t", m=4)
        rb = Region(tmp0)
        p_sb = [rb.take(768) for _ in range(3)]
        pt_sb = [rb.take(768) for _ in range(2)]
        ps_s = rb.take(SW)
        pts = rb.take(7 * 128).rearrange("p (k r) -> p k r", k=7)
        ptn = rb.take(3 * 128).rearrange("p (g r) -> p g r", g=3)
        kv_buf = [rb.take(4 * CK) for _ in range(3)]

        S = {n: sem(n) for n in (
            "tile_done in_setup in_s5 in_att in_kv0 in_kv1 in_kv2 kv_used v_own a_own p_own silu_c "
            "ada_row ada_turned ada_done us_den us_norm sq_ready ms_ready std_ready h_ready s5_trig s5_thr s5_bb s5_tab s5_bu s5_rot s5_rm s5_zin s5_z "
            "s5_op s5_cs s5_ymm s5_hy glu_sig glu_used st_ready x_ready q_copied qsq_ready qms_ready qsd_ready "
            "qn_ready sc_mm sc_copied gate_in gate_exp sel_ready sel_t idx_ready gb_o1 gb_o2 gb_gate gb_mm gb_mul gb_cp "
            "gelu_done w_done aq_copied aq_sq aq_ms aq_sd aq_qn aq_rot aq_done v_copied qz_ready "
            "us_mm us_max us_exp us_t us_cpa us_cpv us_pv us_o ss_mm ss_max ss_exp ss_t ss_cp "
            "ss_norm ss_pv oT_ready out_done st_out kv_out glu_used_v "
            "ss_oc ss_ot s5_rmr s5_sin s5_zl hi_ready lo_u lo_v hh_ready hl_ready wh_ready wl_ready").split()}
        tile_in = [sem(f"tile_in{s}") for s in range(RING)]

        def tile_wait(eng, n, i=0):
            eng.wait_ge(tile_in[n % RING], 16 * i + 16 * (n // RING + 1))

        block = ctx.enter_context(nc.Block())

        @block.sync
        def _(sp):
            stream = I["stream"]
            for s in range(RING):
                sp.dma_start(ring[:, s, :], stream[s]).then_inc(tile_in[s], 16)
            with sp.Fori(1, TILES // RING) as i:
                for s in range(RING):
                    sp.wait_ge(S["tile_done"], RING * i + (s + 1 - RING))
                    sp.dma_start(ring[:, s, :], stream[bass.ds(RING * i + s, 1)].rearrange("a p n -> (a p) n"))\
                      .then_inc(tile_in[s], 16)
            sp.wait_ge(S["x_ready"], 3)
            sp.dma_start(O["yT"], xT_t[:, :]).then_inc(S["out_done"], 16)
            sp.wait_ge(S["out_done"], 16)
            sp.wait_ge(S["st_out"], 16)
            sp.wait_ge(S["kv_out"], 48)

        def ada_row(act, l, nb, half, bank=4):
            act.wait_ge(S["tile_done"], 8 * nb + (ADA[l] + 8))
            if l or nb or half:
                act.wait_ge(S["ada_turned"], 2 * nb + (12 * l + half))
            nc.scalar.activation(gtmp[0:ROWS, 0:512], ps[0:ROWS, bank + half, :], ACT.Copy).then_inc(S["ada_row"], 1)

        def peer_act(act, l):
            act.dma_start(subk_t, I["subk"][l]).then_inc(S["gate_in"], 16)
            act.dma_start(hqm, I["hqm"]).then_inc(S["gate_in"], 16)
            act.dma_start(jsel, I["jsel"]).then_inc(S["gate_in"], 16)
            act.wait_ge(S["h_ready"], 2 * l + 2)
            nc.scalar.activation(h_hi, modsq, ACT.Copy).then_inc(S["hh_ready"], 1)

            def high(n, i=0):
                tile_wait(act, n, i)
                nc.scalar.activation(wt_hi[:, n % 2], ring[:, n % RING], ACT.Copy).then_inc(S["hi_ready"], 1)

            for m in range(8):
                act.wait_ge(S["tile_done"], PQ[l] + m + 1)
                nc.scalar.activation(qraw[:, m, :], ps[:, m % 4, 0:T], ACT.Copy).then_inc(S["q_copied"], 1)
                if m in (5, 6):
                    high(UT[l] + m - 5)

            def gelu_block(i, s, ahead=True):
                act.wait_ge(S["tile_done"], 4 * i + (UT[l] + s + 1))
                if ahead:
                    high(UT[l] + s + 2, i)
                dst = W[:, bass.ds(4 * i + s, 1), :].rearrange("p a t -> p (a t)")
                nc.scalar.activation(dst, ps[:, 6 + s % 2, 0:T], ACT.Gelu).then_inc(S["gelu_done"], 1)

            def gelus(j0, j1):
                with act.Fori(j0 // 4, j1 // 4) as i:
                    for s in range(4):
                        gelu_block(i, s)

            def q_root(n):
                act.wait_ge(S["qms_ready"], 2 * l + n + 1)
                nc.scalar.activation(qrs[:, 4 * n:4 * n + 4, :], ps[:, 0:4, 0:T], ACT.Sqrt, bias=eps_c[:, :],
                                     scale=1.0 / 64).then_inc(S["qsd_ready"], 1)

            def scores_out(n):
                act.wait_ge(S["sc_mm"], 3 * l + n + 1)
                u0, u1 = ((0, 8), (16, 18), (8, 16))[n]
                dst = s_sb.rearrange("p (u z k) -> p z u k", u=UNITS, z=2)[:, :, u0:u1, :]
                if n == 1:
                    src = ps[:, 4:6, 0:256].rearrange("p z (u k) -> p z u k", u=2)
                else:
                    src = ps[:, 0:4, :].rearrange("p (z a) (b k) -> p z (a b) k", z=2, b=4)
                nc.scalar.activation(dst, src, ACT.Copy).then_inc(S["sc_copied"], 1)

            gelus(0, 8)
            q_root(0)
            gelus(8, 12)
            q_root(1)
            gelus(12, 16)
            scores_out(0)
            scores_out(1)
            gelus(16, 20)
            scores_out(2)
            gelus(20, NB0 - 4)
            for s in range(4):
                gelu_block(NB0 // 4 - 1, s, s < 2)
            act.wait_ge(S["gate_exp"], 2 * l + 1)
            nc.scalar.activation(best, best, ACT.Exp).then_inc(S["gate_exp"], 1)
            for n in range(2):
                act.wait_ge(S["sel_t"], 3 * l + n + 1)
                nc.scalar.activation(idx[:, :, n * 128:(n + 1) * 128],
                                     ps[:, n, 0:384].rearrange("p (q t) -> p q t", q=3), ACT.Copy)\
                   .then_inc(S["idx_ready"], 1)
            act.wait_ge(S["sel_t"], 3 * l + 3)
            nc.scalar.activation(idx[:, :, 256:T], ps[:, 2, 0:96].rearrange("p (q t) -> p q t", q=3), ACT.Copy)\
               .then_inc(S["idx_ready"], 1)
            def gate_high(i, q):
                act.wait_ge(S["gb_mul"], GPI * i + (q + 1 + GROUPS * l))
                t0 = 4 * GPI * i + 4 * q
                nc.scalar.activation(W[:, NB0:128, bass.ds(t0, 4)],
                                     ps[:, q % 4, :].rearrange("p (t j) -> p j t", t=4)[:, NB0:128, :], ACT.Copy)\
                    .then_inc(S["gb_cp"], 1)

            def gate_pass(i):
                for q in range(GPI):
                    gate_high(i, q)
                    if l == 0 and q in (8, 10):
                        ada_row(act, 1, i, (q - 8) // 2)

            with act.Fori(0, GROUPS // GPI) as i:
                gate_pass(i)
            high(UT2[l] + NB0)
            high(UT2[l] + NB0 + 1)
            for s in range(4):
                act.wait_ge(S["tile_done"], UT2[l] + NB0 + s + 1)
                high(UT2[l] + NB0 + s + 2)
                if s >= 2:
                    act.wait_ge(S["w_done"], (128 - NB0) * l + s - 1)
                nc.scalar.activation(gtmp[:, (s % 2) * T:(s % 2 + 1) * T], ps[:, 6 + s % 2, 0:T], ACT.Gelu)\
                   .then_inc(S["gelu_done"], 1)
            with act.Fori(NB0 // 4 + 1, 32) as i:
                for s in range(4):
                    act.wait_ge(S["tile_done"], 4 * i + (UT2[l] + s + 1))
                    high(UT2[l] + s + 2, i)
                    act.wait_ge(S["w_done"], 4 * i + (s - 1 - NB0 + (128 - NB0) * l))
                    nc.scalar.activation(gtmp[:, (s % 2) * T:(s % 2 + 1) * T], ps[:, 6 + s % 2, 0:T], ACT.Gelu)\
                       .then_inc(S["gelu_done"], 1)

            def w_high(j, b):
                nc.scalar.activation(w_hi[:, b], W[:, bass.ds(j, 1), :].rearrange("p a t -> p (a t)"), ACT.Copy)\
                   .then_inc(S["wh_ready"], 1)

            act.wait_ge(S["w_done"], (128 - NB0) * (l + 1))
            for b in range(2):
                nc.scalar.activation(w_hi[:, b], W[:, b], ACT.Copy).then_inc(S["wh_ready"], 1)

            def down_high(i, s):
                act.wait_ge(S["tile_done"], 4 * i + (VT[l] + s + 1))
                w_high(4 * i + (s + 2), s % 2)
                high(VT[l] + s + 2, i)

            with act.Fori(0, 31) as i:
                for s in range(4):
                    down_high(i, s)
            for s in range(2):
                down_high(31, s)

        def attention_act(act, own):
            act.wait_ge(S["tile_done"], VT[0] + 128)
            for dst, name in [(rope.rearrange("p z t -> p (z t)"), "rope"), (pmask, "pmask"), (smaskv, "smaskv"), (rotm, "rotm")]:
                act.dma_start(dst, I[name]).then_inc(S["in_att"], 16)

            def load_kv(n):
                half, v, b = n // 8, n % 8 // 4, n // 8 * 4 + n % 4
                if n >= 3:
                    act.wait_ge(S["kv_used"], n - 2)
                act.dma_start(kv_buf[n % 3], I["vc" if v else "kc"][b]).then_inc(S[f"in_kv{n % 3}"], 16)

            for n in range(3):
                load_kv(n)

            def qk_root(gs):
                act.wait_ge(S["aq_ms"], gs + 1)
                nc.scalar.activation(ars, ps[:, 4:8, 0:T], ACT.Sqrt, bias=eps_c[:, :], scale=1.0 / E)\
                   .then_inc(S["aq_sd"], 1)

            for gs in range(6):
                if gs:
                    qk_root(gs - 1)
                act.wait_ge(S["tile_done"], QK + 4 * gs + 4)
                nc.scalar.activation(qk[:, 4 * gs:4 * gs + 4, :], ps[:, 0:4, 0:T], ACT.Copy)\
                   .then_inc(S["aq_copied"], 1)
            qk_root(5)
            for g in range(NG):
                act.wait_ge(S["tile_done"], VP + 4 * g + 4)
                nc.scalar.activation(v_sb[:, 0:2, g, :], ps[:, 0:2, :], ACT.Copy)
                nc.scalar.activation(v_sb[0:32, 2, g, :], ps[0:32, 2, :], ACT.Copy).then_inc(S["v_copied"], 1)
                if g == 1:
                    for n in range(3, 7):
                        load_kv(n)
            act.wait_ge(S["aq_done"], 6)
            act.wait_ge(S["v_copied"], NG)
            act.dma_start(O["qk"], qk).then_inc(S["kv_out"], 16)
            act.dma_start(O["v"], v_sb[:, 0:2]).then_inc(S["kv_out"], 16)
            act.dma_start(O["v_s"], v_sb[0:32, 2]).then_inc(S["kv_out"], 16)
            nkv = [7]

            def more(n):
                while nkv[0] < n:
                    load_kv(nkv[0])
                    nkv[0] += 1

            def sample_exp(hf):
                act.wait_ge(S["ss_max"], hf + 1)
                nc.scalar.activation(ps_s, ps_s, ACT.Exp, bias=sst[:, 0:1], accum_out=sst[:, 1:2])\
                   .then_inc(S["ss_exp"], 1)

            def sample_t(hf):
                act.wait_ge(S["ss_t"], hf + 1)
                nc.scalar.activation(pts, ps[:, 2:4, :].rearrange("p b n -> p (b n)")[:, 0:CK]
                                     .rearrange("p (k r) -> p k r", k=7), ACT.Copy)
                nc.scalar.activation(ptn[0:32], ps[0:32, 7, 0:384].rearrange("p (g r) -> p g r", g=3), ACT.Copy)\
                   .then_inc(S["ss_cp"], 1)

            def unit_exp(u):
                w = 384 * (u // H + 1)
                p = p_sb[u % 3][:, 0:w]
                act.wait_ge(S["us_max"], u + 1)
                nc.scalar.activation(p, p, ACT.Exp, bias=ust[:, 0, u:u + 1], accum_out=ust[:, 1, u:u + 1])\
                   .then_inc(S["us_exp"], 1)

            def unit_t(u):
                w = 384 * (u // H + 1)
                act.wait_ge(S["us_t"], u + 1)
                if u >= 2:
                    act.wait_ge(S["us_pv"], u - 1)
                nc.scalar.activation(pt_sb[u % 2][:, 0:w], ps[:, 2:4, :].rearrange("p b n -> p (b n)")[:, 0:w],
                                     ACT.Copy).then_inc(S["us_cpa"], 1)

            for hf in range(2):
                more(8 * hf + 7)
                sample_exp(hf)
                unit_exp(8 * hf)
                sample_t(hf)
                for u in range(8 * hf, 8 * hf + 8):
                    if u % 8 < 7:
                        unit_exp(u + 1)
                    unit_t(u)
                    if u % 2 == 0 and u > 8 * hf:
                        more(min(8 * hf + 7 + (u - 8 * hf) // 2, 16))
                more(min(8 * hf + 11, 16))

        @block.scalar
        def _(act):
            own = Count(act, S["a_own"])
            setup = [(ccol[:, :], "ccol"), (consts[:, :], "consts"), (gain_t[:, :], "gain"),
                     (bias_t[:, :], "bias"), (xT_t[:, :], "xT"), (smask, "smask"),
                     (h0d, "h0d")]
            for dst, name in setup:
                act.dma_start(dst, I[name]).then_inc(S["in_setup"], 16)
            for dst, name in [(lre, "lre"), (lim, "lim"), (ldt, "ldt"), (sbre, "sbre"), (sbim, "sbim")]:
                act.dma_start(dst, I[name]).then_inc(S["in_s5"], 16)
            act.dma_start(cb[:, 0:2], I["cri"].rearrange("p (z k m) -> p z k m", z=2, k=PAIRS))\
               .then_inc(S["in_s5"], 16)
            act.wait_ge(S["in_setup"], 16 * 7)
            nc.scalar.activation(ccol[:, :], ccol[:, :], ACT.Silu).then_inc(S["silu_c"], 1)
            act.wait_ge(S["in_s5"], 16 * 6)
            nc.scalar.activation(ldt, ldt, ACT.Exp).then_inc(S["s5_trig"], 1)
            act.wait_ge(S["s5_thr"], 1)
            nc.scalar.activation(ssin, sth, ACT.Sin)
            nc.scalar.activation(scos, sth, ACT.Sin, scale=0.5).then_inc(S["s5_trig"], 1)
            act.wait_ge(S["s5_thr"], 2)
            nc.scalar.activation(sr, sr, ACT.Exp).then_inc(S["s5_trig"], 1)
            for n in range(12):
                ada_row(act, 0, n // 2, n % 2, 2 + 2 * (n // 2 % 2))
            act.wait_ge(S["s5_tab"], 1)
            for z, (src, dst) in enumerate(((sbre, bb_re), (sbim, bb_im))):
                for gl in range(8):
                    ins = nc.scalar.activation(dst[:, :, gl, :], src.rearrange("p (c n) -> p c n", c=NC),
                                               ACT.Copy, scale=gmask[:, gl:gl + 1])
            ins.then_inc(S["s5_bb"], 1)

            def root_mean(q, bank=7):
                act.wait_ge(S["ms_ready"], q + 1)
                nc.scalar.activation(rstd, ps[:, bank, 0:T], ACT.Sqrt, bias=eps_c[:, :], scale=1.0 / D)\
                   .then_inc(S["std_ready"], 1)

            root_mean(0)
            act.wait_ge(S["s5_bb"], 1)
            for k in range(PAIRS):
                if k >= 2:
                    act.wait_ge(S["s5_z"], k - 1)
                    nc.scalar.activation(zl[:, :, k - 2], zin[k % 2][:, :, 255:T:4], ACT.Copy).then_inc(S["s5_zl"], 1)
                nc.scalar.activation(rm5[k % 2], smask, ACT.Copy, scale=r_col[:, k:k + 1])
                nc.scalar.activation(hr5[k % 2], h0[:, :, k, :], ACT.Copy, scale=r_col[:, k:k + 1])\
                    .then_inc(S["s5_rmr"], 1)
            for k in (PAIRS - 2, PAIRS - 1):
                act.wait_ge(S["s5_z"], k + 1)
                nc.scalar.activation(zl[:, :, k], zin[k % 2][:, :, 255:T:4], ACT.Copy).then_inc(S["s5_zl"], 1)
            act.wait_ge(S["s5_rm"], 1)
            act.dma_start(O["st"], st_t).then_inc(S["st_out"], 16)
            def sigmoids(i, first):
                for m in range(2):
                    act.wait_ge(S["tile_done"], 4 * i + (GLU + 2 * m + 2))
                    if not first:
                        act.wait_ge(S["glu_used"], 2 * i + (m - 1))
                    nc.scalar.activation(gtmp[:, m * T:(m + 1) * T], ps[:, 2 * m + 1, 0:T], ACT.Sigmoid)\
                       .then_inc(S["glu_sig"], 1)

            sigmoids(0, True)
            with act.Fori(1, 4) as i:
                sigmoids(i, False)
            root_mean(1)
            act.wait_ge(S["st_out"], 16)
            peer_act(act, 0)
            root_mean(2)
            attention_act(act, own)
            root_mean(3)
            act.wait_ge(S["kv_out"], 48)
            peer_act(act, 1)

        def attention_pe(pe, wide):
            mm = nc.tensor.matmul
            pe.wait_ge(S["h_ready"], 3)

            def norm(gs):
                pe.wait_ge(S["aq_sq"], gs + 1)
                if gs:
                    pe.wait_ge(S["aq_done"], gs)
                for m in range(4):
                    ins = mm(ps[:, 4 + m, 0:T], blk64, asq[:, m, :], start=True, stop=True)
                ins.then_inc(S["aq_ms"], 1)

            def rotate(gs):
                pe.wait_ge(S["aq_qn"], gs + 1)
                for m in range(4):
                    ins = mm(ps[:, 4 + m, 0:T], rotm, qk[:, 4 * gs + m, :], start=True, stop=True)
                ins.then_inc(S["aq_rot"], 1)

            for gs in range(6):
                if gs:
                    pe.wait_ge(S["aq_copied"], gs)
                for m in range(4):
                    if gs and m == 1:
                        norm(gs - 1)
                    if gs and m == 3:
                        rotate(gs - 1)
                    wide(QK + 4 * gs + m, m, ps[:, m, 0:T], hT).then_inc(S["tile_done"], 1)
            def kv(n):
                pe.wait_ge(S[f"in_kv{n % 3}"], 16 * (n // 3 + 1))
                return kv_buf[n % 3]

            def sample_scores(hf):
                if hf:
                    pe.wait_ge(S["us_max"], H)
                for bb in range(4):
                    b = 4 * hf + bb
                    kb = kv(8 * hf + bb).rearrange("p (q k) -> p q k", q=HP)
                    rows = slice(32 * bb, 32 * bb + 32)
                    for g in range(NG):
                        bank, c0 = (5, 0) if g == 1 else (6, KOFF[g] - 512)
                        for q in range(HP):
                            ins = mm(ps[rows, bank, c0:c0 + NK[g]], qz[:, g, b, q, :, :].rearrange("p h t -> p (h t)"),
                                     kb[:, q, KOFF[g]:KOFF[g] + NK[g]], start=(q == 0), stop=(q == HP - 1))
                    ins.then_inc(S["kv_used"], 1)
                    for g in range(NG):
                        c0 = NEWC - 512 + 32 * g
                        for q in range(HP):
                            ins = mm(ps[rows, 6, c0:c0 + 32], qz[:, g, b, q, :, :].rearrange("p h t -> p (h t)"),
                                     qk[:, 8 * g + 4 + q, 256:T], start=(q == 0), stop=(q == HP - 1))
                ins.then_inc(S["ss_mm"], 1)

            pe.wait_ge(S["aq_copied"], 6)
            for g in range(NG):
                if g:
                    pe.wait_ge(S["v_copied"], g)
                for s in range(4):
                    tile_wait(pe, VP + 4 * g + s)
                    for z in range(2):
                        c = 2 * s + z
                        for a, n in ((0, 128), (1, 128), (2, 32)):
                            ins = mm(ps[0:n, a, :], hT[:, c, 128 * a:128 * a + n], ring[:, s, z * 512:(z + 1) * 512],
                                     start=(c == 0), stop=(c == NC - 1))
                    ins.then_inc(S["tile_done"], 1)
                    if g == 0 and s == 0:
                        norm(5)
                    if g == 0 and s == 2:
                        rotate(5)
                if g == 1:
                    pe.wait_ge(S["aq_done"], 6)
                    pe.wait_ge(S["qz_ready"], 1)
                    sample_scores(0)
            pe.wait_ge(S["v_copied"], NG)

            def sample_turn(hf):
                pe.wait_ge(S["ss_norm"], hf + 1)
                if hf:
                    pe.wait_ge(S["oT_ready"], hf)
                for k in range(7):
                    nc.tensor.transpose(ps[:, 2 + k // 4, (k % 4) * 128:(k % 4 + 1) * 128],
                                        ps_s[:, 128 * k:128 * k + 128], ident)
                for g in range(NG):
                    ins = nc.tensor.transpose(ps[0:32, 7, g * 128:(g + 1) * 128],
                                              ps_s[:, NEWC + 32 * g:NEWC + 32 * g + 32], ident)
                ins.then_inc(S["ss_t"], 1)

            def sample_pv(hf, bb):
                vb = kv(8 * hf + 4 + bb).rearrange("p (k n) -> p k n", k=7)
                r = slice(32 * bb, 32 * bb + 32)
                for k in range(7):
                    ins = mm(ps[r, 7, :], pts[:, k, r], vb[:, k, :], start=(k == 0), stop=False)
                ins.then_inc(S["kv_used"], 1)
                for g in range(NG):
                    ins = mm(ps[r, 7, :], ptn[0:32, g, r], v_sb[0:32, 2, g, :], start=False, stop=(g == NG - 1))
                if bb == 3:
                    ins.then_inc(S["ss_pv"], 1)

            def sample_fold(hf):
                pe.wait_ge(S["ss_oc"], hf + 1)
                for q in range(HP):
                    ins = nc.tensor.transpose(ps[:, 2, 128 * q:128 * q + 128], ps_s[:, 128 * q:128 * q + 128], ident)
                ins.then_inc(S["ss_ot"], 1)

            def unit_scores(u):
                qt, h = u // H, u % H
                r = slice(64 * (h % 2), 64 * (h % 2) + 64)
                if u >= 2:
                    pe.wait_ge(S["us_max"], u - 1)
                if h == 1:
                    pe.wait_ge(S["ss_max"], qt + 1)
                w, b0 = 128 * (qt + 1), 5 * (u % 2)
                for g in range(NG):
                    bank, c0 = (b0, g * w) if g * w < 512 else (b0 + 1, 0)
                    ins = mm(ps[:, bank, c0:c0 + w], qk[r, 8 * g + h // 2, 128 * qt:128 * qt + 128],
                             qk[r, 8 * g + 4 + h // 2, 0:w], start=True, stop=True)
                ins.then_inc(S["us_mm"], 1)

            def unit_turn(u):
                pe.wait_ge(S["us_norm"], u + 1)
                if u:
                    pe.wait_ge(S["us_cpa"], u)
                if u % H == 0:
                    pe.wait_ge(S["ss_cp"], u // H + 1)
                for k in range(NG * (u // H + 1)):
                    ins = nc.tensor.transpose(ps[:, 2 + k // 4, (k % 4) * 128:(k % 4 + 1) * 128],
                                              p_sb[u % 3][:, 128 * k:128 * k + 128], ident)
                ins.then_inc(S["us_t"], 1)

            def unit_pv(u):
                qt, h = u // H, u % H
                pe.wait_ge(S["us_cpa"], u + 1)
                if u:
                    pe.wait_ge(S["us_o"], u)
                r = slice(64 * (h % 2), 64 * (h % 2) + 64)
                n = NG * (qt + 1)
                for k in range(n):
                    g, kt = k // (qt + 1), k % (qt + 1)
                    ins = mm(ps[r, 4, 0:128], v_sb[:, kt, g, 64 * h:64 * h + 64],
                             pt_sb[u % 2][:, 128 * k:128 * k + 128], start=(k == 0), stop=(k == n - 1))
                ins.then_inc(S["us_pv"], 1)

            for hf in range(2):
                if hf:
                    sample_scores(hf)
                u0 = 8 * hf
                unit_scores(u0)
                sample_turn(hf)
                unit_scores(u0 + 1)
                for u in range(u0, u0 + 8):
                    unit_turn(u)
                    if u + 2 < u0 + 8:
                        unit_scores(u + 2)
                    if u > u0:
                        unit_pv(u - 1)
                    if u % 2:
                        sample_pv(hf, (u - u0) // 2)
                unit_pv(u0 + 7)
                sample_fold(hf)
            pe.wait_ge(S["oT_ready"], 2)
            for s in range(4):
                for z in range(2):
                    ins = wide(WO + s, s, ps[:, 2 * s + z, 0:T], oT, 0, HP, z * 512)
                ins.then_inc(S["tile_done"], 1)

        @block.tensor
        def _(pe):
            mm = nc.tensor.matmul

            def ada_tile(l, nb, c, bank=4, i=0):
                tile_wait(pe, ADA[l] + 8 * nb + c, 2 * i)
                for z in range(2):
                    ins = mm(ps[0:ROWS, bank + z, :], ccol[:, c * ROWS:(c + 1) * ROWS],
                             ring[:, c % RING, 512 * z:512 * z + 512], start=(c == 0), stop=(c == NC - 1))
                ins.then_inc(S["tile_done"], 1)

            def ada_turn(l, nb, half):
                pe.wait_ge(S["ada_row"], 2 * nb + (12 * l + half + 1))
                for q in range(4):
                    ins = mm(ps[:, 6, bass.ds((8 * nb + 4 * half + q) * ROWS, ROWS)],
                             gtmp[0:ROWS, 128 * q:128 * q + 128], ident[0:ROWS, 0:ROWS], start=True, stop=True)
                ins.then_inc(S["ada_turned"], 1)

            def mean_square(q):
                pe.wait_ge(S["sq_ready"], q + 1)
                for c in range(NC):
                    ins = mm(ps[:, 7, 0:T], ones, modsq[:, c, :] if q else hT[:, c, :], start=(c == 0), stop=(c == NC - 1))
                ins.then_inc(S["ms_ready"], 1)

            def wide(n, s, out, rhs, i=0, chunks=NC, off=0):
                tile_wait(pe, n, i)
                for c in range(chunks):
                    ins = mm(out, ring[:, s, off + c * 128:off + (c + 1) * 128], rhs[:, c, :], start=(c == 0),
                             stop=(c == chunks - 1))
                return ins

            pe.wait_ge(S["in_setup"], 16 * 7)
            pe.wait_ge(S["silu_c"], 1)
            for nb in range(7):
                for c in range(NC):
                    if nb < 6:
                        if nb >= 2 and c == 0:
                            pe.wait_ge(S["ada_row"], 2 * nb - 2)
                        ada_tile(0, nb, c, 2 + 2 * (nb % 2))
                    if nb and c in (2, 5):
                        ada_turn(0, nb - 1, c // 3)
            mean_square(0)

            pe.wait_ge(S["s5_bb"], 1)
            pe.wait_ge(S["h_ready"], 1)
            pe.wait_ge(S["s5_cs"], 1)

            def s5_in(k):
                if k >= 3:
                    pe.wait_ge(S["s5_rot"], k - 2)
                c, gl = k // 4, 2 * (k % 4)
                for z, b in enumerate((bb_re, bb_im)):
                    ins = mm(ps[:, BU_BANK[k % 3] + z, 0:T], b[:, c, gl:gl + 2, :].rearrange("p g n -> p (g n)"),
                             hT[:, c, :], start=True, stop=True)
                ins.then_inc(S["s5_bu"], 1)

            def s5_out(k):
                c, kk = k // 4, k % 4
                pe.wait_ge(S["s5_op"], k + 1)
                pe.wait_ge(S["s5_sin"], k + 1)
                if kk == 0 and c >= 2:
                    pe.wait_ge(S["s5_hy"], c - 1)
                o = o5[k % 2]
                for n, z in enumerate((0, 1, 1, 2)):
                    ins = mm(ps[32 * kk:32 * kk + 32, 4 + c % 2, 0:T], cb[:, z, k, :], o[:, n, :], start=(n == 0),
                             stop=(n == 3))
                ins.then_inc(S["s5_ymm"], 1)

            for k in range(PAIRS + 3):
                if k < PAIRS:
                    s5_in(k)
                if k >= 3:
                    s5_out(k - 3)

            pe.wait_ge(S["s5_hy"], NC)

            def glu(i, first):
                for m in range(2):
                    if not first:
                        pe.wait_ge(S["glu_used"], 2 * i + (m - 1))
                    for z in range(2):
                        s = 2 * m + z
                        wide(GLU + s, s, ps[:, s, 0:T], hT, i).then_inc(S["tile_done"], 1)

            glu(0, True)
            with pe.Fori(1, 4) as i:
                glu(i, False)

            def peer_pe(l):
                pe.wait_ge(S["h_ready"], 2 * l + 2)
                for m in range(8):
                    if m >= 4:
                        pe.wait_ge(S["q_copied"], 8 * l + m - 3)
                    wide(PQ[l] + m, m % 4, ps[:, m % 4, 0:T], modsq).then_inc(S["tile_done"], 1)

                def up(j, s, out):
                    pe.wait_ge(S["hi_ready"], j + (256 * l + s + 1))
                    for c in range(NC):
                        w = wt_hi[:, s % 2, c * 128:(c + 1) * 128]
                        mm(out, w, h_hi[:, c], start=(c == 0), stop=False)
                        mm(out, w, h_lo[:, c], start=False, stop=False)
                    pe.wait_ge(S["lo_u"], j + (128 * l + s + 1))
                    for c in range(NC):
                        ins = mm(out, ring_lo[:, s, c * 128:(c + 1) * 128], h_hi[:, c], start=False,
                                 stop=(c == NC - 1))
                    ins.then_inc(S["tile_done"], 1)

                def experts(j0, j1):
                    with pe.Fori(j0 // 4, j1 // 4) as i:
                        for s in range(4):
                            pe.wait_ge(S["gelu_done"], 4 * i + (s - 1 + 128 * l))
                            up(4 * i, s, ps[:, 6 + s % 2, 0:T])

                def q_norm(n):
                    pe.wait_ge(S["qsq_ready"], l + 1)
                    if n:
                        pe.wait_ge(S["qsd_ready"], 2 * l + 1)
                    for m in range(4):
                        ins = mm(ps[:, m, 0:T], blk64, qsq[:, 4 * n + m, :], start=True, stop=True)
                    ins.then_inc(S["qms_ready"], 1)

                def scores(n):
                    if n == 0:
                        pe.wait_ge(S["qn_ready"], l + 1)
                        pe.wait_ge(S["gate_in"], 48 * (l + 1))
                    if n == 2:
                        pe.wait_ge(S["sc_copied"], 3 * l + 1)
                    for h in range(PH):
                        for z in range(2):
                            r = slice(64 * z, 64 * z + 64)
                            if n != 1:
                                t0 = 128 * (n // 2)
                                out = ps[:, 2 * z + h // 4, (h % 4) * 128:(h % 4 + 1) * 128]
                                lhs = qraw[r, h, t0:t0 + 128]
                            else:
                                q = 32 * (h % 4)
                                out = ps[q:q + 32, 4 + z, (h // 4) * 128:(h // 4 + 1) * 128]
                                lhs = qraw[r, h, 256:T]
                            ins = mm(out, lhs, subk[r, h, :], start=True, stop=True)
                    ins.then_inc(S["sc_mm"], 1)

                pe.wait_ge(S["hh_ready"], l + 1)
                pe.wait_ge(S["hl_ready"], l + 1)
                for s in range(4):
                    if s >= 2:
                        pe.wait_ge(S["gelu_done"], 128 * l + s - 1)
                    up(0, s, ps[:, 6 + s % 2, 0:T])
                experts(4, 8)
                q_norm(0)
                experts(8, 12)
                q_norm(1)
                experts(12, 16)
                scores(0)
                scores(1)
                experts(16, 20)
                scores(2)
                experts(20, NB0)
                pe.wait_ge(S["sel_ready"], l + 1)
                pe.wait_ge(S["sc_copied"], 3 * l + 3)
                for n in range(2):
                    for q in range(3):
                        ins = nc.tensor.transpose(ps[:, n, 128 * q:128 * q + 128],
                                                  sel3[:, q, 8 * n:8 * n + 8, :].rearrange("p u k -> p (u k)"), ident)
                    ins.then_inc(S["sel_t"], 1)
                for q in range(3):
                    ins = mm(ps[:, 2, 32 * q:32 * q + 32], selz[:, q, :], jsel, start=True, stop=True)
                ins.then_inc(S["sel_t"], 1)
                pe.wait_ge(S["idx_ready"], 3 * l + 3)

                def gates(i, q, first):
                    n = q + GROUPS * l
                    pe.wait_ge(S["gb_o1"], GPI * i + (n + 1))
                    pe.wait_ge(S["gb_gate"], GPI * i + (n + 1))
                    if q >= 4 or not first:
                        pe.wait_ge(S["gb_cp"], GPI * i + (n - 3))
                    for t in range(4):
                        ins = mm(ps[:, q % 4, 128 * t:128 * t + 128], oh[:, 0, q % 2, t, :], oh[:, 1, q % 2, t, :],
                                 start=True, stop=True)
                    ins.then_inc(S["gb_mm"], 1)

                def gate_pass(i, first):
                    for q in range(GPI):
                        gates(i, q, first)
                        if l == 0:
                            if q < NC:
                                ada_tile(1, 0, q, 4, i)
                            if q in (9, 11):
                                ada_turn(1, i, (q - 9) // 2)

                if l == 0:
                    pe.wait_ge(S["gelu_done"], NB0)
                gate_pass(0, True)
                with pe.Fori(1, GROUPS // GPI) as i:
                    gate_pass(i, False)
                if l == 0:
                    pe.wait_ge(S["ada_done"], 2)
                experts(NB0, 128)
                pe.wait_ge(S["w_done"], (128 - NB0) * (l + 1))
                pe.wait_ge(S["gb_cp"], GROUPS * (l + 1))

                def down(i, first, last=False):
                    for s in range(4):
                        pe.wait_ge(S["hi_ready"], 4 * i + (256 * l + 128 + s + 1))
                        pe.wait_ge(S["wh_ready"], 4 * i + (128 * l + s + 1))
                        for c in range(NC):
                            mm(ps[:, c, 0:T], wt_hi[:, s % 2, c * 128:(c + 1) * 128], w_hi[:, s % 2],
                               start=(first and s == 0), stop=False, skip_group_check=True)
                        pe.wait_ge(S["wl_ready"], 4 * i + (128 * l + s + 1))
                        for c in range(NC):
                            mm(ps[:, c, 0:T], wt_hi[:, s % 2, c * 128:(c + 1) * 128], w_lo[:, s % 2],
                               start=False, stop=False, skip_group_check=True)
                        pe.wait_ge(S["lo_v"], 4 * i + (128 * l + s + 1))
                        for c in range(NC):
                            ins = mm(ps[:, c, 0:T], ring_lo[:, s, c * 128:(c + 1) * 128], w_hi[:, s % 2],
                                     start=False, stop=(last and s == 3), skip_group_check=True)
                        ins.then_inc(S["tile_done"], 1)

                down(0, True)
                with pe.Fori(1, 31) as i:
                    down(i, False)
                down(31, False, True)

            mean_square(1)
            peer_pe(0)
            mean_square(2)
            attention_pe(pe, wide)
            mean_square(3)
            peer_pe(1)

        def attention_dve(v, own, residual):
            TT, TS, STT, CP = (nc.vector.tensor_tensor, nc.vector.tensor_scalar, nc.vector.scalar_tensor_tensor,
                               nc.vector.tensor_copy)
            v.wait_ge(S["in_att"], 64)

            def finish(gs):
                q = qk[:, 4 * gs:4 * gs + 4, :]
                v.wait_ge(S["aq_rot"], gs + 1)
                own(TT(asq, ps[:, 4:8, 0:T], rope[:, 1].unsqueeze(1).broadcast_to([P, 4, T]), ALU.mult))
                own(TT(q, q, rope[:, 0].unsqueeze(1).broadcast_to([P, 4, T]), ALU.mult))
                own.settle()
                TT(q, q, asq, ALU.add).then_inc(S["aq_done"], 1)

            def scale_qk(gs):
                q = qk[:, 4 * gs:4 * gs + 4, :]
                v.wait_ge(S["aq_sd"], gs + 1)
                own(nc.vector.reciprocal(ars, ars))
                own.settle()
                STT(out=q, in0=q, scalar=(kg if gs % 2 else qg), in1=ars, op0=ALU.mult, op1=ALU.mult)\
                    .then_inc(S["aq_qn"], 1)
                v.wait_ge(S["aq_qn"], gs + 1)

            for gs in range(6):
                if gs:
                    scale_qk(gs - 1)
                    finish(gs - 1)
                    v.wait_ge(S["aq_done"], gs)
                v.wait_ge(S["aq_copied"], gs + 1)
                q = qk[:, 4 * gs:4 * gs + 4, :]
                TT(asq, q, q, ALU.mult).then_inc(S["aq_sq"], 1)
            scale_qk(5)
            finish(5)

            def sample_max(hf):
                v.wait_ge(S["ss_mm"], hf + 1)
                own(STT(out=ps_s[:, 0:512], in0=ps[:, 5, :], scalar=E ** -0.5, in1=smaskv[:, 0:512],
                        op0=ALU.mult, op1=ALU.add))
                own(STT(out=ps_s[:, 512:CK], in0=ps[:, 6, 0:CK - 512], scalar=E ** -0.5, in1=smaskv[:, 512:CK],
                        op0=ALU.mult, op1=ALU.add))
                own(STT(out=ps_s[:, CK:SW], in0=ps[:, 6, CK - 512:SW - 512], scalar=E ** -0.5,
                        in1=smaskv[:, CK + 96 * hf:CK + 96 * hf + 96], op0=ALU.mult, op1=ALU.add))
                own.settle()
                own(nc.vector.tensor_reduce(sst[:, 2:3], ps_s, X, ALU.max))
                own.settle()
                TS(sst[:, 0:1], sst[:, 2:3], -1.0, None, ALU.mult).then_inc(S["ss_max"], 1)

            def sample_norm(hf):
                v.wait_ge(S["ss_exp"], hf + 1)
                own(nc.vector.reciprocal(sst[:, 3:4], sst[:, 1:2]))
                own.settle()
                TS(ps_s, ps_s, sst[:, 3:4], None, ALU.mult).then_inc(S["ss_norm"], 1)

            def sample_out(hf):
                v.wait_ge(S["ss_pv"], hf + 1)
                CP(ps_s[:, 0:512], ps[:, 7, :]).then_inc(S["ss_oc"], 1)
                v.wait_ge(S["ss_ot"], hf + 1)
                t0 = 256 + 16 * hf
                for q in range(HP):
                    for h2 in range(2):
                        r, c = slice(64 * h2, 64 * h2 + 64), 8 * q + 4 * h2
                        src = ps[r, 2, 128 * q:128 * q + 128].rearrange("p (b n) -> p b n", b=4)[:, :, c:c + 4]
                        ins = CP(oT[r, q, t0:t0 + 16].rearrange("p (b t) -> p b t", b=4), src)
                ins.then_inc(S["oT_ready"], 1)

            def unit_max(u):
                qt = u // H
                w = 384 * (qt + 1)
                v.wait_ge(S["us_mm"], u + 1)
                if u >= 3:
                    v.wait_ge(S["us_t"], u - 2)
                p, b0 = p_sb[u % 3][:, 0:w], 5 * (u % 2)
                own(STT(out=p, in0=ps[:, b0:b0 + 2, :].rearrange("p b n -> p (b n)")[:, 0:w], scalar=E ** -0.5,
                        in1=pmask[:, 384 * qt:384 * qt + w], op0=ALU.mult, op1=ALU.add))
                own.settle()
                own(nc.vector.tensor_reduce(ust[:, 2, u:u + 1], p, X, ALU.max))
                own.settle()
                TS(ust[:, 0, u:u + 1], ust[:, 2, u:u + 1], -1.0, None, ALU.mult).then_inc(S["us_max"], 1)

            def unit_den(u):
                v.wait_ge(S["us_exp"], u + 1)
                nc.vector.reciprocal(ust[:, 1, u:u + 1], ust[:, 1, u:u + 1]).then_inc(S["us_den"], 1)

            def unit_out(u):
                qt, h = u // H, u % H
                r = slice(64 * (h % 2), 64 * (h % 2) + 64)
                v.wait_ge(S["us_pv"], u + 1)
                CP(oT[r, h // 2, 128 * qt:128 * qt + 128], ps[r, 4, 0:128]).then_inc(S["us_o"], 1)

            for hf in range(2):
                u0 = 8 * hf
                sample_max(hf)
                unit_max(u0)
                sample_norm(hf)
                unit_max(u0 + 1)
                for u in range(u0, u0 + 8):
                    unit_den(u)
                    if u + 2 < u0 + 8:
                        unit_max(u + 2)
                    if u > u0:
                        unit_out(u - 1)
                unit_out(u0 + 7)
                sample_out(hf)
            v.wait_ge(S["tile_done"], WO + 4)
            residual(ada[:, 1, 2], ps[:, :, 0:T], 0, NC, gtmp[:, 0:256].rearrange("p (c t) -> p c t", c=NC), S["x_ready"])

        @block.vector
        def _(v):
            own = Count(v, S["v_own"])
            TT, TS, STT, CP = (nc.vector.tensor_tensor, nc.vector.tensor_scalar, nc.vector.scalar_tensor_tensor,
                               nc.vector.tensor_copy)
            own(nc.vector.memset(eps_c[:, :], EPS))
            v.wait_ge(S["in_setup"], 16 * 7)

            def square_x(q, dst):
                TT(dst, xT, xT, ALU.mult).then_inc(S["sq_ready"], 1)

            own.settle()
            square_x(0, hT)
            v.wait_ge(S["in_s5"], 16 * 6)
            v.wait_ge(S["s5_trig"], 1)
            own(TT(sth, lim, ldt, ALU.mult))
            own(TT(sr, lre, ldt, ALU.mult))
            own.settle()
            own(TS(sq1, sth, 1.0 / TWO_PI, MAGIC, ALU.mult, ALU.add))
            own.settle()
            own(TS(sq1, sq1, MAGIC, None, ALU.subtract))
            own.settle()
            for part in (C1, C2, C3):
                own(STT(out=sth, in0=sq1, scalar=-part, in1=sth, op0=ALU.mult, op1=ALU.add))
                own.settle()
            TS(sth, sth, PI_LO, -PI_LO, ALU.min, ALU.max).then_inc(S["s5_thr"], 1)
            v.wait_ge(S["s5_trig"], 2)
            own(TT(scos, scos, scos, ALU.mult))
            own.settle()
            TS(scos, scos, -2.0, 1.0, ALU.mult, ALU.add).then_inc(S["s5_thr"], 1)
            v.wait_ge(S["s5_trig"], 3)
            v.wait_ge(S["s5_thr"], 2)
            own(CP(r_col, sr[:, 512:LW]))
            a = slice(0, 512)
            are, aim, den, t1 = sq1[:, a], sth[:, a], ldt[:, a], st1[:, a]
            own(TT(are, sr[:, a], scos[:, a], ALU.mult))
            own(TT(aim, sr[:, a], ssin[:, a], ALU.mult))
            own(TT(den, lre[:, a], lre[:, a], ALU.mult))
            own(TT(t1, lim[:, a], lim[:, a], ALU.mult))
            own.settle()
            own(TS(are, are, 1.0, None, ALU.subtract))
            own(TT(den, den, t1, ALU.add))
            own.settle()
            own(nc.vector.reciprocal(den, den))
            own(TT(t1, are, lre[:, a], ALU.mult))
            own(TT(sr[:, a], aim, lim[:, a], ALU.mult))
            own.settle()
            own(TT(t1, t1, sr[:, a], ALU.add))
            own(TT(aim, aim, lre[:, a], ALU.mult))
            own(TT(are, are, lim[:, a], ALU.mult))
            own.settle()
            own(TT(aim, aim, are, ALU.subtract))
            own(TT(t1, t1, den, ALU.mult))
            own.settle()
            own(TT(aim, aim, den, ALU.mult))
            own.settle()
            own(TT(lre[:, a], t1, sbre, ALU.mult))
            own(TT(lim[:, a], aim, sbim, ALU.mult))
            own(TT(are, t1, sbim, ALU.mult))
            own(TT(den, aim, sbre, ALU.mult))
            own.settle()
            own(TT(sbre, lre[:, a], lim[:, a], ALU.subtract))
            own(TT(sbim, are, den, ALU.add))
            b = slice(512, LW)
            ec, es, tc, ts = scos[:, b], ssin[:, b], lre[:, b], lim[:, b]
            td = ldt[:, b]
            own(nc.vector.memset(tcos[:, :, 0:1], 1.0))
            own(nc.vector.memset(tsin[:, :, 0:1], 0.0))
            own.settle()
            n = 1
            scr = bb_im_f
            while n < 256:
                s1 = scr[:, 0:PAIRS * n].rearrange("p (k t) -> p k t", k=PAIRS)
                s2 = bb_re.rearrange("p c g n -> p (c g n)")[:, 0:PAIRS * n].rearrange("p (k t) -> p k t", k=PAIRS)
                cc, ss = (e.unsqueeze(2).broadcast_to([P, PAIRS, n]) for e in (ec, es))
                own(TT(tcos[:, :, n:2 * n], tcos[:, :, 0:n], cc, ALU.mult))
                own(TT(s1, tsin[:, :, 0:n], ss, ALU.mult))
                own(TT(tsin[:, :, n:2 * n], tsin[:, :, 0:n], cc, ALU.mult))
                own(TT(s2, tcos[:, :, 0:n], ss, ALU.mult))
                own(TT(tc, ec, ec, ALU.mult))
                own(TT(ts, es, es, ALU.mult))
                own(TT(td, ec, es, ALU.mult))
                own.settle()
                own(TT(tcos[:, :, n:2 * n], tcos[:, :, n:2 * n], s1, ALU.subtract))
                own(TT(tsin[:, :, n:2 * n], tsin[:, :, n:2 * n], s2, ALU.add))
                own(TT(ec, tc, ts, ALU.subtract))
                own(TS(es, td, 2.0, None, ALU.mult))
                own.settle()
                n *= 2
            for tab in (tcos, tsin):
                src = tab[:, :, 1:5].unsqueeze(2).broadcast_to([P, PAIRS, SB, ST])
                ins = CP(tab[:, :, 256:T].rearrange("p k (b t) -> p k b t", b=SB), src)
            ins.then_inc(S["s5_tab"], 1)

            def ada_finish(l):
                v.wait_ge(S["ada_turned"], 12 * (l + 1))
                flat = ada_t[:, l * 48 * ROWS:(l + 1) * 48 * ROWS].rearrange("p (m r) -> p m r", r=ROWS)
                own(TT(flat, ps[:, 6, 0:48 * ROWS].rearrange("p (m r) -> p m r", r=ROWS),
                       bias_t[:, 48 * l:48 * l + 48].unsqueeze(2).broadcast_to([P, 48, ROWS]), ALU.add))
                own.settle()
                for w in range(2):
                    sc = ada[:, l, 3 * w + 1]
                    g0 = (2 * l + w) * NC
                    ins = STT(out=sc, in0=sc, scalar=1.0,
                              in1=gain_t[:, g0:g0 + NC].unsqueeze(2).broadcast_to([P, NC, ROWS]),
                              op0=ALU.add, op1=ALU.mult)
                ins.then_inc(S["ada_done"], 1)

            def by_sample(row):
                return row.unsqueeze(3).broadcast_to([P, row.shape[1], SB, ST])

            def tokens4(x):
                return x.rearrange("p c (b t) -> p c b t", b=SB)

            def modulate(q):
                l, w = q // 2, q % 2
                v.wait_ge(S["std_ready"], q + 1)
                own(nc.vector.reciprocal(rstd, rstd))
                own.settle()
                h = modsq if w else hT
                own(TT(h, xT, rstd.unsqueeze(1).broadcast_to([P, NC, T]), ALU.mult))
                own.settle()
                sc, sh = ada[:, l, 3 * w + 1], ada[:, l, 3 * w]
                own(TT(tokens4(h[:, :, 256:T]), tokens4(h[:, :, 256:T]), by_sample(sc[:, :, 1:]), ALU.mult))
                for c in range(NC):
                    own(TS(h[:, c, 0:256], h[:, c, 0:256], sc[:, c, 0:1], sh[:, c, 0:1], ALU.mult, ALU.add))
                own.settle()
                TT(tokens4(h[:, :, 256:T]), tokens4(h[:, :, 256:T]), by_sample(sh[:, :, 1:]), ALU.add)\
                    .then_inc(S["h_ready"], 1)

            def residual(gate, src, m0, m1, tmp, done):
                own(TT(tokens4(tmp), tokens4(src[:, :, 256:T]), by_sample(gate[:, m0:m1, 1:]), ALU.mult))
                for m in range(m0, m1):
                    own(STT(out=xT[:, m, 0:256], in0=src[:, m - m0, 0:256], scalar=gate[:, m, 0:1],
                            in1=xT[:, m, 0:256], op0=ALU.mult, op1=ALU.add))
                own.settle()
                TT(xT[:, m0:m1, 256:T], xT[:, m0:m1, 256:T], tmp, ALU.add).then_inc(done, 1)

            ada_finish(0)
            v.wait_ge(S["ada_done"], 1)
            modulate(0)
            v.wait_ge(S["h_ready"], 1)
            v.wait_ge(S["s5_bb"], 1)

            def twice(table):
                return table.unsqueeze(1).broadcast_to([P, 2, T])

            def rot_in(k):
                v.wait_ge(S["s5_bu"], k + 1)
                if k >= 2:
                    v.wait_ge(S["s5_zin"], k - 1)
                reim, m = ps[:, BU_BANK[k % 3]:BU_BANK[k % 3] + 2, 0:T], m5[k % 2]
                TT(m[:, 0:2], twice(tcos[:, k]), reim, ALU.mult)
                TT(m[:, 2:4], twice(tsin[:, k]), reim, ALU.mult).then_inc(S["s5_rot"], 1)

            def scan(k):
                v.wait_ge(S["s5_zin"], k + 1)
                v.wait_ge(S["s5_rmr"], k + 1)
                for z in range(2):
                    ins = nc.vector.tensor_tensor_scan(zin[k % 2][:, z], rm5[k % 2], zin[k % 2][:, z], 0.0,
                                                       ALU.mult, ALU.add)
                ins.then_inc(S["s5_z"], 1)
                v.wait_ge(S["s5_z"], k + 1)
                if k >= 2:
                    v.wait_ge(S["s5_ymm"], k - 1)
                TT(o5[k % 2][:, 0:2], twice(tcos[:, k]), zin[k % 2], ALU.mult)
                TT(o5[k % 2][:, 2], tsin[:, k], zin[k % 2][:, 0], ALU.mult).then_inc(S["s5_op"], 1)

            def chunk_y(c):
                v.wait_ge(S["s5_ymm"], 4 * c + 4)
                STT(out=hT[:, c], in0=hT[:, c], scalar=dskip[:, c:c + 1], in1=ps[:, 4 + c % 2, 0:T],
                    op0=ALU.mult, op1=ALU.add).then_inc(S["s5_hy"], 1)

            for k in range(PAIRS + 3):
                if k < PAIRS:
                    rot_in(k)
                if 1 <= k <= PAIRS:
                    scan(k - 1)
                if k >= 6 and (k - 6) % 4 == 0:
                    chunk_y((k - 6) // 4)
            for m in range(NC):
                v.wait_ge(S["glu_sig"], m + 1)
                g = gtmp[:, (m % 2) * T:(m % 2 + 1) * T]
                TT(g, ps[:, 2 * (m % 2), 0:T], g, ALU.mult).then_inc(S["glu_used_v"], 1)
                v.wait_ge(S["glu_used_v"], m + 1)
                residual(ada[:, 0, 2], g.unsqueeze(1), m, m + 1, small[:, 64:96].unsqueeze(1), S["glu_used"])
            v.wait_ge(S["glu_used"], NC)
            v.wait_ge(S["s5_rm"], 1)
            square_x(1, modsq)

            def peer_dve(l):
                last = S["q_copied"]
                v.wait_ge(last, 8 * l + 8)
                TT(qsq, qraw, qraw, ALU.mult).then_inc(S["qsq_ready"], 1)
                v.wait_ge(S["qsd_ready"], 2 * l + 2)
                own(nc.vector.reciprocal(qrs, qrs))
                own.settle()
                TT(qraw, qraw, qrs, ALU.mult).then_inc(S["qn_ready"], 1)
                v.wait_ge(S["sc_copied"], 3 * l + 3)
                s4 = s_sb.rearrange("p (u z k) -> p u z k", u=UNITS, z=2)
                s24 = s_two.rearrange("p (u z k) -> p u z k", u=UNITS, z=2)
                uz = [(u, z) for u in range(UNITS) for z in range(2)]
                VM, VI, MR = nc.vector.max, nc.vector.max_index, nc.vector.match_replace
                for u, z in uz:
                    own(VM(v16[:, u, z, 0:8], s4[:, u, z]))
                own.settle()
                for u, z in uz:
                    own(VI(i16u[:, u, z, 0:8], v16[:, u, z, 0:8], s4[:, u, z]))
                    own(MR(s24[:, u, z], v16[:, u, z, 0:8], s4[:, u, z], -3.0e38))
                own.settle()
                for u, z in uz:
                    own(VM(v16[:, u, z, 8:16], s24[:, u, z]))
                own.settle()
                for u, z in uz:
                    own(VI(i16u[:, u, z, 8:16], v16[:, u, z, 8:16], s24[:, u, z]))
                c4 = cand.rearrange("p (u a b) -> p u a b", u=UNITS, a=16)
                own(TT(c4, v16[:, :, 0].unsqueeze(3).broadcast_to([P, UNITS, 16, 16]),
                       v16[:, :, 1].unsqueeze(2).broadcast_to([P, UNITS, 16, 16]), ALU.add))
                own.settle()
                own(CP(i16f, i16u))
                cu = cand.rearrange("p (u n) -> p u n", u=UNITS)
                c2 = s_sb.rearrange("p (u n) -> p u n", u=UNITS)
                for u in range(UNITS):
                    own(VM(best[:, u, 0:8], cu[:, u]))
                own.settle()
                for u in range(UNITS):
                    own(VI(selu[:, u, 0:8], best[:, u, 0:8], cu[:, u]))
                    own(MR(c2[:, u], best[:, u, 0:8], cu[:, u], -3.0e38))
                own.settle()
                for u in range(UNITS):
                    own(VM(best[:, u, 8:16], c2[:, u]))
                own.settle()
                for u in range(UNITS):
                    own(VI(selu[:, u, 8:16], best[:, u, 8:16], c2[:, u]))
                own(CP(gsum[:, 0:UNITS], best[:, :, 0]))
                own.settle()
                TT(best, best, gsum[:, 0:UNITS].unsqueeze(2).broadcast_to([P, UNITS, 16]), ALU.subtract)\
                    .then_inc(S["gate_exp"], 1)
                own(TS(selabu[:, 0], selu, 4, None, ALU.logical_shift_right))
                own(TS(selabu[:, 1], selu, 15, None, ALU.bitwise_and))
                own.settle()
                own(CP(selab, selabu))
                own.settle()
                e4 = eq.rearrange("p (u k a) -> p u k a", u=UNITS, k=16)
                for z in range(2):
                    own(TT(e4, selab[:, z].unsqueeze(3).broadcast_to([P, UNITS, 16, 16]),
                           iota[:, 0:16].unsqueeze(1).unsqueeze(1).broadcast_to([P, UNITS, 16, 16]), ALU.is_equal))
                    own.settle()
                    own(TT(e4, e4, i16f[:, :, z].unsqueeze(2).broadcast_to([P, UNITS, 16, 16]), ALU.mult))
                    own.settle()
                    own(nc.vector.tensor_reduce(sel3[:, z], e4, X, ALU.add))
                    own.settle()
                v.wait_ge(S["gate_exp"], 2 * l + 2)
                own(nc.vector.tensor_reduce(gsum[:, 0:UNITS], best, X, ALU.add))
                own.settle()
                own(nc.vector.reciprocal(gsum[:, 0:UNITS], gsum[:, 0:UNITS]))
                own.settle()
                own(TT(sel3[:, 2], best, gsum[:, 0:UNITS].unsqueeze(2).broadcast_to([P, UNITS, 16]), ALU.mult))
                own.settle()
                v.wait_ge(S["gate_in"], 48 * (l + 1))
                for q in range(3):
                    ins = TT(selz[:, q].rearrange("p (u h k) -> p u h k", u=2, h=4),
                             sel3[:, q, 16:18].unsqueeze(2).broadcast_to([P, 2, 4, 16]),
                             hqm.unsqueeze(1).unsqueeze(3).broadcast_to([P, 2, 4, 16]), ALU.mult)
                ins.then_inc(S["sel_ready"], 1)
                v.wait_ge(S["idx_ready"], 3 * l + 3)
                v.wait_ge(S["gelu_done"], 128 * l + NB0)

                def one_hots(i, q, first):
                    n = q + GROUPS * l
                    if q >= 2 or not first:
                        v.wait_ge(S["gb_mm"], GPI * i + (n - 1))
                    for w in (1, 0):
                        TT(oh[:, w, q % 2], iota.unsqueeze(1).broadcast_to([P, 4, 128]),
                           idx[:, w, bass.ds(4 * GPI * i + 4 * q, 4)].unsqueeze(2).broadcast_to([P, 4, 128]),
                           ALU.is_equal).then_inc(S[f"gb_o{w + 1}"], 1)

                def gate_low(i, q):
                    v.wait_ge(S["gb_mm"], GPI * i + (q + 1 + GROUPS * l))
                    w = W[:, 0:NB0, bass.ds(4 * GPI * i + 4 * q, 4)]
                    TT(w, w, ps[:, q % 4, :].rearrange("p (t j) -> p j t", t=4)[:, 0:NB0, :], ALU.mult)\
                        .then_inc(S["gb_mul"], 1)

                def gate_pass(i, first):
                    for q in range(GPI):
                        one_hots(i, q, first)
                        if q or not first:
                            gate_low(i, q - 1)

                gate_pass(0, True)
                with v.Fori(1, GROUPS // GPI) as i:
                    gate_pass(i, False)
                gate_low(GROUPS // GPI - 1, GPI - 1)
                if l == 0:
                    ada_finish(1)
                v.wait_ge(S["gb_cp"], GROUPS * (l + 1))
                v.wait_ge(S["gb_cp"], 72 * (l + 1))
                with v.Fori(NB0 // 4, 32) as i:
                    for s in range(4):
                        v.wait_ge(S["gelu_done"], 4 * i + (s + 1 + 128 * l))
                        w = W[:, bass.ds(4 * i + s, 1), :].rearrange("p a t -> p (a t)")
                        TT(w, w, gtmp[:, (s % 2) * T:(s % 2 + 1) * T], ALU.mult).then_inc(S["w_done"], 1)
                with v.Fori(0, 32) as i:
                    for s in range(4):
                        v.wait_ge(S["hi_ready"], 4 * i + (256 * l + 128 + s + 1))
                        TT(ring_lo[:, s], ring[:, s], wt_hi[:, s % 2].bitcast(F32), ALU.subtract)\
                            .then_inc(S["lo_v"], 1)
                v.wait_ge(S["tile_done"], VT[l] + 128)
                residual(ada[:, l, 5], ps[:, :, 0:T], 0, NC, gtmp[:, 0:256].rearrange("p (c t) -> p c t", c=NC),
                         S["x_ready"])

            modulate(1)
            peer_dve(0)
            v.wait_ge(S["x_ready"], 1)
            square_x(2, modsq)
            modulate(2)
            attention_dve(v, own, residual)
            v.wait_ge(S["x_ready"], 2)
            square_x(3, modsq)
            modulate(3)
            peer_dve(1)

        @block.gpsimd
        def _(pool):
            own = Count(pool, S["p_own"])
            TT, TS, CP = nc.gpsimd.tensor_tensor, nc.gpsimd.tensor_scalar, nc.gpsimd.tensor_copy
            pool.wait_ge(S["in_s5"], 16 * 6)
            TS(cb[:, 2], cb[:, 0], -1.0, None, ALU.mult)
            TS(cb[:, 1], cb[:, 1], -1.0, None, ALU.mult).then_inc(S["s5_cs"], 1)
            pool.wait_ge(S["s5_bb"], 1)
            pool.wait_ge(S["in_setup"], 16 * 7)

            def z_in(k):
                m, z = m5[k % 2], zin[k % 2]
                if k >= 2:
                    pool.wait_ge(S["s5_op"], k - 1)
                    pool.wait_ge(S["s5_sin"], k - 1)
                    pool.wait_ge(S["s5_zl"], k - 1)
                pool.wait_ge(S["s5_rot"], k + 1)
                own(TT(z[:, 0], m[:, 0], m[:, 3], ALU.add))
                own(TT(z[:, 1], m[:, 1], m[:, 2], ALU.subtract))
                own.settle()
                pool.wait_ge(S["s5_rmr"], k + 1)
                first = z[:, :, 256:T].rearrange("p z (b t) -> p z b t", t=ST)[:, :, :, 0]
                TT(first, first, hr5[k % 2], ALU.add).then_inc(S["s5_zin"], 1)

            def sin_z(k):
                pool.wait_ge(S["s5_z"], k + 1)
                if k >= 2:
                    pool.wait_ge(S["s5_ymm"], k - 1)
                TT(o5[k % 2][:, 3], tsin[:, k], zin[k % 2][:, 1], ALU.mult).then_inc(S["s5_sin"], 1)

            for k in range(PAIRS + 1):
                if k < PAIRS:
                    z_in(k)
                if k >= 1:
                    sin_z(k - 1)
            pool.wait_ge(S["s5_zl"], PAIRS)
            pool.wait_ge(S["s5_op"], PAIRS)
            zr, zi = zl[:, 0], zl[:, 1]
            co, si = tcos[:, :, 255:T:4], tsin[:, :, 255:T:4]
            own(TT(st[:, 0], zr, co, ALU.mult))
            own(TT(st[:, 1], zi, co, ALU.mult))
            own(TT(zr, zr, si, ALU.mult))
            own(TT(zi, zi, si, ALU.mult))
            own.settle()
            TT(st[:, 0], st[:, 0], zi, ALU.subtract)
            TT(st[:, 1], st[:, 1], zr, ALU.add).then_inc(S["s5_rm"], 1)


            def low_u(l, j0, j1):
                with pool.Fori(j0 // 4, j1 // 4) as i:
                    for s in range(4):
                        pool.wait_ge(S["hi_ready"], 4 * i + (256 * l + s + 1))
                        TT(ring_lo[:, s], ring[:, s], wt_hi[:, s % 2].bitcast(F32), ALU.subtract)\
                            .then_inc(S["lo_u"], 1)

            def peer_pool(l):
                pool.wait_ge(S["hh_ready"], l + 1)
                TT(h_lo, modsq, h_hi.bitcast(F32), ALU.subtract).then_inc(S["hl_ready"], 1)
                low_u(l, 0, NB0)
                with pool.Fori(0, GROUPS // GPI) as i:
                    for q in range(GPI):
                        pool.wait_ge(S["gb_o2"], GPI * i + (q + 1 + GROUPS * l))
                        o = oh[:, 1, q % 2]
                        TT(o, o, idx[:, 2, bass.ds(4 * GPI * i + 4 * q, 4)].unsqueeze(2).broadcast_to([P, 4, 128]),
                           ALU.mult).then_inc(S["gb_gate"], 1)
                low_u(l, NB0, 128)
                with pool.Fori(0, 32) as i:
                    for s in range(4):
                        pool.wait_ge(S["wh_ready"], 4 * i + (128 * l + s + 1))
                        TT(w_lo[:, s % 2], W[:, bass.ds(4 * i + s, 1), :].rearrange("p a t -> p (a t)"),
                           w_hi[:, s % 2].bitcast(F32), ALU.subtract).then_inc(S["wl_ready"], 1)

            peer_pool(0)
            pool.wait_ge(S["tile_done"], VT[0] + 128)
            own(nc.gpsimd.memset(qz_t, 0.0))
            own.settle()
            pool.wait_ge(S["aq_done"], 6)
            for g in range(NG):
                for q in range(HP):
                    for h2 in range(2):
                        r = slice(64 * h2, 64 * h2 + 64)
                        ins = CP(qz[r, g, :, q, 2 * q + h2, :],
                                 qk[r, 8 * g + q, 256:T].rearrange("p (b t) -> p b t", b=SB))
            ins.then_inc(S["qz_ready"], 1)
            for u in range(2 * H):
                pool.wait_ge(S["us_den"], u + 1)
                p = p_sb[u % 3][:, 0:384 * (u // H + 1)]
                TS(p, p, ust[:, 1, u:u + 1], None, ALU.mult).then_inc(S["us_norm"], 1)
            peer_pool(1)


def kernel(**inp):
    import numpy as np
    import concourse.bacc as bacc
    from concourse import mybir as mb
    from concourse.bass_utils import run_bass_kernel_spmd

    a = {k: np.asarray(v) for k, v in inp.items()}
    f = np.float32
    ca = np.ascontiguousarray

    def cols(w, nt, kc=8):
        return w.reshape(kc, P, nt, P).transpose(2, 1, 0, 3).reshape(nt, P, kc * P)

    def u_tiles(u):
        return u.reshape(128, 128, 8, 128).transpose(1, 3, 2, 0).reshape(128, P, 1024)

    def v_tiles(w):
        return w.reshape(128, 128, 1024).transpose(1, 0, 2)

    glu = cols(a["ssm_w_glu"][0], 16).reshape(2, 8, P, 1024).transpose(1, 0, 2, 3).reshape(16, P, 1024)
    wq = a["attn_w_qkv"][0].reshape(D, 3, 3, 512)
    qkt = cols(ca(wq[:, :, 0:2].reshape(D, 3072)), 24)
    vpt = wq[:, :, 2].reshape(4, 2, P, 3, 512).transpose(3, 0, 2, 1, 4).reshape(12, P, 1024)
    wo = cols(a["attn_w_o"][0], 8, 4).reshape(4, 2, P, 512).transpose(0, 2, 1, 3).reshape(4, P, 1024)
    ada = [w.reshape(8, P, 6, 1024).transpose(2, 0, 1, 3).reshape(48, P, 1024) for w in a["ada_w"]]
    u0 = u_tiles(a["peer_u"][0])
    parts = [ada[0], glu, cols(a["peer_w_q"][0], 8), u0[:NB0], ada[1], u0[NB0:], v_tiles(a["peer_v"][0]), qkt, vpt, wo, cols(a["peer_w_q"][1], 8),
             u_tiles(a["peer_u"][1]), v_tiles(a["peer_v"][1])]
    A = {"stream": np.concatenate(parts)}
    x = np.concatenate([a["x_prompt"][0], a["x_sample"].reshape(32, D)])
    A["xT"] = x.reshape(T, NC, P).transpose(2, 1, 0).reshape(P, NC * T)
    c = np.concatenate([a["c_prompt"], a["c_sample"]])
    A["ccol"] = c.reshape(ROWS, NC, P).transpose(2, 1, 0).reshape(P, -1)
    A["bias"] = a["ada_b"].reshape(L, 48, P).transpose(2, 0, 1).reshape(P, -1)
    gains = np.stack([a["norm_mix"], a["norm_ffn"]], 1)
    A["gain"] = gains.reshape(2 * L, NC, P).transpose(2, 0, 1).reshape(P, -1)
    ones = np.ones((P, P), f)
    blk = np.kron(np.eye(2), np.ones((64, 64))).astype(f)
    rot = np.zeros((P, P), f)
    for h in range(2):
        for i in range(8):
            rot[64 * h + 8 + i, 64 * h + i] = -1.0
            rot[64 * h + i, 64 * h + 8 + i] = 1.0
    iota = np.tile(np.arange(P, dtype=f), (P, 1))
    gm = (np.arange(P)[:, None] // 16 == np.arange(8)[None]).astype(f)
    qkg = np.stack([np.concatenate([a["attn_q_norm"][0]] * 2), np.concatenate([a["attn_k_norm"][0]] * 2)], 1)
    A["consts"] = np.concatenate([ones, blk, np.eye(P, dtype=f), iota, gm, qkg], 1)
    A["rotm"] = rot
    t = np.arange(T)
    sm = np.tile(((t < 256) | ((t - 256) % 4 != 0)).astype(f), (P, 1))
    A["smask"] = sm
    h0 = a["state_ssm"][0].reshape(SB, 2, PAIRS, P).transpose(3, 1, 2, 0).reshape(P, -1)
    A["h0d"] = np.concatenate([h0, a["ssm_d"][0].reshape(NC, P).transpose(1, 0)], 1)

    def both(w):
        one = np.broadcast_to(w.reshape(8, 8, 1, 64), (8, 8, 16, 64)).transpose(1, 2, 0, 3).reshape(P, 512)
        return np.concatenate([one, w.reshape(PAIRS, P).transpose(1, 0)], 1)

    A["lre"], A["lim"] = both(a["ssm_lam_re"][0]), both(a["ssm_lam_im"][0])
    A["ldt"] = both(np.broadcast_to(a["ssm_log_dt"][0][:, None], (64, 64)))
    for n, k in (("sbre", "ssm_b_re"), ("sbim", "ssm_b_im")):
        A[n] = a[k][0].reshape(8, 8, 64, 16).transpose(1, 3, 0, 2).reshape(P, 512)
    cc = []
    for k in ("ssm_c_re", "ssm_c_im"):
        w = a[k][0].reshape(PAIRS, 2, 16, 64).transpose(1, 3, 0, 2)
        z = np.zeros((2, 64, PAIRS, 2, 16), f)
        z[0, :, :, 0], z[1, :, :, 1] = w[0], w[1]
        cc.append(z.reshape(P, 1024))
    A["cri"] = np.concatenate(cc, 1)
    A["subk"] = a["peer_sub_keys"].transpose(0, 2, 4, 1, 3).reshape(L, P, PH * NKEYS)
    A["hqm"] = (np.arange(P)[:, None] // 32 == np.arange(4)[None]).astype(f)
    A["jsel"] = (np.arange(P)[:, None] % 32 == np.arange(32)[None]).astype(f)
    pos = np.concatenate([np.arange(256), PAST + (t[256:] - 256) % 4]).astype(f)
    inv = (f(500000.0) ** (-np.arange(8, dtype=f) / f(8))).astype(f)
    ang = (pos[:, None] * inv[None]).astype(f)
    cs, sn = np.ones((64, T), f), np.zeros((64, T), f)
    cs[0:8] = cs[8:16] = np.cos(ang).T
    sn[0:8] = sn[8:16] = np.sin(ang).T
    A["rope"] = np.concatenate([np.tile(cs, (2, 1)), np.tile(sn, (2, 1))], 1)
    NEG = f(-1e30)
    pm = []
    for qt in range(2):
        q, k = 128 * qt + np.arange(128)[:, None], np.arange(128 * (qt + 1))[None]
        for g in range(NG):
            ok = (k <= q) & ((q - k) % DIL[g] == 0) & ((q - k) // DIL[g] <= WIN[g] // DIL[g])
            pm.append(np.where(ok, f(0), NEG).astype(f))
    A["pmask"] = np.concatenate(pm, 1)
    row = np.arange(P)
    bq, tq = row[:, None] // 32, row[:, None] % 4
    m1 = np.arange(512)[None] % 4 == tq
    m0 = np.arange(128)[None] >= tq
    m2 = np.arange(256)[None] % 4 == tq
    smk = [m1, m0, m2]
    nb, nt = np.arange(32)[None] // 4, np.arange(32)[None] % 4
    for hf in range(2):
        smk += [(nb == bq + 4 * hf) & (nt <= tq)] + [(nb == bq + 4 * hf) & (nt == tq)] * 2
    A["smaskv"] = np.where(np.concatenate(smk, 1), f(0), NEG).astype(f)
    kc, vc = [], []
    for g, name in ((1, "cache_kv_w512"), (0, "cache_kv_w128"), (2, "cache_kv_w2048")):
        cch = a[name][0]
        if g == 2:
            cch = cch.reshape(SB, 2, 64, 16, H, E)[:, :, :, 0:4].reshape(SB, 2, 256, H, E)
        kc.append(cch[:, 0].reshape(SB, -1, HP, P).transpose(0, 3, 2, 1))
        vc.append(cch[:, 1].reshape(SB, -1, P, 512).transpose(0, 2, 1, 3))
    A["kc"] = np.concatenate(kc, 3).reshape(SB, P, HP * CK)
    A["vc"] = np.concatenate(vc, 2).reshape(SB, P, 7 * 512)

    nc = bacc.Bacc("TRN2", target_bir_lowering=False, num_devices=1)
    arrays, I, O = {}, {}, {}
    for n, w in A.items():
        w = ca(w)
        arrays["in_" + n] = w
        I[n] = nc.dram_tensor("in_" + n, w.shape, mb.dt.from_np(w.dtype), kind="ExternalInput").ap()
    for n, shape in (("st", (P, 2 * PAIRS * ROWS)), ("yT", (P, NC * T)), ("qk", (P, 24, T)), ("v", (P, 2, 3, 512)), ("v_s", (32, 3, 512))):
        O[n] = nc.dram_tensor("out_" + n, shape, mb.dt.float32, kind="ExternalOutput").ap()
    build(nc, I, O)
    r = run_bass_kernel_spmd(nc, [arrays], core_ids=[0]).results[0]
    y = r["out_yT"].reshape(P, NC, T).transpose(2, 1, 0).reshape(T, D)
    s = r["out_st"].reshape(P, 2, PAIRS, ROWS).transpose(3, 1, 2, 0).reshape(ROWS, 2, G64, SN)
    k = r["out_qk"].reshape(P, NG, 2, HP, T)[:, :, 1].transpose(1, 3, 2, 0).reshape(NG, T, H, E)
    vv = np.concatenate([r["out_v"].transpose(2, 1, 0, 3).reshape(NG, 256, H, E),
                         r["out_v_s"].transpose(1, 0, 2).reshape(NG, 32, H, E)], 1)
    kvp, kvs = [], []
    for g in range(NG):
        keep = min(WIN[g], 256)
        kvp.append(ca(np.stack([k[g, 256 - keep:256], vv[g, 256 - keep:256]])[None, None]))
        kvs.append(ca(np.stack([k[g, 256:T].reshape(SB, ST, H, E), vv[g, 256:T].reshape(SB, ST, H, E)], 1)[None]))
    return (ca(y[0:256][None]), ca(y[256:].reshape(SB, ST, D)), ca(s[0:1][None]), *kvp, ca(s[1:][None]), *kvs)
```

```python
from contextlib import ExitStack

import concourse.bass as bass
from concourse import mybir

P = 128
D = 1024
NC = D // P
SP_, SB, ST = 256, 8, 4
T = SP_ + SB * ST
ROWS = 1 + SB
L = 2
G64, SN = 64, 64
PAIRS = G64 // 2
H, E = 8, 64
HP = H // 2
NG = 3
WIN, DIL, PAST = (128, 512, 2048), (1, 4, 16), 1024
NK = (128, 512, 256)
KOFF = (512, 0, 640)
CK = sum(NK)
NEWC = CK
SW = CK + NG * 32
PH, NKEYS, TOPK = 8, 128, 16
NCAND = 4 * 16 + 12 * 4
UNITS = 18
EPS = 1e-6
RING = 4

NB0 = 48
ADA, GLU, PQ = (0, 120), 48, (64, 416)
UT, UT2, VT = (72, 424), (120, 424), (248, 552)
QK, VP, WO, TILES = 376, 400, 412, 680
HI, LO = (16, 40 + 256), (16, 40 + 128)
GROUPS, GPI = T // 4, 12

F32 = mybir.dt.float32
F32R = mybir.dt.float32r
BF16 = mybir.dt.bfloat16
U32 = mybir.dt.uint32
ALU = mybir.AluOpType
ACT = mybir.ActivationFunctionType
X = mybir.AxisListType.X
BU_BANK = (0, 2, 6)
TWO_PI = 6.283185307179586
C1 = 6.28125
C2 = 0.0019350051879882812
C3 = 3.019916050e-07
MAGIC = 12582912.0
PI_LO = 3.1415925


class Count:

    def __init__(self, eng, sem):
        self.eng, self.sem, self.n = eng, sem, 0

    def __call__(self, ins):
        self.n += 1
        ins.then_inc(self.sem, 1)

    def settle(self):
        self.eng.wait_ge(self.sem, self.n)


def build(nc, I, O):
    ctx = ExitStack()
    with ctx:
        def sb(name, words, dt=F32):
            return ctx.enter_context(nc.sbuf_tensor(name, [P, words], dt))

        def sem(name):
            return ctx.enter_context(nc.semaphore(name))

        big = sb("big", 128 * T)
        with nc.sbuf_tensor("ring", [P, RING, 1024], F32) as ring:
            pass
        ring_lo = ctx.enter_context(nc.sbuf_tensor("ring_lo", [P, RING, 1024], F32R))
        with nc.sbuf_tensor("oh", [P, 4 * 512], F32) as oh_t:
            pass
        wt_hi = ctx.enter_context(nc.sbuf_tensor("wt_hi", [P, 2, 1024], F32R))
        with nc.sbuf_tensor("scratch", [P, 2 * NC * T], F32) as scratch:
            pass
        split_t = ctx.enter_context(nc.sbuf_tensor("split", [P, 2 * NC * T], F32R))
        y_lo, y_hi = (split_t[:, z * NC * T:(z + 1) * NC * T].rearrange("p (c t) -> p c t", c=NC) for z in range(2))
        h_hi, h_lo = (split_t[:, z * NC * T:(z + 1) * NC * T].rearrange("p (c t) -> p c t", c=NC) for z in range(2))
        w_hi, w_lo = (split_t[:, 2 * z * T:2 * (z + 1) * T].rearrange("p (b t) -> p b t", b=2) for z in range(2))
        xT_t = sb("xT", NC * T)
        xT = xT_t[:, :].rearrange("p (c t) -> p c t", c=NC)
        hT = scratch[:, 0:NC * T].rearrange("p (c t) -> p c t", c=NC)
        ada_t = sb("ada", L * 48 * ROWS)
        ada = ada_t[:, :].rearrange("p (l j c r) -> p l j c r", l=L, j=6, c=NC)
        consts = sb("consts", 4 * 128 + 10)
        ones = consts[:, 0:128]
        blk64 = consts[:, 128:256]
        ident = consts[:, 256:384]
        iota = consts[:, 384:512]
        gmask = consts[:, 512:520]
        qg, kg = consts[:, 520:521], consts[:, 521:522]
        ccol = sb("ccol", NC * ROWS)
        bias_t = sb("bias", L * 48)
        gain_t = sb("gain", 2 * L * NC)
        eps_c = sb("eps_c", 1)
        idx_t = sb("idx", 3 * T)
        idx = idx_t[:, :].rearrange("p (q t) -> p q t", q=3)
        gtmp = sb("gtmp", 2 * T)
        rstd = gtmp[:, T:2 * T]
        oh = oh_t[:, :].rearrange("p (w b t k) -> p w b t k", w=2, b=2, t=4)
        small = sb("small", 96)
        r_col = small[:, 0:PAIRS]
        st_t = idx_t[:, 0:2 * PAIRS * ROWS]
        st = st_t.rearrange("p (z k r) -> p z k r", z=2, k=PAIRS)
        ps = ctx.enter_context(nc.psum_tensor("ps", [P, 8, 512], F32))

        class Region:

            def __init__(self, at=0):
                self.at = at

            def take(self, words):
                a = big[:, self.at:self.at + words]
                self.at += words
                assert self.at <= 128 * T, self.at
                return a

        W = big[:, :].rearrange("p (j t) -> p j t", j=128)
        rg = Region(NB0 * T)
        s_sb = rg.take(UNITS * 256)
        cand = rg.take(UNITS * 256)
        eq = rg.take(UNITS * 256)
        s_two = eq
        qraw_t = cand
        qraw = qraw_t[:, 0:NC * T].rearrange("p (c t) -> p c t", c=NC)
        qsq_t = eq
        qsq = qsq_t[:, 0:NC * T].rearrange("p (c t) -> p c t", c=NC)
        qrs = eq[:, NC * T:2 * NC * T].rearrange("p (c t) -> p c t", c=NC)
        v16 = rg.take(2 * UNITS * 16).rearrange("p (u z a) -> p u z a", u=UNITS, z=2)
        i16_f = rg.take(2 * UNITS * 16).bitcast(BF16)
        i16 = i16_f[:, 0:2 * UNITS * 16].rearrange("p (u z a) -> p u z a", u=UNITS, z=2)
        iota16 = i16_f[:, 2 * UNITS * 16:2 * UNITS * 16 + 16]
        i16u_f = rg.take(2 * UNITS * 16)
        i16u = i16u_f.bitcast(U32).rearrange("p (u z a) -> p u z a", u=UNITS, z=2)
        best = rg.take(UNITS * 16).rearrange("p (u k) -> p u k", u=UNITS)
        selu = rg.take(UNITS * 16).bitcast(U32).rearrange("p (u k) -> p u k", u=UNITS)
        KU = UNITS * 16
        e_bf = eq[:, 0:UNITS * 128].bitcast(BF16)
        selabu = eq[:, UNITS * 128:UNITS * 128 + 5 * KU].bitcast(U32).rearrange("p (z n) -> p z n", z=5)
        selab5 = rg.take(2 * KU + KU // 2).bitcast(BF16).rearrange("p (z n) -> p z n", z=5)
        sel3 = rg.take(3 * UNITS * 16).rearrange("p (q u k) -> p q u k", q=3, u=UNITS)
        selz = rg.take(3 * 128).rearrange("p (q s) -> p q s", q=3)
        gsum = rg.take(2 * UNITS)
        hqm = rg.take(4)
        jsel = rg.take(32)
        subk_t = rg.take(PH * NKEYS)
        subk = subk_t.rearrange("p (h k) -> p h k", h=PH)
        modsq = big[:, 128 * T - NC * T:128 * T].rearrange("p (c t) -> p c t", c=NC)

        rs = Region()
        tcos = rs.take(PAIRS * T).rearrange("p (k t) -> p k t", k=PAIRS)
        tsin = rs.take(PAIRS * T).rearrange("p (k t) -> p k t", k=PAIRS)
        bb_re = rs.take(4096).rearrange("p (c g n) -> p c g n", c=NC, g=8)
        bb_im_f = rs.take(4096)
        bb_im = bb_im_f.rearrange("p (c g n) -> p c g n", c=NC, g=8)
        cb = rs.take(3 * 1024).rearrange("p (z k m) -> p z k m", z=3, k=PAIRS)
        ring5 = rs.at
        LW = 512 + PAIRS
        lre, lim, ldt = rs.take(LW), rs.take(LW), rs.take(LW)
        sth, sq1, ssin, scos, sr, st1 = (rs.take(LW) for _ in range(6))
        sbre, sbim = rs.take(512), rs.take(512)
        assert rs.at <= 128 * T
        r5 = Region(ring5)
        m5 = [r5.take(4 * T).rearrange("p (q t) -> p q t", q=4) for _ in range(2)]
        zin = [r5.take(2 * T).rearrange("p (q t) -> p q t", q=2) for _ in range(2)]
        z5 = zin
        o5 = [r5.take(4 * T).rearrange("p (q t) -> p q t", q=4) for _ in range(2)]
        rm5 = [r5.take(T) for _ in range(2)]
        zl = gtmp[:, 0:2 * PAIRS * ROWS].rearrange("p (z k r) -> p z k r", z=2, k=PAIRS)

        smask = r5.take(T)
        h0d = r5.take(520)
        h0 = h0d[:, 0:512].rearrange("p (z k b) -> p z k b", z=2, k=PAIRS)
        dskip = h0d[:, 512:520]
        hr5 = [small[:, 32 + 16 * n:48 + 16 * n].rearrange("p (z b) -> p z b", z=2) for n in range(2)]

        ra = Region()
        qk = ra.take(24 * T).rearrange("p (m t) -> p m t", m=24)
        v_sb = ra.take(9 * 512).rearrange("p (a g n) -> p a g n", a=3, g=NG)
        rotm = ra.take(128)
        spread = ra.take(512)
        rope = ra.take(2 * T).rearrange("p (z t) -> p z t", z=2)
        pmask = ra.take(384 + 768)
        smaskv = ra.take(SW + 96)
        qz_t = ra.take(NG * SB * HP * 32)
        qz = qz_t.rearrange("p (g b q h t) -> p g b q h t", g=NG, b=SB, q=HP, h=H)
        oT = ra.take(HP * T).rearrange("p (q t) -> p q t", q=HP)
        sst = ra.take(4)
        ust = ra.take(48).rearrange("p (z u) -> p z u", z=3)
        tmp0 = ra.at
        asq = ra.take(4 * T).rearrange("p (m t) -> p m t", m=4)
        ars = ra.take(T)
        rb = Region(tmp0)
        p_sb = [scratch[:, NC * T + 768 * n:NC * T + 768 * (n + 1)] for n in range(3)]
        pt_sb = [rb.take(768) for _ in range(2)]
        ps_s = rb.take(SW)
        pts = rb.take(7 * 128).rearrange("p (k r) -> p k r", k=7)
        ptn = rb.take(3 * 128).rearrange("p (g r) -> p g r", g=3)
        kv_buf = [rb.take(4 * CK) for _ in range(3)]
        assert rb.at <= 128 * T - NC * T

        S = {n: sem(n) for n in (
            "tile_done in_setup in_s5 in_att in_kv0 in_kv1 in_kv2 kv_used v_own a_own p_own silu_c "
            "ada_row ada_turned ada_done us_norm sq_ready ms_ready std_ready h_ready s5_trig s5_thr s5_bb s5_tab s5_bu s5_rot s5_rm s5_zin s5_z "
            "s5_op s5_cs s5_ymm s5_hy glu_sig glu_used st_ready x_ready q_copied qsq_ready qms_ready qsd_ready "
            "qn_ready sc_mm sc_copied gate_in gate_exp sel_ready sel_t idx_ready gb_o1 gb_o2 gb_gate gb_mm gb_mul gb_cp "
            "gelu_done w_done aq_copied aq_sq aq_ms aq_sd aq_qn aq_rot aq_done v_copied qz_ready "
            "us_mm us_max us_exp us_t us_cpa us_cpv us_pv us_o ss_mm ss_max ss_exp ss_t ss_cp "
            "ss_norm ss_pv oT_ready out_done st_out kv_out glu_used_v "
            "aq_rc aq_sp hq_ready hq_lo hq_lo_v yh_ready yl_ready s5_bbi ss_oc ss_ot s5_rmr s5_sin s5_zl hi_ready lo_u lo_v hh_ready hl_ready wh_ready wl_ready").split()}
        tile_in = [sem(f"tile_in{s}") for s in range(RING)]

        def tile_wait(eng, n, i=0):
            eng.wait_ge(tile_in[n % RING], 16 * i + 16 * (n // RING + 1))

        block = ctx.enter_context(nc.Block())

        @block.sync
        def _(sp):
            stream = I["stream"]
            for s in range(RING):
                sp.dma_start(ring[:, s, :], stream[s]).then_inc(tile_in[s], 16)
            with sp.Fori(1, TILES // RING) as i:
                for s in range(RING):
                    sp.wait_ge(S["tile_done"], RING * i + (s + 1 - RING))
                    sp.dma_start(ring[:, s, :], stream[bass.ds(RING * i + s, 1)].rearrange("a p n -> (a p) n"))\
                      .then_inc(tile_in[s], 16)
            sp.wait_ge(S["x_ready"], 3)
            sp.dma_start(O["yT"], xT_t[:, :]).then_inc(S["out_done"], 16)
            sp.wait_ge(S["out_done"], 16)
            sp.wait_ge(S["st_out"], 16)
            sp.wait_ge(S["kv_out"], 48)

        def ada_row(act, l, nb, half, bank=4):
            act.wait_ge(S["tile_done"], 8 * nb + (ADA[l] + 8))
            if l or nb or half:
                act.wait_ge(S["ada_turned"], 2 * nb + (12 * l + half))
            nc.scalar.activation(gtmp[0:ROWS, 0:512], ps[0:ROWS, bank + half, :], ACT.Copy).then_inc(S["ada_row"], 1)

        def high(act, n, i=0):
            tile_wait(act, n, i)
            nc.scalar.activation(wt_hi[:, n % 2], ring[:, n % RING], ACT.Copy).then_inc(S["hi_ready"], 1)

        def peer_act(act, l):
            act.dma_start(subk_t, I["subk"][l]).then_inc(S["gate_in"], 16)
            act.dma_start(hqm, I["hqm"]).then_inc(S["gate_in"], 16)
            act.dma_start(jsel, I["jsel"]).then_inc(S["gate_in"], 16)
            act.wait_ge(S["h_ready"], 4 * l + 4)
            nc.scalar.activation(h_hi, modsq, ACT.Copy).then_inc(S["hh_ready"], 1)

            for m in range(8):
                act.wait_ge(S["tile_done"], PQ[l] + m + 1)
                nc.scalar.activation(qraw[:, m, :], ps[:, m % 4, 0:T], ACT.Copy).then_inc(S["q_copied"], 1)
                if m in (5, 6):
                    high(act, UT[l] + m - 5)

            def gelu_block(i, s, ahead=True):
                act.wait_ge(S["tile_done"], 4 * i + (UT[l] + s + 1))
                if ahead:
                    high(act, UT[l] + s + 2, i)
                dst = W[:, bass.ds(4 * i + s, 1), :].rearrange("p a t -> p (a t)")
                nc.scalar.activation(dst, ps[:, 6 + s % 2, 0:T], ACT.Gelu).then_inc(S["gelu_done"], 1)

            def gelus(j0, j1):
                with act.Fori(j0 // 4, j1 // 4) as i:
                    for s in range(4):
                        gelu_block(i, s)

            def q_root(n):
                act.wait_ge(S["qms_ready"], 2 * l + n + 1)
                nc.scalar.activation(qrs[:, 4 * n:4 * n + 4, :], ps[:, 0:4, 0:T], ACT.Sqrt, bias=eps_c[:, :],
                                     scale=1.0 / 64).then_inc(S["qsd_ready"], 1)

            def scores_out(n):
                act.wait_ge(S["sc_mm"], 3 * l + n + 1)
                u0, u1 = ((0, 8), (16, 18), (8, 16))[n]
                dst = s_sb.rearrange("p (u z k) -> p z u k", u=UNITS, z=2)[:, :, u0:u1, :]
                if n == 1:
                    src = ps[:, 4:6, 0:256].rearrange("p z (u k) -> p z u k", u=2)
                else:
                    src = ps[:, 0:4, :].rearrange("p (z a) (b k) -> p z (a b) k", z=2, b=4)
                nc.scalar.activation(dst, src, ACT.Copy).then_inc(S["sc_copied"], 1)

            gelus(0, 4)
            q_root(0)
            gelus(4, 8)
            q_root(1)
            gelus(8, 12)
            scores_out(0)
            scores_out(1)
            gelus(12, 16)
            scores_out(2)
            gelus(16, NB0 - 8)
            act.wait_ge(S["gate_exp"], 2 * l + 1)
            nc.scalar.activation(best, best, ACT.Exp).then_inc(S["gate_exp"], 1)
            gelus(NB0 - 8, NB0 - 4)
            for s in range(2):
                gelu_block(NB0 // 4 - 1, s)
            for n in range(2):
                act.wait_ge(S["sel_t"], 3 * l + n + 1)
                nc.scalar.activation(idx[:, :, n * 128:(n + 1) * 128],
                                     ps[:, n, 0:384].rearrange("p (q t) -> p q t", q=3), ACT.Copy)\
                   .then_inc(S["idx_ready"], 1)
            act.wait_ge(S["sel_t"], 3 * l + 3)
            nc.scalar.activation(idx[:, :, 256:T], ps[:, 2, 0:96].rearrange("p (q t) -> p q t", q=3), ACT.Copy)\
               .then_inc(S["idx_ready"], 1)
            for s in range(2, 4):
                gelu_block(NB0 // 4 - 1, s, False)
            def gate_high(i, q):
                act.wait_ge(S["gb_mul"], GPI * i + (q + 1 + GROUPS * l))
                t0 = 4 * GPI * i + 4 * q
                nc.scalar.activation(W[:, NB0:128, bass.ds(t0, 4)],
                                     ps[:, q % 4, :].rearrange("p (t j) -> p j t", t=4)[:, NB0:128, :], ACT.Copy)\
                    .then_inc(S["gb_cp"], 1)

            def gate_pass(i):
                for q in range(GPI):
                    gate_high(i, q)
                    if l == 0 and q in (8, 10):
                        ada_row(act, 1, i, (q - 8) // 2)

            with act.Fori(0, GROUPS // GPI) as i:
                gate_pass(i)
            high(act, UT2[l] + NB0)
            high(act, UT2[l] + NB0 + 1)
            for s in range(4):
                act.wait_ge(S["tile_done"], UT2[l] + NB0 + s + 1)
                high(act, UT2[l] + NB0 + s + 2)
                if s >= 2:
                    act.wait_ge(S["w_done"], (128 - NB0) * l + s - 1)
                nc.scalar.activation(gtmp[:, (s % 2) * T:(s % 2 + 1) * T], ps[:, 6 + s % 2, 0:T], ACT.Gelu)\
                   .then_inc(S["gelu_done"], 1)
            with act.Fori(NB0 // 4 + 1, 32) as i:
                for s in range(4):
                    act.wait_ge(S["tile_done"], 4 * i + (UT2[l] + s + 1))
                    high(act, UT2[l] + s + 2, i)
                    act.wait_ge(S["w_done"], 4 * i + (s - 1 - NB0 + (128 - NB0) * l))
                    nc.scalar.activation(gtmp[:, (s % 2) * T:(s % 2 + 1) * T], ps[:, 6 + s % 2, 0:T], ACT.Gelu)\
                       .then_inc(S["gelu_done"], 1)

            def w_high(j, b):
                nc.scalar.activation(w_hi[:, b], W[:, bass.ds(j, 1), :].rearrange("p a t -> p (a t)"), ACT.Copy)\
                   .then_inc(S["wh_ready"], 1)

            act.wait_ge(S["w_done"], (128 - NB0) * (l + 1))
            for b in range(2):
                nc.scalar.activation(w_hi[:, b], W[:, b], ACT.Copy).then_inc(S["wh_ready"], 1)

            def down_high(i, s):
                act.wait_ge(S["tile_done"], 4 * i + (VT[l] + s + 1))
                w_high(4 * i + (s + 2), s % 2)
                high(act, VT[l] + s + 2, i)

            with act.Fori(0, 31) as i:
                for s in range(4):
                    down_high(i, s)
            for s in range(2):
                down_high(31, s)

        def attention_act(act, own):
            act.wait_ge(S["tile_done"], VT[0] + 128)
            for dst, name in [(rope.rearrange("p z t -> p (z t)"), "rope"), (pmask, "pmask"), (smaskv, "smaskv"), (rotm, "rotm"), (spread, "spread")]:
                act.dma_start(dst, I[name]).then_inc(S["in_att"], 16)

            def load_kv(n):
                half, v, b = n // 8, n % 8 // 4, n // 8 * 4 + n % 4
                if n >= 3:
                    act.wait_ge(S["kv_used"], n - 2)
                act.dma_start(kv_buf[n % 3], I["vc" if v else "kc"][b]).then_inc(S[f"in_kv{n % 3}"], 16)

            for n in range(3):
                load_kv(n)

            for n in range(2):
                act.wait_ge(S["h_ready"], 5 + n)
                m = slice(4 * n, 4 * n + 4)
                nc.scalar.activation(h_hi[:, m], modsq[:, m], ACT.Copy).then_inc(S["hq_ready"], 1)
                high(act, QK + n)

            def qk_root(gs):
                act.wait_ge(S["aq_ms"], gs + 1)
                nc.scalar.activation(ars, ps[:, 4, 0:T], ACT.Sqrt, bias=eps_c[:, :], scale=1.0 / E)\
                   .then_inc(S["aq_sd"], 1)

            for gs in range(6):
                for m in range(4):
                    act.wait_ge(S["tile_done"], QK + 4 * gs + m + 1)
                    if gs < 5 or m < 2:
                        high(act, QK + 4 * gs + m + 2)
                    if gs and m == 0:
                        qk_root(gs - 1)
                nc.scalar.activation(qk[:, 4 * gs:4 * gs + 4, :], ps[:, 0:4, 0:T], ACT.Copy)\
                   .then_inc(S["aq_copied"], 1)
            qk_root(5)
            for g in range(NG):
                act.wait_ge(S["tile_done"], VP + 4 * g + 4)
                nc.scalar.activation(v_sb[:, 0:2, g, :], ps[:, 0:2, :], ACT.Copy)
                nc.scalar.activation(v_sb[0:32, 2, g, :], ps[0:32, 2, :], ACT.Copy).then_inc(S["v_copied"], 1)
                if g < 2:
                    for n in (3 + 2 * g, 4 + 2 * g):
                        load_kv(n)
            act.wait_ge(S["aq_done"], 6)
            act.wait_ge(S["v_copied"], NG)
            act.dma_start(O["qk"], qk).then_inc(S["kv_out"], 16)
            act.dma_start(O["v"], v_sb[:, 0:2]).then_inc(S["kv_out"], 16)
            act.dma_start(O["v_s"], v_sb[0:32, 2]).then_inc(S["kv_out"], 16)
            nkv = [7]

            def more(n):
                while nkv[0] < n:
                    load_kv(nkv[0])
                    nkv[0] += 1

            def sample_exp(hf):
                act.wait_ge(S["ss_max"], hf + 1)
                nc.scalar.activation(ps_s, ps_s, ACT.Exp, bias=sst[:, 0:1], accum_out=sst[:, 1:2])\
                   .then_inc(S["ss_exp"], 1)

            def sample_t(hf):
                act.wait_ge(S["ss_t"], hf + 1)
                nc.scalar.activation(pts, ps[:, 2:4, :].rearrange("p b n -> p (b n)")[:, 0:CK]
                                     .rearrange("p (k r) -> p k r", k=7), ACT.Copy)
                nc.scalar.activation(ptn[0:32], ps[0:32, 7, 0:384].rearrange("p (g r) -> p g r", g=3), ACT.Copy)\
                   .then_inc(S["ss_cp"], 1)

            def unit_exp(u):
                w = 384 * (u // H + 1)
                p = p_sb[u % 3][:, 0:w]
                act.wait_ge(S["us_max"], u + 1)
                nc.scalar.activation(p, p, ACT.Exp, bias=ust[:, 0, u:u + 1], accum_out=ust[:, 1, u:u + 1])\
                   .then_inc(S["us_exp"], 1)

            def unit_t(u):
                w = 384 * (u // H + 1)
                act.wait_ge(S["us_t"], u + 1)
                if u >= 2:
                    act.wait_ge(S["us_pv"], u - 1)
                nc.scalar.activation(pt_sb[u % 2][:, 0:w], ps[:, 2:4, :].rearrange("p b n -> p (b n)")[:, 0:w],
                                     ACT.Copy).then_inc(S["us_cpa"], 1)

            for hf in range(2):
                more(8 * hf + 7)
                sample_exp(hf)
                unit_exp(8 * hf)
                sample_t(hf)
                for u in range(8 * hf, 8 * hf + 8):
                    if u % 8 < 7:
                        unit_exp(u + 1)
                    unit_t(u)
                    if u % 2 == 0 and u > 8 * hf:
                        more(min(8 * hf + 7 + (u - 8 * hf) // 2, 16))
                more(min(8 * hf + 11, 16))

        @block.scalar
        def _(act):
            own = Count(act, S["a_own"])
            setup = [(ccol[:, :], "ccol"), (consts[:, :], "consts"), (gain_t[:, :], "gain"),
                     (bias_t[:, :], "bias"), (xT_t[:, :], "xT"), (smask, "smask"),
                     (h0d, "h0d")]
            for dst, name in setup:
                act.dma_start(dst, I[name]).then_inc(S["in_setup"], 16)
            for dst, name in [(lre, "lre"), (lim, "lim"), (ldt, "ldt"), (sbre, "sbre"), (sbim, "sbim")]:
                act.dma_start(dst, I[name]).then_inc(S["in_s5"], 16)
            act.dma_start(cb[:, 0:2], I["cri"].rearrange("p (z k m) -> p z k m", z=2, k=PAIRS))\
               .then_inc(S["in_s5"], 16)
            act.wait_ge(S["in_setup"], 16 * 7)
            nc.scalar.activation(ccol[:, :], ccol[:, :], ACT.Silu).then_inc(S["silu_c"], 1)
            act.wait_ge(S["in_s5"], 16 * 6)
            nc.scalar.activation(ldt, ldt, ACT.Exp).then_inc(S["s5_trig"], 1)
            act.wait_ge(S["s5_thr"], 1)
            nc.scalar.activation(ssin, sth, ACT.Sin)
            nc.scalar.activation(scos, sth, ACT.Sin, scale=0.5).then_inc(S["s5_trig"], 1)
            act.wait_ge(S["s5_thr"], 2)
            nc.scalar.activation(sr, sr, ACT.Exp).then_inc(S["s5_trig"], 1)
            for n in range(12):
                ada_row(act, 0, n // 2, n % 2, 2 + 2 * (n // 2 % 2))
            def root_mean(q, bank=7):
                if q == 0:
                    act.wait_ge(S["ada_turned"], 12)
                act.wait_ge(S["ms_ready"], q + 1)
                nc.scalar.activation(rstd, ps[:, bank, 0:T], ACT.Sqrt, bias=eps_c[:, :], scale=1.0 / D)\
                   .then_inc(S["std_ready"], 1)

            root_mean(0)
            act.wait_ge(S["s5_tab"], 1)
            for gl in range(8):
                ins = nc.scalar.activation(bb_re[:, :, gl, :], sbre.rearrange("p (c n) -> p c n", c=NC),
                                           ACT.Copy, scale=gmask[:, gl:gl + 1])
            ins.then_inc(S["s5_bb"], 1)

            act.wait_ge(S["s5_bb"], 1)
            act.wait_ge(S["s5_bbi"], 1)
            high(act, GLU)
            high(act, GLU + 1)

            def y_high(c):
                act.wait_ge(S["s5_hy"], c + 1)
                nc.scalar.activation(y_hi[:, c], hT[:, c], ACT.Copy).then_inc(S["yh_ready"], 1)

            for k in range(PAIRS):
                if k >= 9 and k % 4 == 1:
                    y_high(k // 4 - 2)
                if k >= 2:
                    act.wait_ge(S["s5_z"], k - 1)
                    nc.scalar.activation(zl[:, :, k - 2], zin[k % 2][:, :, 255:T:4], ACT.Copy).then_inc(S["s5_zl"], 1)
                nc.scalar.activation(rm5[k % 2], smask, ACT.Copy, scale=r_col[:, k:k + 1])
                nc.scalar.activation(hr5[k % 2], h0[:, :, k, :], ACT.Copy, scale=r_col[:, k:k + 1])\
                    .then_inc(S["s5_rmr"], 1)
            for k in (PAIRS - 2, PAIRS - 1):
                act.wait_ge(S["s5_z"], k + 1)
                nc.scalar.activation(zl[:, :, k], zin[k % 2][:, :, 255:T:4], ACT.Copy).then_inc(S["s5_zl"], 1)
            y_high(NC - 2)
            y_high(NC - 1)
            act.wait_ge(S["s5_rm"], 1)
            act.dma_start(O["st"], st_t).then_inc(S["st_out"], 16)
            def sigmoids(i, first, last=False):
                for m in range(2):
                    for z in range(2):
                        act.wait_ge(S["tile_done"], 4 * i + (GLU + 2 * m + z + 1))
                        if not last or m == 0:
                            high(act, GLU + 2 * m + z + 2, i)
                    if not first:
                        act.wait_ge(S["glu_used"], 2 * i + (m - 1))
                    nc.scalar.activation(gtmp[:, m * T:(m + 1) * T], ps[:, 2 * m + 1, 0:T], ACT.Sigmoid)\
                       .then_inc(S["glu_sig"], 1)

            sigmoids(0, True)
            with act.Fori(1, 3) as i:
                sigmoids(i, False)
            sigmoids(3, False, True)
            root_mean(1)
            act.wait_ge(S["st_out"], 16)
            peer_act(act, 0)
            root_mean(2)
            attention_act(act, own)
            root_mean(3)
            act.wait_ge(S["kv_out"], 48)
            peer_act(act, 1)

        def attention_pe(pe, wide):
            mm = nc.tensor.matmul

            def qk_tile(n, out):
                s = n % RING
                pe.wait_ge(S["hi_ready"], HI[0] + 256 + n + 1)
                for c in range(NC):
                    if n == 0 and c % 4 == 0:
                        pe.wait_ge(S["hq_ready"], 1 + c // 4)
                    mm(out, wt_hi[:, s % 2, c * 128:(c + 1) * 128], h_hi[:, c], start=(c == 0), stop=False)
                for c in range(NC):
                    if n == 0 and c % 4 == 0:
                        pe.wait_ge(S[("hq_lo", "hq_lo_v")[c // 4]], 1)
                    mm(out, wt_hi[:, s % 2, c * 128:(c + 1) * 128], h_lo[:, c], start=False, stop=False)
                pe.wait_ge(S["lo_u"], LO[0] + 128 + n + 1)
                for c in range(NC):
                    ins = mm(out, ring_lo[:, s, c * 128:(c + 1) * 128], h_hi[:, c], start=False, stop=(c == NC - 1))
                ins.then_inc(S["tile_done"], 1)

            def norm(gs):
                pe.wait_ge(S["aq_sq"], gs + 1)
                if gs:
                    pe.wait_ge(S["aq_done"], gs)
                for m in range(4):
                    ins = mm(ps[32 * m:32 * m + 32, 4, 0:T], blk64[:, 48:80], asq[:, m, :], start=True, stop=True)
                ins.then_inc(S["aq_ms"], 1)

            def spread_out(gs):
                pe.wait_ge(S["aq_rc"], gs + 1)
                for m in range(4):
                    ins = mm(ps[:, 4 + m, 0:T], spread[:, 128 * m:128 * m + 128], ars, start=True, stop=True)
                ins.then_inc(S["aq_sp"], 1)

            def rotate(gs):
                pe.wait_ge(S["aq_qn"], gs + 1)
                for m in range(4):
                    ins = mm(ps[:, 4 + m, 0:T], rotm, qk[:, 4 * gs + m, :], start=True, stop=True)
                ins.then_inc(S["aq_rot"], 1)

            for gs in range(6):
                if gs:
                    pe.wait_ge(S["aq_copied"], gs)
                for m in range(4):
                    qk_tile(4 * gs + m, ps[:, m, 0:T])
                    if gs and m == 0:
                        norm(gs - 1)
                    if gs and m == 1:
                        spread_out(gs - 1)
                    if gs and m == 2:
                        rotate(gs - 1)
            def kv(n):
                pe.wait_ge(S[f"in_kv{n % 3}"], 16 * (n // 3 + 1))
                return kv_buf[n % 3]

            def sample_scores(hf, b0=0, b1=4):
                if hf:
                    pe.wait_ge(S["us_max"], H)
                for bb in range(b0, b1):
                    b = 4 * hf + bb
                    kb = kv(8 * hf + bb).rearrange("p (q k) -> p q k", q=HP)
                    rows = slice(32 * bb, 32 * bb + 32)
                    for g in range(NG):
                        bank, c0 = (5, 0) if g == 1 else (6, KOFF[g] - 512)
                        for q in range(HP):
                            ins = mm(ps[rows, bank, c0:c0 + NK[g]], qz[:, g, b, q, :, :].rearrange("p h t -> p (h t)"),
                                     kb[:, q, KOFF[g]:KOFF[g] + NK[g]], start=(q == 0), stop=(q == HP - 1))
                    ins.then_inc(S["kv_used"], 1)
                    for g in range(NG):
                        c0 = NEWC - 512 + 32 * g
                        for q in range(HP):
                            ins = mm(ps[rows, 6, c0:c0 + 32], qz[:, g, b, q, :, :].rearrange("p h t -> p (h t)"),
                                     qk[:, 8 * g + 4 + q, 256:T], start=(q == 0), stop=(q == HP - 1))
                if b1 == 4:
                    ins.then_inc(S["ss_mm"], 1)

            pe.wait_ge(S["aq_copied"], 6)
            for g in range(NG):
                if g:
                    pe.wait_ge(S["v_copied"], g)
                for s in range(4):
                    tile_wait(pe, VP + 4 * g + s)
                    for z in range(2):
                        c = 2 * s + z
                        for a, n in ((0, 128), (1, 128), (2, 32)):
                            ins = mm(ps[0:n, a, :], modsq[:, c, 128 * a:128 * a + n], ring[:, s, z * 512:(z + 1) * 512],
                                     start=(c == 0), stop=(c == NC - 1))
                    ins.then_inc(S["tile_done"], 1)
                    if g == 0 and s == 0:
                        norm(5)
                    if g == 0 and s == 1:
                        spread_out(5)
                    if g == 0 and s == 2:
                        rotate(5)
                    if g == 1 and s == 0:
                        pe.wait_ge(S["aq_done"], 6)
                        pe.wait_ge(S["qz_ready"], 1)
                        sample_scores(0, 0, 2)
                if g == 1:
                    sample_scores(0, 2, 4)
            pe.wait_ge(S["v_copied"], NG)

            def sample_turn(hf):
                pe.wait_ge(S["ss_norm"], hf + 1)
                if hf:
                    pe.wait_ge(S["oT_ready"], hf)
                for k in range(7):
                    nc.tensor.transpose(ps[:, 2 + k // 4, (k % 4) * 128:(k % 4 + 1) * 128],
                                        ps_s[:, 128 * k:128 * k + 128], ident)
                for g in range(NG):
                    ins = nc.tensor.transpose(ps[0:32, 7, g * 128:(g + 1) * 128],
                                              ps_s[:, NEWC + 32 * g:NEWC + 32 * g + 32], ident)
                ins.then_inc(S["ss_t"], 1)

            def sample_pv(hf, bb):
                vb = kv(8 * hf + 4 + bb).rearrange("p (k n) -> p k n", k=7)
                r = slice(32 * bb, 32 * bb + 32)
                for k in range(7):
                    ins = mm(ps[r, 7, :], pts[:, k, r], vb[:, k, :], start=(k == 0), stop=False)
                ins.then_inc(S["kv_used"], 1)
                for g in range(NG):
                    ins = mm(ps[r, 7, :], ptn[0:32, g, r], v_sb[0:32, 2, g, :], start=False, stop=(g == NG - 1))
                if bb == 3:
                    ins.then_inc(S["ss_pv"], 1)

            def sample_fold(hf):
                pe.wait_ge(S["ss_oc"], hf + 1)
                for q in range(HP):
                    ins = nc.tensor.transpose(ps[:, 2, 128 * q:128 * q + 128], ps_s[:, 128 * q:128 * q + 128], ident)
                ins.then_inc(S["ss_ot"], 1)

            def unit_scores(u):
                qt, h = u // H, u % H
                r = slice(64 * (h % 2), 64 * (h % 2) + 64)
                if u >= 2:
                    pe.wait_ge(S["us_max"], u - 1)
                if h == 1:
                    pe.wait_ge(S["ss_max"], qt + 1)
                w, b0 = 128 * (qt + 1), 5 * (u % 2)
                for g in range(NG):
                    bank, c0 = (b0, g * w) if g * w < 512 else (b0 + 1, 0)
                    ins = mm(ps[:, bank, c0:c0 + w], qk[r, 8 * g + h // 2, 128 * qt:128 * qt + 128],
                             qk[r, 8 * g + 4 + h // 2, 0:w], start=True, stop=True)
                ins.then_inc(S["us_mm"], 1)

            def unit_turn(u):
                pe.wait_ge(S["us_norm"], u + 1)
                if u:
                    pe.wait_ge(S["us_cpa"], u)
                if u % H == 0:
                    pe.wait_ge(S["ss_cp"], u // H + 1)
                for k in range(NG * (u // H + 1)):
                    ins = nc.tensor.transpose(ps[:, 2 + k // 4, (k % 4) * 128:(k % 4 + 1) * 128],
                                              p_sb[u % 3][:, 128 * k:128 * k + 128], ident)
                ins.then_inc(S["us_t"], 1)

            def unit_pv(u):
                qt, h = u // H, u % H
                pe.wait_ge(S["us_cpa"], u + 1)
                if u:
                    pe.wait_ge(S["us_o"], u)
                r = slice(64 * (h % 2), 64 * (h % 2) + 64)
                n = NG * (qt + 1)
                for k in range(n):
                    g, kt = k // (qt + 1), k % (qt + 1)
                    ins = mm(ps[r, 4, 0:128], v_sb[:, kt, g, 64 * h:64 * h + 64],
                             pt_sb[u % 2][:, 128 * k:128 * k + 128], start=(k == 0), stop=(k == n - 1))
                ins.then_inc(S["us_pv"], 1)

            for hf in range(2):
                if hf:
                    sample_scores(hf)
                u0 = 8 * hf
                unit_scores(u0)
                sample_turn(hf)
                unit_scores(u0 + 1)
                for u in range(u0, u0 + 8):
                    unit_turn(u)
                    if u + 2 < u0 + 8:
                        unit_scores(u + 2)
                    if u > u0:
                        unit_pv(u - 1)
                    if u % 2:
                        sample_pv(hf, (u - u0) // 2)
                unit_pv(u0 + 7)
                sample_fold(hf)
            pe.wait_ge(S["oT_ready"], 2)
            for s in range(4):
                for z in range(2):
                    ins = wide(WO + s, s, ps[:, 2 * s + z, 0:T], oT, 0, HP, z * 512)
                ins.then_inc(S["tile_done"], 1)

        @block.tensor
        def _(pe):
            mm = nc.tensor.matmul

            def ada_tile(l, nb, c, bank=4, i=0):
                tile_wait(pe, ADA[l] + 8 * nb + c, 2 * i)
                for z in range(2):
                    ins = mm(ps[0:ROWS, bank + z, :], ccol[:, c * ROWS:(c + 1) * ROWS],
                             ring[:, c % RING, 512 * z:512 * z + 512], start=(c == 0), stop=(c == NC - 1))
                ins.then_inc(S["tile_done"], 1)

            def ada_turn(l, nb, half):
                pe.wait_ge(S["ada_row"], 2 * nb + (12 * l + half + 1))
                for q in range(4):
                    ins = mm(ps[:, 6, bass.ds((8 * nb + 4 * half + q) * ROWS, ROWS)],
                             gtmp[0:ROWS, 128 * q:128 * q + 128], ident[0:ROWS, 0:ROWS], start=True, stop=True)
                ins.then_inc(S["ada_turned"], 1)

            def mean_square(q):
                for c in range(NC):
                    if c % 4 == 0:
                        pe.wait_ge(S["sq_ready"], 2 * q + 1 + c // 4)
                    ins = mm(ps[:, 7, 0:T], ones, modsq[:, c, :] if q else hT[:, c, :], start=(c == 0), stop=(c == NC - 1))
                ins.then_inc(S["ms_ready"], 1)

            def wide(n, s, out, rhs, i=0, chunks=NC, off=0, h=0):
                tile_wait(pe, n, i)
                for c in range(chunks):
                    if h and c == 4:
                        pe.wait_ge(S["h_ready"], h)
                    ins = mm(out, ring[:, s, off + c * 128:off + (c + 1) * 128], rhs[:, c, :], start=(c == 0),
                             stop=(c == chunks - 1))
                return ins

            pe.wait_ge(S["in_setup"], 16 * 7)
            pe.wait_ge(S["silu_c"], 1)
            for nb in range(7):
                for c in range(NC):
                    if nb < 6:
                        if nb >= 2 and c == 0:
                            pe.wait_ge(S["ada_row"], 2 * nb - 2)
                        ada_tile(0, nb, c, 2 + 2 * (nb % 2))
                    if nb and c in (2, 5):
                        ada_turn(0, nb - 1, c // 3)
                if nb == 3:
                    mean_square(0)

            pe.wait_ge(S["s5_bb"], 1)
            pe.wait_ge(S["s5_bbi"], 1)
            pe.wait_ge(S["h_ready"], 2)
            pe.wait_ge(S["s5_cs"], 1)

            def s5_in(k):
                if k >= 3:
                    pe.wait_ge(S["s5_rot"], k - 2)
                c, gl = k // 4, 2 * (k % 4)
                for z, b in enumerate((bb_re, bb_im)):
                    ins = mm(ps[:, BU_BANK[k % 3] + z, 0:T], b[:, c, gl:gl + 2, :].rearrange("p g n -> p (g n)"),
                             hT[:, c, :], start=True, stop=True)
                ins.then_inc(S["s5_bu"], 1)

            def s5_out(k):
                c, kk = k // 4, k % 4
                pe.wait_ge(S["s5_op"], k + 1)
                pe.wait_ge(S["s5_sin"], k + 1)
                if kk == 0 and c >= 2:
                    pe.wait_ge(S["s5_hy"], c - 1)
                o = o5[k % 2]
                for n, z in enumerate((0, 1, 1, 2)):
                    ins = mm(ps[32 * kk:32 * kk + 32, 4 + c % 2, 0:T], cb[:, z, k, :], o[:, n, :], start=(n == 0),
                             stop=(n == 3))
                ins.then_inc(S["s5_ymm"], 1)

            for k in range(PAIRS + 3):
                if k < PAIRS:
                    s5_in(k)
                if k >= 3:
                    s5_out(k - 3)

            def glu(i, first):
                for m in range(2):
                    if not first:
                        pe.wait_ge(S["glu_used"], 2 * i + (m - 1))
                    for z in range(2):
                        s = 2 * m + z
                        pe.wait_ge(S["hi_ready"], 4 * i + (s + 1))
                        for c in range(NC):
                            w = wt_hi[:, s % 2, c * 128:(c + 1) * 128]
                            if first and s == 0:
                                pe.wait_ge(S["yh_ready"], c + 1)
                            mm(ps[:, s, 0:T], w, y_hi[:, c], start=(c == 0), stop=False)
                        for c in range(NC):
                            w = wt_hi[:, s % 2, c * 128:(c + 1) * 128]
                            if first and s == 0:
                                pe.wait_ge(S["yl_ready"], c + 1)
                            mm(ps[:, s, 0:T], w, y_lo[:, c], start=False, stop=False)
                        pe.wait_ge(S["lo_u"], 4 * i + (s + 1))
                        for c in range(NC):
                            ins = mm(ps[:, s, 0:T], ring_lo[:, s, c * 128:(c + 1) * 128], y_hi[:, c], start=False,
                                     stop=(c == NC - 1))
                        ins.then_inc(S["tile_done"], 1)

            glu(0, True)
            with pe.Fori(1, 4) as i:
                glu(i, False)

            def peer_pe(l):
                pe.wait_ge(S["h_ready"], 4 * l + 3)
                for m in range(8):
                    if m >= 4:
                        pe.wait_ge(S["q_copied"], 8 * l + m - 3)
                    wide(PQ[l] + m, m % 4, ps[:, m % 4, 0:T], modsq, h=0 if m else 4 * l + 4).then_inc(S["tile_done"], 1)

                def up(j, s, out):
                    pe.wait_ge(S["hi_ready"], j + (HI[l] + s + 1))
                    for c in range(NC):
                        w = wt_hi[:, s % 2, c * 128:(c + 1) * 128]
                        mm(out, w, h_hi[:, c], start=(c == 0), stop=False)
                        mm(out, w, h_lo[:, c], start=False, stop=False)
                    pe.wait_ge(S["lo_u"], j + (LO[l] + s + 1))
                    for c in range(NC):
                        ins = mm(out, ring_lo[:, s, c * 128:(c + 1) * 128], h_hi[:, c], start=False,
                                 stop=(c == NC - 1))
                    ins.then_inc(S["tile_done"], 1)

                def experts(j0, j1):
                    with pe.Fori(j0 // 4, j1 // 4) as i:
                        for s in range(4):
                            pe.wait_ge(S["gelu_done"], 4 * i + (s - 1 + 128 * l))
                            up(4 * i, s, ps[:, 6 + s % 2, 0:T])

                def q_norm(n):
                    pe.wait_ge(S["qsq_ready"], l + 1)
                    if n:
                        pe.wait_ge(S["qsd_ready"], 2 * l + 1)
                    for m in range(4):
                        ins = mm(ps[:, m, 0:T], blk64, qsq[:, 4 * n + m, :], start=True, stop=True)
                    ins.then_inc(S["qms_ready"], 1)

                def scores(n):
                    if n == 0:
                        pe.wait_ge(S["qn_ready"], l + 1)
                        pe.wait_ge(S["gate_in"], 48 * (l + 1))
                    if n == 2:
                        pe.wait_ge(S["sc_copied"], 3 * l + 1)
                    for h in range(PH):
                        for z in range(2):
                            r = slice(64 * z, 64 * z + 64)
                            if n != 1:
                                t0 = 128 * (n // 2)
                                out = ps[:, 2 * z + h // 4, (h % 4) * 128:(h % 4 + 1) * 128]
                                lhs = qraw[r, h, t0:t0 + 128]
                            else:
                                q = 32 * (h % 4)
                                out = ps[q:q + 32, 4 + z, (h // 4) * 128:(h // 4 + 1) * 128]
                                lhs = qraw[r, h, 256:T]
                            ins = mm(out, lhs, subk[r, h, :], start=True, stop=True)
                    ins.then_inc(S["sc_mm"], 1)

                pe.wait_ge(S["hh_ready"], l + 1)
                pe.wait_ge(S["hl_ready"], l + 1)
                for s in range(4):
                    if s >= 2:
                        pe.wait_ge(S["gelu_done"], 128 * l + s - 1)
                    up(0, s, ps[:, 6 + s % 2, 0:T])
                q_norm(0)
                experts(4, 8)
                q_norm(1)
                experts(8, 12)
                scores(0)
                scores(1)
                experts(12, 16)
                scores(2)
                experts(16, NB0 - 4)

                def last_experts(s0):
                    for s in (s0, s0 + 1):
                        pe.wait_ge(S["gelu_done"], NB0 - 4 + s - 1 + 128 * l)
                        up(NB0 - 4, s, ps[:, 6 + s % 2, 0:T])

                last_experts(0)
                pe.wait_ge(S["sel_ready"], l + 1)
                pe.wait_ge(S["sc_copied"], 3 * l + 3)
                for n in range(2):
                    for q in range(3):
                        ins = nc.tensor.transpose(ps[:, n, 128 * q:128 * q + 128],
                                                  sel3[:, q, 8 * n:8 * n + 8, :].rearrange("p u k -> p (u k)"), ident)
                    ins.then_inc(S["sel_t"], 1)
                for q in range(3):
                    ins = mm(ps[:, 2, 32 * q:32 * q + 32], selz[:, q, :], jsel, start=True, stop=True)
                ins.then_inc(S["sel_t"], 1)
                last_experts(2)
                pe.wait_ge(S["idx_ready"], 3 * l + 3)

                def gates(i, q, first):
                    n = q + GROUPS * l
                    pe.wait_ge(S["gb_o1"], GPI * i + (n + 1))
                    pe.wait_ge(S["gb_gate"], GPI * i + (n + 1))
                    if q >= 4 or not first:
                        pe.wait_ge(S["gb_cp"], GPI * i + (n - 3))
                    for t in range(4):
                        ins = mm(ps[:, q % 4, 128 * t:128 * t + 128], oh[:, 0, q % 2, t, :], oh[:, 1, q % 2, t, :],
                                 start=True, stop=True)
                    ins.then_inc(S["gb_mm"], 1)

                def gate_pass(i, first):
                    for q in range(GPI):
                        gates(i, q, first)
                        if l == 0:
                            if q < NC:
                                ada_tile(1, 0, q, 4, i)
                            if q in (9, 11):
                                ada_turn(1, i, (q - 9) // 2)

                if l == 0:
                    pe.wait_ge(S["gelu_done"], NB0)
                gate_pass(0, True)
                with pe.Fori(1, GROUPS // GPI) as i:
                    gate_pass(i, False)
                if l == 0:
                    pe.wait_ge(S["ada_done"], 2)
                experts(NB0, 128)
                pe.wait_ge(S["w_done"], (128 - NB0) * (l + 1))
                pe.wait_ge(S["gb_cp"], GROUPS * (l + 1))

                def down(i, first, last=False):
                    for s in range(4):
                        pe.wait_ge(S["hi_ready"], 4 * i + (HI[l] + 128 + s + 1))
                        pe.wait_ge(S["wh_ready"], 4 * i + (128 * l + s + 1))
                        for c in range(NC):
                            mm(ps[:, c, 0:T], wt_hi[:, s % 2, c * 128:(c + 1) * 128], w_hi[:, s % 2],
                               start=(first and s == 0), stop=False, skip_group_check=True)
                        pe.wait_ge(S["wl_ready"], 4 * i + (128 * l + s + 1))
                        for c in range(NC):
                            mm(ps[:, c, 0:T], wt_hi[:, s % 2, c * 128:(c + 1) * 128], w_lo[:, s % 2],
                               start=False, stop=False, skip_group_check=True)
                        pe.wait_ge(S["lo_v"], 4 * i + (128 * l + s + 1))
                        for c in range(NC):
                            ins = mm(ps[:, c, 0:T], ring_lo[:, s, c * 128:(c + 1) * 128], w_hi[:, s % 2],
                                     start=False, stop=(last and s == 3), skip_group_check=True)
                        ins.then_inc(S["tile_done"], 1)

                down(0, True)
                with pe.Fori(1, 31) as i:
                    down(i, False)
                down(31, False, True)

            mean_square(1)
            peer_pe(0)
            mean_square(2)
            attention_pe(pe, wide)
            mean_square(3)
            peer_pe(1)

        def attention_dve(v, own, residual):
            TT, TS, STT, CP = (nc.vector.tensor_tensor, nc.vector.tensor_scalar, nc.vector.scalar_tensor_tensor,
                               nc.vector.tensor_copy)
            v.wait_ge(S["in_att"], 80)

            def finish(gs):
                q = qk[:, 4 * gs:4 * gs + 4, :]
                v.wait_ge(S["aq_rot"], gs + 1)
                own(TT(asq, ps[:, 4:8, 0:T], rope[:, 1].unsqueeze(1).broadcast_to([P, 4, T]), ALU.mult))
                own(TT(q, q, rope[:, 0].unsqueeze(1).broadcast_to([P, 4, T]), ALU.mult))
                own.settle()
                TT(q, q, asq, ALU.add).then_inc(S["aq_done"], 1)

            def scale_qk(gs):
                q = qk[:, 4 * gs:4 * gs + 4, :]
                v.wait_ge(S["aq_sd"], gs + 1)
                nc.vector.reciprocal(ars, ars).then_inc(S["aq_rc"], 1)
                v.wait_ge(S["aq_sp"], gs + 1)
                STT(out=q, in0=q, scalar=(kg if gs % 2 else qg), in1=ps[:, 4:8, 0:T], op0=ALU.mult, op1=ALU.mult)\
                    .then_inc(S["aq_qn"], 1)
                v.wait_ge(S["aq_qn"], gs + 1)

            for gs in range(6):
                if gs:
                    scale_qk(gs - 1)
                    finish(gs - 1)
                    v.wait_ge(S["aq_done"], gs)
                v.wait_ge(S["aq_copied"], gs + 1)
                q = qk[:, 4 * gs:4 * gs + 4, :]
                TT(asq, q, q, ALU.mult).then_inc(S["aq_sq"], 1)
            scale_qk(5)
            finish(5)

            def sample_max(hf):
                v.wait_ge(S["ss_mm"], hf + 1)
                own(STT(out=ps_s[:, 0:512], in0=ps[:, 5, :], scalar=E ** -0.5, in1=smaskv[:, 0:512],
                        op0=ALU.mult, op1=ALU.add))
                own(STT(out=ps_s[:, 512:CK], in0=ps[:, 6, 0:CK - 512], scalar=E ** -0.5, in1=smaskv[:, 512:CK],
                        op0=ALU.mult, op1=ALU.add))
                own(STT(out=ps_s[:, CK:SW], in0=ps[:, 6, CK - 512:SW - 512], scalar=E ** -0.5,
                        in1=smaskv[:, CK + 96 * hf:CK + 96 * hf + 96], op0=ALU.mult, op1=ALU.add))
                own.settle()
                own(nc.vector.tensor_reduce(sst[:, 2:3], ps_s, X, ALU.max))
                own.settle()
                TS(sst[:, 0:1], sst[:, 2:3], -1.0, None, ALU.mult).then_inc(S["ss_max"], 1)

            def sample_norm(hf):
                v.wait_ge(S["ss_exp"], hf + 1)
                own(nc.vector.reciprocal(sst[:, 3:4], sst[:, 1:2]))
                own.settle()
                TS(ps_s, ps_s, sst[:, 3:4], None, ALU.mult).then_inc(S["ss_norm"], 1)

            def sample_out(hf):
                v.wait_ge(S["ss_pv"], hf + 1)
                CP(ps_s[:, 0:512], ps[:, 7, :]).then_inc(S["ss_oc"], 1)
                v.wait_ge(S["ss_ot"], hf + 1)
                t0 = 256 + 16 * hf
                for q in range(HP):
                    for h2 in range(2):
                        r, c = slice(64 * h2, 64 * h2 + 64), 8 * q + 4 * h2
                        src = ps[r, 2, 128 * q:128 * q + 128].rearrange("p (b n) -> p b n", b=4)[:, :, c:c + 4]
                        ins = CP(oT[r, q, t0:t0 + 16].rearrange("p (b t) -> p b t", b=4), src)
                ins.then_inc(S["oT_ready"], 1)

            def unit_max(u):
                qt = u // H
                w = 384 * (qt + 1)
                v.wait_ge(S["us_mm"], u + 1)
                if u >= 3:
                    v.wait_ge(S["us_t"], u - 2)
                p, b0 = p_sb[u % 3][:, 0:w], 5 * (u % 2)
                own(STT(out=p, in0=ps[:, b0:b0 + 2, :].rearrange("p b n -> p (b n)")[:, 0:w], scalar=E ** -0.5,
                        in1=pmask[:, 384 * qt:384 * qt + w], op0=ALU.mult, op1=ALU.add))
                own.settle()
                own(nc.vector.tensor_reduce(ust[:, 2, u:u + 1], p, X, ALU.max))
                own.settle()
                TS(ust[:, 0, u:u + 1], ust[:, 2, u:u + 1], -1.0, None, ALU.mult).then_inc(S["us_max"], 1)

            def unit_den(u):
                v.wait_ge(S["us_exp"], u + 1)
                own(nc.vector.reciprocal(ust[:, 1, u:u + 1], ust[:, 1, u:u + 1]))
                own.settle()
                p = p_sb[u % 3][:, 0:384 * (u // H + 1)]
                TS(p, p, ust[:, 1, u:u + 1], None, ALU.mult).then_inc(S["us_norm"], 1)

            def unit_out(u):
                qt, h = u // H, u % H
                r = slice(64 * (h % 2), 64 * (h % 2) + 64)
                v.wait_ge(S["us_pv"], u + 1)
                CP(oT[r, h // 2, 128 * qt:128 * qt + 128], ps[r, 4, 0:128]).then_inc(S["us_o"], 1)

            for hf in range(2):
                u0 = 8 * hf
                sample_max(hf)
                unit_max(u0)
                sample_norm(hf)
                unit_max(u0 + 1)
                for u in range(u0, u0 + 8):
                    unit_den(u)
                    if u + 2 < u0 + 8:
                        unit_max(u + 2)
                    if u > u0:
                        unit_out(u - 1)
                unit_out(u0 + 7)
                sample_out(hf)
            v.wait_ge(S["tile_done"], WO + 4)
            residual(ada[:, 1, 2], ps[:, :, 0:T], 0, NC, gtmp[:, 0:256].rearrange("p (c t) -> p c t", c=NC), S["x_ready"])

        @block.vector
        def _(v):
            own = Count(v, S["v_own"])
            TT, TS, STT, CP = (nc.vector.tensor_tensor, nc.vector.tensor_scalar, nc.vector.scalar_tensor_tensor,
                               nc.vector.tensor_copy)
            own(nc.vector.memset(eps_c[:, :], EPS))
            v.wait_ge(S["in_setup"], 16 * 7)

            def square_x(q, dst):
                for m in (slice(0, 4), slice(4, 8)):
                    TT(dst[:, m], xT[:, m], xT[:, m], ALU.mult).then_inc(S["sq_ready"], 1)

            own.settle()
            square_x(0, hT)
            v.wait_ge(S["in_s5"], 16 * 6)
            v.wait_ge(S["s5_trig"], 1)
            own(TT(sth, lim, ldt, ALU.mult))
            own(TT(sr, lre, ldt, ALU.mult))
            own.settle()
            own(TS(sq1, sth, 1.0 / TWO_PI, MAGIC, ALU.mult, ALU.add))
            own.settle()
            own(TS(sq1, sq1, MAGIC, None, ALU.subtract))
            own.settle()
            for part in (C1, C2, C3):
                own(STT(out=sth, in0=sq1, scalar=-part, in1=sth, op0=ALU.mult, op1=ALU.add))
                own.settle()
            TS(sth, sth, PI_LO, -PI_LO, ALU.min, ALU.max).then_inc(S["s5_thr"], 1)
            v.wait_ge(S["s5_trig"], 2)
            own(TT(scos, scos, scos, ALU.mult))
            own.settle()
            TS(scos, scos, -2.0, 1.0, ALU.mult, ALU.add).then_inc(S["s5_thr"], 1)
            v.wait_ge(S["s5_trig"], 3)
            v.wait_ge(S["s5_thr"], 2)
            own(CP(r_col, sr[:, 512:LW]))
            a = slice(0, 512)
            are, aim, den, t1 = sq1[:, a], sth[:, a], ldt[:, a], st1[:, a]
            own(TT(are, sr[:, a], scos[:, a], ALU.mult))
            own(TT(aim, sr[:, a], ssin[:, a], ALU.mult))
            own(TT(den, lre[:, a], lre[:, a], ALU.mult))
            own(TT(t1, lim[:, a], lim[:, a], ALU.mult))
            own.settle()
            own(TS(are, are, 1.0, None, ALU.subtract))
            own(TT(den, den, t1, ALU.add))
            own.settle()
            own(nc.vector.reciprocal(den, den))
            own(TT(t1, are, lre[:, a], ALU.mult))
            own(TT(sr[:, a], aim, lim[:, a], ALU.mult))
            own.settle()
            own(TT(t1, t1, sr[:, a], ALU.add))
            own(TT(aim, aim, lre[:, a], ALU.mult))
            own(TT(are, are, lim[:, a], ALU.mult))
            own.settle()
            own(TT(aim, aim, are, ALU.subtract))
            own(TT(t1, t1, den, ALU.mult))
            own.settle()
            own(TT(aim, aim, den, ALU.mult))
            own.settle()
            own(TT(lre[:, a], t1, sbre, ALU.mult))
            own(TT(lim[:, a], aim, sbim, ALU.mult))
            own(TT(are, t1, sbim, ALU.mult))
            own(TT(den, aim, sbre, ALU.mult))
            own.settle()
            own(TT(sbre, lre[:, a], lim[:, a], ALU.subtract))
            own(TT(sbim, are, den, ALU.add))
            b = slice(512, LW)
            ec, es, tc, ts = scos[:, b], ssin[:, b], lre[:, b], lim[:, b]
            td = ldt[:, b]
            own(nc.vector.memset(tcos[:, :, 0:1], 1.0))
            own(nc.vector.memset(tsin[:, :, 0:1], 0.0))
            own.settle()
            n = 1
            scr = bb_im_f
            while n < 256:
                s1 = scr[:, 0:PAIRS * n].rearrange("p (k t) -> p k t", k=PAIRS)
                s2 = bb_re.rearrange("p c g n -> p (c g n)")[:, 0:PAIRS * n].rearrange("p (k t) -> p k t", k=PAIRS)
                cc, ss = (e.unsqueeze(2).broadcast_to([P, PAIRS, n]) for e in (ec, es))
                own(TT(tcos[:, :, n:2 * n], tcos[:, :, 0:n], cc, ALU.mult))
                own(TT(s1, tsin[:, :, 0:n], ss, ALU.mult))
                own(TT(tsin[:, :, n:2 * n], tsin[:, :, 0:n], cc, ALU.mult))
                own(TT(s2, tcos[:, :, 0:n], ss, ALU.mult))
                own(TT(tc, ec, ec, ALU.mult))
                own(TT(ts, es, es, ALU.mult))
                own(TT(td, ec, es, ALU.mult))
                own.settle()
                own(TT(tcos[:, :, n:2 * n], tcos[:, :, n:2 * n], s1, ALU.subtract))
                own(TT(tsin[:, :, n:2 * n], tsin[:, :, n:2 * n], s2, ALU.add))
                own(TT(ec, tc, ts, ALU.subtract))
                own(TS(es, td, 2.0, None, ALU.mult))
                own.settle()
                n *= 2
            for tab in (tcos, tsin):
                src = tab[:, :, 1:5].unsqueeze(2).broadcast_to([P, PAIRS, SB, ST])
                ins = CP(tab[:, :, 256:T].rearrange("p k (b t) -> p k b t", b=SB), src)
            ins.then_inc(S["s5_tab"], 1)

            def ada_finish(l):
                v.wait_ge(S["ada_turned"], 12 * (l + 1))
                flat = ada_t[:, l * 48 * ROWS:(l + 1) * 48 * ROWS].rearrange("p (m r) -> p m r", r=ROWS)
                own(TT(flat, ps[:, 6, 0:48 * ROWS].rearrange("p (m r) -> p m r", r=ROWS),
                       bias_t[:, 48 * l:48 * l + 48].unsqueeze(2).broadcast_to([P, 48, ROWS]), ALU.add))
                own.settle()
                for w in range(2):
                    sc = ada[:, l, 3 * w + 1]
                    g0 = (2 * l + w) * NC
                    ins = STT(out=sc, in0=sc, scalar=1.0,
                              in1=gain_t[:, g0:g0 + NC].unsqueeze(2).broadcast_to([P, NC, ROWS]),
                              op0=ALU.add, op1=ALU.mult)
                ins.then_inc(S["ada_done"], 1)

            def by_sample(row):
                return row.unsqueeze(3).broadcast_to([P, row.shape[1], SB, ST])

            def tokens4(x):
                return x.rearrange("p c (b t) -> p c b t", b=SB)

            def modulate(q):
                l, w = q // 2, q % 2
                v.wait_ge(S["std_ready"], q + 1)
                own(nc.vector.reciprocal(rstd, rstd))
                own.settle()
                h = modsq if q else hT
                sc, sh = ada[:, l, 3 * w + 1], ada[:, l, 3 * w]
                for half in range(2):
                    m = slice(4 * half, 4 * half + 4)
                    own(TT(h[:, m], xT[:, m], rstd.unsqueeze(1).broadcast_to([P, 4, T]), ALU.mult))
                    own.settle()
                    hs = tokens4(h[:, m, 256:T])
                    own(TT(hs, hs, by_sample(sc[:, m, 1:]), ALU.mult))
                    for c in range(4 * half, 4 * half + 4):
                        own(TS(h[:, c, 0:256], h[:, c, 0:256], sc[:, c, 0:1], sh[:, c, 0:1], ALU.mult, ALU.add))
                    own.settle()
                    TT(hs, hs, by_sample(sh[:, m, 1:]), ALU.add).then_inc(S["h_ready"], 1)

            def residual(gate, src, m0, m1, tmp, done):
                own(TT(tokens4(tmp), tokens4(src[:, :, 256:T]), by_sample(gate[:, m0:m1, 1:]), ALU.mult))
                for m in range(m0, m1):
                    own(STT(out=xT[:, m, 0:256], in0=src[:, m - m0, 0:256], scalar=gate[:, m, 0:1],
                            in1=xT[:, m, 0:256], op0=ALU.mult, op1=ALU.add))
                own.settle()
                TT(xT[:, m0:m1, 256:T], xT[:, m0:m1, 256:T], tmp, ALU.add).then_inc(done, 1)

            ada_finish(0)
            v.wait_ge(S["ada_done"], 1)
            modulate(0)
            v.wait_ge(S["h_ready"], 2)
            v.wait_ge(S["s5_bb"], 1)
            v.wait_ge(S["s5_bbi"], 1)

            def twice(table):
                return table.unsqueeze(1).broadcast_to([P, 2, T])

            def rot_in(k):
                v.wait_ge(S["s5_bu"], k + 1)
                if k >= 2:
                    v.wait_ge(S["s5_zin"], k - 1)
                reim, m = ps[:, BU_BANK[k % 3]:BU_BANK[k % 3] + 2, 0:T], m5[k % 2]
                TT(m[:, 0:2], twice(tcos[:, k]), reim, ALU.mult)
                TT(m[:, 2:4], twice(tsin[:, k]), reim, ALU.mult).then_inc(S["s5_rot"], 1)

            def scan(k):
                v.wait_ge(S["s5_zin"], k + 1)
                v.wait_ge(S["s5_rmr"], k + 1)
                for z in range(2):
                    ins = nc.vector.tensor_tensor_scan(zin[k % 2][:, z], rm5[k % 2], zin[k % 2][:, z], 0.0,
                                                       ALU.mult, ALU.add)
                ins.then_inc(S["s5_z"], 1)
                v.wait_ge(S["s5_z"], k + 1)
                if k >= 2:
                    v.wait_ge(S["s5_ymm"], k - 1)
                TT(o5[k % 2][:, 0:2], twice(tcos[:, k]), zin[k % 2], ALU.mult)
                TT(o5[k % 2][:, 2], tsin[:, k], zin[k % 2][:, 0], ALU.mult).then_inc(S["s5_op"], 1)

            def chunk_y(c):
                v.wait_ge(S["s5_ymm"], 4 * c + 4)
                STT(out=hT[:, c], in0=hT[:, c], scalar=dskip[:, c:c + 1], in1=ps[:, 4 + c % 2, 0:T],
                    op0=ALU.mult, op1=ALU.add).then_inc(S["s5_hy"], 1)

            for k in range(PAIRS + 3):
                if k < PAIRS:
                    rot_in(k)
                if 1 <= k <= PAIRS:
                    scan(k - 1)
                if k >= 6 and (k - 6) % 4 == 0:
                    chunk_y((k - 6) // 4)
            v.wait_ge(S["s5_zl"], PAIRS)
            zr, zi = zl[:, 0], zl[:, 1]
            co, si = tcos[:, :, 255:T:4], tsin[:, :, 255:T:4]
            own(TT(st[:, 0], zr, co, ALU.mult))
            own(TT(st[:, 1], zi, co, ALU.mult))
            own(TT(zr, zr, si, ALU.mult))
            own(TT(zi, zi, si, ALU.mult))
            own.settle()
            TT(st[:, 0], st[:, 0], zi, ALU.subtract)
            TT(st[:, 1], st[:, 1], zr, ALU.add).then_inc(S["s5_rm"], 1)
            for m in range(NC):
                v.wait_ge(S["glu_sig"], m + 1)
                g = gtmp[:, (m % 2) * T:(m % 2 + 1) * T]
                TT(g, ps[:, 2 * (m % 2), 0:T], g, ALU.mult).then_inc(S["glu_used_v"], 1)
                v.wait_ge(S["glu_used_v"], m + 1)
                residual(ada[:, 0, 2], g.unsqueeze(1), m, m + 1, small[:, 64:96].unsqueeze(1), S["glu_used"])
            v.wait_ge(S["glu_used"], NC)
            v.wait_ge(S["s5_rm"], 1)
            square_x(1, modsq)

            def peer_dve(l):
                last = S["q_copied"]
                v.wait_ge(last, 8 * l + 8)
                TT(qsq, qraw, qraw, ALU.mult).then_inc(S["qsq_ready"], 1)
                for n in range(2):
                    q, r = qraw[:, 4 * n:4 * n + 4, :], qrs[:, 4 * n:4 * n + 4, :]
                    v.wait_ge(S["qsd_ready"], 2 * l + n + 1)
                    own(nc.vector.reciprocal(r, r))
                    own.settle()
                    ins = TT(q, q, r, ALU.mult)
                ins.then_inc(S["qn_ready"], 1)
                v.wait_ge(S["sc_copied"], 3 * l + 3)
                s4 = s_sb.rearrange("p (u z k) -> p u z k", u=UNITS, z=2)
                s24 = s_two.rearrange("p (u z k) -> p u z k", u=UNITS, z=2)
                uz = [(u, z) for u in range(UNITS) for z in range(2)]
                VM, VI, MR = nc.vector.max, nc.vector.max_index, nc.vector.match_replace
                for u, z in uz:
                    own(VM(v16[:, u, z, 0:8], s4[:, u, z]))
                own.settle()
                for u, z in uz:
                    own(VI(i16u[:, u, z, 0:8], v16[:, u, z, 0:8], s4[:, u, z]))
                    own(MR(s24[:, u, z], v16[:, u, z, 0:8], s4[:, u, z], -3.0e38))
                own.settle()
                for u, z in uz:
                    own(VM(v16[:, u, z, 8:16], s24[:, u, z]))
                own.settle()
                for u, z in uz:
                    own(VI(i16u[:, u, z, 8:16], v16[:, u, z, 8:16], s24[:, u, z]))
                cu = cand[:, 0:UNITS * NCAND].rearrange("p (u n) -> p u n", u=UNITS)
                c2 = s_sb[:, 0:UNITS * NCAND].rearrange("p (u n) -> p u n", u=UNITS)
                for n0, a0, a1, nb in ((0, 0, 4, 16), (64, 4, 16, 4)):
                    na = a1 - a0
                    own(TT(cu[:, :, n0:n0 + na * nb].rearrange("p u (a b) -> p u a b", a=na),
                           v16[:, :, 0, a0:a1].unsqueeze(3).broadcast_to([P, UNITS, na, nb]),
                           v16[:, :, 1, 0:nb].unsqueeze(2).broadcast_to([P, UNITS, na, nb]), ALU.add))
                own.settle()
                own(CP(i16, i16u))
                own(CP(iota16, iota[:, 0:16]))
                for u in range(UNITS):
                    own(VM(best[:, u, 0:8], cu[:, u]))
                own.settle()
                for u in range(UNITS):
                    own(VI(selu[:, u, 0:8], best[:, u, 0:8], cu[:, u]))
                    own(MR(c2[:, u], best[:, u, 0:8], cu[:, u], -3.0e38))
                own.settle()
                for u in range(UNITS):
                    own(VM(best[:, u, 8:16], c2[:, u]))
                own.settle()
                for u in range(UNITS):
                    own(VI(selu[:, u, 8:16], best[:, u, 8:16], c2[:, u]))
                own(CP(gsum[:, 0:UNITS], best[:, :, 0]))
                own.settle()
                TT(best, best, gsum[:, 0:UNITS].unsqueeze(2).broadcast_to([P, UNITS, 16]), ALU.subtract)\
                    .then_inc(S["gate_exp"], 1)
                sf = selu.rearrange("p u k -> p (u k)")
                for z, (amount, op) in enumerate(((4, ALU.logical_shift_right), (15, ALU.bitwise_and),
                                                  (2, ALU.logical_shift_right), (3, ALU.bitwise_and),
                                                  (6, ALU.logical_shift_right))):
                    own(TS(selabu[:, z], sf, amount, None, op))
                own.settle()
                own(CP(selab5, selabu))
                own.settle()
                ab, other = selab5[:, 0:2], selab5[:, 2:4]
                own(TS(selab5[:, 2], selab5[:, 2], 12.0, None, ALU.subtract))
                own.settle()
                own(TT(other, other, ab, ALU.subtract))
                own.settle()
                own(TT(other, other, selab5[:, 4].unsqueeze(1).broadcast_to([P, 2, KU]), ALU.mult))
                own.settle()
                own(TT(ab, ab, other, ALU.add))
                own.settle()
                e4 = e_bf.rearrange("p (u k a) -> p u k a", u=UNITS, k=16)
                for z in range(2):
                    own(TT(e4, ab[:, z].rearrange("p (u k) -> p u k", k=16).unsqueeze(3)
                           .broadcast_to([P, UNITS, 16, 16]),
                           iota16.unsqueeze(1).unsqueeze(1).broadcast_to([P, UNITS, 16, 16]), ALU.is_equal))
                    own.settle()
                    own(TT(e4, e4, i16[:, :, z].unsqueeze(2).broadcast_to([P, UNITS, 16, 16]), ALU.mult))
                    own.settle()
                    for n in (8, 4, 2):
                        own(TT(e4[:, :, :, 0:n], e4[:, :, :, 0:n], e4[:, :, :, n:2 * n], ALU.add))
                        own.settle()
                    own(TT(sel3[:, z], e4[:, :, :, 0], e4[:, :, :, 1], ALU.add))
                    own.settle()
                v.wait_ge(S["gate_exp"], 2 * l + 2)
                own(nc.vector.tensor_reduce(gsum[:, 0:UNITS], best, X, ALU.add))
                own.settle()
                own(nc.vector.reciprocal(gsum[:, 0:UNITS], gsum[:, 0:UNITS]))
                own.settle()
                own(TT(sel3[:, 2], best, gsum[:, 0:UNITS].unsqueeze(2).broadcast_to([P, UNITS, 16]), ALU.mult))
                own.settle()
                v.wait_ge(S["gate_in"], 48 * (l + 1))
                for q in range(3):
                    ins = TT(selz[:, q].rearrange("p (u h k) -> p u h k", u=2, h=4),
                             sel3[:, q, 16:18].unsqueeze(2).broadcast_to([P, 2, 4, 16]),
                             hqm.unsqueeze(1).unsqueeze(3).broadcast_to([P, 2, 4, 16]), ALU.mult)
                ins.then_inc(S["sel_ready"], 1)
                v.wait_ge(S["idx_ready"], 3 * l + 3)
                v.wait_ge(S["gelu_done"], 128 * l + NB0)

                def one_hots(i, q, first):
                    n = q + GROUPS * l
                    if q >= 2 or not first:
                        v.wait_ge(S["gb_mm"], GPI * i + (n - 1))
                    for w in (1, 0):
                        TT(oh[:, w, q % 2], iota.unsqueeze(1).broadcast_to([P, 4, 128]),
                           idx[:, w, bass.ds(4 * GPI * i + 4 * q, 4)].unsqueeze(2).broadcast_to([P, 4, 128]),
                           ALU.is_equal).then_inc(S[f"gb_o{w + 1}"], 1)

                def gate_low(i, q):
                    v.wait_ge(S["gb_mm"], GPI * i + (q + 1 + GROUPS * l))
                    w = W[:, 0:NB0, bass.ds(4 * GPI * i + 4 * q, 4)]
                    TT(w, w, ps[:, q % 4, :].rearrange("p (t j) -> p j t", t=4)[:, 0:NB0, :], ALU.mult)\
                        .then_inc(S["gb_mul"], 1)

                def gate_pass(i, first):
                    for q in range(GPI):
                        one_hots(i, q, first)
                        if q or not first:
                            gate_low(i, q - 1)

                gate_pass(0, True)
                with v.Fori(1, GROUPS // GPI) as i:
                    gate_pass(i, False)
                gate_low(GROUPS // GPI - 1, GPI - 1)
                if l == 0:
                    ada_finish(1)
                v.wait_ge(S["gb_cp"], GROUPS * (l + 1))
                v.wait_ge(S["gb_cp"], 72 * (l + 1))
                with v.Fori(NB0 // 4, 32) as i:
                    for s in range(4):
                        v.wait_ge(S["gelu_done"], 4 * i + (s + 1 + 128 * l))
                        w = W[:, bass.ds(4 * i + s, 1), :].rearrange("p a t -> p (a t)")
                        TT(w, w, gtmp[:, (s % 2) * T:(s % 2 + 1) * T], ALU.mult).then_inc(S["w_done"], 1)
                with v.Fori(0, 32) as i:
                    for s in range(4):
                        v.wait_ge(S["hi_ready"], 4 * i + (HI[l] + 128 + s + 1))
                        TT(ring_lo[:, s], ring[:, s], wt_hi[:, s % 2].bitcast(F32), ALU.subtract)\
                            .then_inc(S["lo_v"], 1)
                v.wait_ge(S["tile_done"], VT[l] + 128)
                residual(ada[:, l, 5], ps[:, :, 0:T], 0, NC, gtmp[:, 0:256].rearrange("p (c t) -> p c t", c=NC),
                         S["x_ready"])

            modulate(1)
            peer_dve(0)
            v.wait_ge(S["x_ready"], 1)
            square_x(2, modsq)
            modulate(2)
            v.wait_ge(S["hq_ready"], 2)
            TT(h_lo[:, 4:8], modsq[:, 4:8], h_hi[:, 4:8].bitcast(F32), ALU.subtract).then_inc(S["hq_lo_v"], 1)
            attention_dve(v, own, residual)
            v.wait_ge(S["x_ready"], 2)
            square_x(3, modsq)
            modulate(3)
            peer_dve(1)

        @block.gpsimd
        def _(pool):
            own = Count(pool, S["p_own"])
            TT, TS, CP = nc.gpsimd.tensor_tensor, nc.gpsimd.tensor_scalar, nc.gpsimd.tensor_copy
            pool.wait_ge(S["in_s5"], 16 * 6)
            TS(cb[:, 2], cb[:, 0], -1.0, None, ALU.mult)
            TS(cb[:, 1], cb[:, 1], -1.0, None, ALU.mult).then_inc(S["s5_cs"], 1)
            pool.wait_ge(S["in_setup"], 16 * 7)
            pool.wait_ge(S["s5_tab"], 1)
            for gl in range(8):
                ins = TS(bb_im[:, :, gl, :], sbim.rearrange("p (c n) -> p c n", c=NC), gmask[:, gl:gl + 1], None,
                         ALU.mult)
            ins.then_inc(S["s5_bbi"], 1)
            pool.wait_ge(S["s5_bbi"], 1)
            pool.wait_ge(S["s5_bb"], 1)

            def z_in(k):
                m, z = m5[k % 2], zin[k % 2]
                if k >= 2:
                    pool.wait_ge(S["s5_op"], k - 1)
                    pool.wait_ge(S["s5_sin"], k - 1)
                    pool.wait_ge(S["s5_zl"], k - 1)
                pool.wait_ge(S["s5_rot"], k + 1)
                own(TT(z[:, 0], m[:, 0], m[:, 3], ALU.add))
                own(TT(z[:, 1], m[:, 1], m[:, 2], ALU.subtract))
                own.settle()
                pool.wait_ge(S["s5_rmr"], k + 1)
                first = z[:, :, 256:T].rearrange("p z (b t) -> p z b t", t=ST)[:, :, :, 0]
                TT(first, first, hr5[k % 2], ALU.add).then_inc(S["s5_zin"], 1)

            def sin_z(k):
                pool.wait_ge(S["s5_z"], k + 1)
                if k >= 2:
                    pool.wait_ge(S["s5_ymm"], k - 1)
                TT(o5[k % 2][:, 3], tsin[:, k], zin[k % 2][:, 1], ALU.mult).then_inc(S["s5_sin"], 1)

            def y_low(c):
                pool.wait_ge(S["yh_ready"], c + 1)
                TT(y_lo[:, c], hT[:, c], y_hi[:, c].bitcast(F32), ALU.subtract).then_inc(S["yl_ready"], 1)

            for k in range(PAIRS + 1):
                if k < PAIRS:
                    z_in(k)
                if k >= 1:
                    sin_z(k - 1)
                if k >= 10 and k % 4 == 2:
                    y_low(k // 4 - 2)
            for c in (NC - 2, NC - 1):
                y_low(c)

            def low_u(l, j0, j1):
                with pool.Fori(j0 // 4, j1 // 4) as i:
                    for s in range(4):
                        pool.wait_ge(S["hi_ready"], 4 * i + (HI[l] + s + 1))
                        TT(ring_lo[:, s], ring[:, s], wt_hi[:, s % 2].bitcast(F32), ALU.subtract)\
                            .then_inc(S["lo_u"], 1)

            with pool.Fori(0, 4) as i:
                for s in range(4):
                    pool.wait_ge(S["hi_ready"], 4 * i + (s + 1))
                    TT(ring_lo[:, s], ring[:, s], wt_hi[:, s % 2].bitcast(F32), ALU.subtract).then_inc(S["lo_u"], 1)

            def peer_pool(l):
                pool.wait_ge(S["hh_ready"], l + 1)
                TT(h_lo, modsq, h_hi.bitcast(F32), ALU.subtract).then_inc(S["hl_ready"], 1)
                low_u(l, 0, NB0)
                with pool.Fori(0, GROUPS // GPI) as i:
                    for q in range(GPI):
                        pool.wait_ge(S["gb_o2"], GPI * i + (q + 1 + GROUPS * l))
                        o = oh[:, 1, q % 2]
                        TT(o, o, idx[:, 2, bass.ds(4 * GPI * i + 4 * q, 4)].unsqueeze(2).broadcast_to([P, 4, 128]),
                           ALU.mult).then_inc(S["gb_gate"], 1)
                low_u(l, NB0, 128)
                with pool.Fori(0, 32) as i:
                    for s in range(4):
                        pool.wait_ge(S["wh_ready"], 4 * i + (128 * l + s + 1))
                        TT(w_lo[:, s % 2], W[:, bass.ds(4 * i + s, 1), :].rearrange("p a t -> p (a t)"),
                           w_hi[:, s % 2].bitcast(F32), ALU.subtract).then_inc(S["wl_ready"], 1)

            peer_pool(0)
            pool.wait_ge(S["tile_done"], VT[0] + 128)
            own(nc.gpsimd.memset(qz_t, 0.0))
            own.settle()
            pool.wait_ge(S["hq_ready"], 1)
            TT(h_lo[:, 0:4], modsq[:, 0:4], h_hi[:, 0:4].bitcast(F32), ALU.subtract).then_inc(S["hq_lo"], 1)
            with pool.Fori(0, 6) as i:
                for s in range(4):
                    pool.wait_ge(S["hi_ready"], 4 * i + (HI[0] + 256 + s + 1))
                    TT(ring_lo[:, s], ring[:, s], wt_hi[:, s % 2].bitcast(F32), ALU.subtract).then_inc(S["lo_u"], 1)
            pool.wait_ge(S["aq_done"], 6)
            for g in range(NG):
                for q in range(HP):
                    for h2 in range(2):
                        r = slice(64 * h2, 64 * h2 + 64)
                        ins = CP(qz[r, g, :, q, 2 * q + h2, :],
                                 qk[r, 8 * g + q, 256:T].rearrange("p (b t) -> p b t", b=SB))
            ins.then_inc(S["qz_ready"], 1)
            peer_pool(1)


def kernel(**inp):
    import numpy as np
    import concourse.bacc as bacc
    from concourse import mybir as mb
    from concourse.bass_utils import run_bass_kernel_spmd

    a = {k: np.asarray(v) for k, v in inp.items()}
    f = np.float32
    ca = np.ascontiguousarray

    def cols(w, nt, kc=8):
        return w.reshape(kc, P, nt, P).transpose(2, 1, 0, 3).reshape(nt, P, kc * P)

    def u_tiles(u):
        return u.reshape(128, 128, 8, 128).transpose(1, 3, 2, 0).reshape(128, P, 1024)

    def v_tiles(w):
        return w.reshape(128, 128, 1024).transpose(1, 0, 2)

    glu = cols(a["ssm_w_glu"][0], 16).reshape(2, 8, P, 1024).transpose(1, 0, 2, 3).reshape(16, P, 1024)
    wq = a["attn_w_qkv"][0].reshape(D, 3, 3, 512)
    qkt = cols(ca(wq[:, :, 0:2].reshape(D, 3072)), 24)
    vpt = wq[:, :, 2].reshape(4, 2, P, 3, 512).transpose(3, 0, 2, 1, 4).reshape(12, P, 1024)
    wo = cols(a["attn_w_o"][0], 8, 4).reshape(4, 2, P, 512).transpose(0, 2, 1, 3).reshape(4, P, 1024)
    ada = [w.reshape(8, P, 6, 1024).transpose(2, 0, 1, 3).reshape(48, P, 1024) for w in a["ada_w"]]
    u0 = u_tiles(a["peer_u"][0])
    parts = [ada[0], glu, cols(a["peer_w_q"][0], 8), u0[:NB0], ada[1], u0[NB0:], v_tiles(a["peer_v"][0]), qkt, vpt, wo, cols(a["peer_w_q"][1], 8),
             u_tiles(a["peer_u"][1]), v_tiles(a["peer_v"][1])]
    A = {"stream": np.concatenate(parts)}
    x = np.concatenate([a["x_prompt"][0], a["x_sample"].reshape(32, D)])
    A["xT"] = x.reshape(T, NC, P).transpose(2, 1, 0).reshape(P, NC * T)
    c = np.concatenate([a["c_prompt"], a["c_sample"]])
    A["ccol"] = c.reshape(ROWS, NC, P).transpose(2, 1, 0).reshape(P, -1)
    A["bias"] = a["ada_b"].reshape(L, 48, P).transpose(2, 0, 1).reshape(P, -1)
    gains = np.stack([a["norm_mix"], a["norm_ffn"]], 1)
    A["gain"] = gains.reshape(2 * L, NC, P).transpose(2, 0, 1).reshape(P, -1)
    ones = np.ones((P, P), f)
    blk = np.kron(np.eye(2), np.ones((64, 64))).astype(f)
    rot = np.zeros((P, P), f)
    for h in range(2):
        for i in range(8):
            rot[64 * h + 8 + i, 64 * h + i] = -1.0
            rot[64 * h + i, 64 * h + 8 + i] = 1.0
    iota = np.tile(np.arange(P, dtype=f), (P, 1))
    gm = (np.arange(P)[:, None] // 16 == np.arange(8)[None]).astype(f)
    qkg = np.stack([np.concatenate([a["attn_q_norm"][0]] * 2), np.concatenate([a["attn_k_norm"][0]] * 2)], 1)
    A["consts"] = np.concatenate([ones, blk, np.eye(P, dtype=f), iota, gm, qkg], 1)
    A["rotm"] = rot
    k, p = np.arange(P)[:, None, None], np.arange(P)[None, None]
    A["spread"] = (k == 32 * np.arange(4)[None, :, None] + 16 * (p // 64)).astype(f).reshape(P, 4 * P)
    t = np.arange(T)
    sm = np.tile(((t < 256) | ((t - 256) % 4 != 0)).astype(f), (P, 1))
    A["smask"] = sm
    h0 = a["state_ssm"][0].reshape(SB, 2, PAIRS, P).transpose(3, 1, 2, 0).reshape(P, -1)
    A["h0d"] = np.concatenate([h0, a["ssm_d"][0].reshape(NC, P).transpose(1, 0)], 1)

    def both(w):
        one = np.broadcast_to(w.reshape(8, 8, 1, 64), (8, 8, 16, 64)).transpose(1, 2, 0, 3).reshape(P, 512)
        return np.concatenate([one, w.reshape(PAIRS, P).transpose(1, 0)], 1)

    A["lre"], A["lim"] = both(a["ssm_lam_re"][0]), both(a["ssm_lam_im"][0])
    A["ldt"] = both(np.broadcast_to(a["ssm_log_dt"][0][:, None], (64, 64)))
    for n, k in (("sbre", "ssm_b_re"), ("sbim", "ssm_b_im")):
        A[n] = a[k][0].reshape(8, 8, 64, 16).transpose(1, 3, 0, 2).reshape(P, 512)
    cc = []
    for k in ("ssm_c_re", "ssm_c_im"):
        w = a[k][0].reshape(PAIRS, 2, 16, 64).transpose(1, 3, 0, 2)
        z = np.zeros((2, 64, PAIRS, 2, 16), f)
        z[0, :, :, 0], z[1, :, :, 1] = w[0], w[1]
        cc.append(z.reshape(P, 1024))
    A["cri"] = np.concatenate(cc, 1)
    A["subk"] = a["peer_sub_keys"].transpose(0, 2, 4, 1, 3).reshape(L, P, PH * NKEYS)
    A["hqm"] = (np.arange(P)[:, None] // 32 == np.arange(4)[None]).astype(f)
    A["jsel"] = (np.arange(P)[:, None] % 32 == np.arange(32)[None]).astype(f)
    pos = np.concatenate([np.arange(256), PAST + (t[256:] - 256) % 4]).astype(f)
    inv = (f(500000.0) ** (-np.arange(8, dtype=f) / f(8))).astype(f)
    ang = (pos[:, None] * inv[None]).astype(f)
    cs, sn = np.ones((64, T), f), np.zeros((64, T), f)
    cs[0:8] = cs[8:16] = np.cos(ang).T
    sn[0:8] = sn[8:16] = np.sin(ang).T
    A["rope"] = np.concatenate([np.tile(cs, (2, 1)), np.tile(sn, (2, 1))], 1)
    NEG = f(-1e30)
    pm = []
    for qt in range(2):
        q, k = 128 * qt + np.arange(128)[:, None], np.arange(128 * (qt + 1))[None]
        for g in range(NG):
            ok = (k <= q) & ((q - k) % DIL[g] == 0) & ((q - k) // DIL[g] <= WIN[g] // DIL[g])
            pm.append(np.where(ok, f(0), NEG).astype(f))
    A["pmask"] = np.concatenate(pm, 1)
    row = np.arange(P)
    bq, tq = row[:, None] // 32, row[:, None] % 4
    m1 = np.arange(512)[None] % 4 == tq
    m0 = np.arange(128)[None] >= tq
    m2 = np.arange(256)[None] % 4 == tq
    smk = [m1, m0, m2]
    nb, nt = np.arange(32)[None] // 4, np.arange(32)[None] % 4
    for hf in range(2):
        smk += [(nb == bq + 4 * hf) & (nt <= tq)] + [(nb == bq + 4 * hf) & (nt == tq)] * 2
    A["smaskv"] = np.where(np.concatenate(smk, 1), f(0), NEG).astype(f)
    kc, vc = [], []
    for g, name in ((1, "cache_kv_w512"), (0, "cache_kv_w128"), (2, "cache_kv_w2048")):
        cch = a[name][0]
        if g == 2:
            cch = cch.reshape(SB, 2, 64, 16, H, E)[:, :, :, 0:4].reshape(SB, 2, 256, H, E)
        kc.append(cch[:, 0].reshape(SB, -1, HP, P).transpose(0, 3, 2, 1))
        vc.append(cch[:, 1].reshape(SB, -1, P, 512).transpose(0, 2, 1, 3))
    A["kc"] = np.concatenate(kc, 3).reshape(SB, P, HP * CK)
    A["vc"] = np.concatenate(vc, 2).reshape(SB, P, 7 * 512)

    nc = bacc.Bacc("TRN2", target_bir_lowering=False, num_devices=1)
    arrays, I, O = {}, {}, {}
    for n, w in A.items():
        w = ca(w)
        arrays["in_" + n] = w
        I[n] = nc.dram_tensor("in_" + n, w.shape, mb.dt.from_np(w.dtype), kind="ExternalInput").ap()
    for n, shape in (("st", (P, 2 * PAIRS * ROWS)), ("yT", (P, NC * T)), ("qk", (P, 24, T)), ("v", (P, 2, 3, 512)), ("v_s", (32, 3, 512))):
        O[n] = nc.dram_tensor("out_" + n, shape, mb.dt.float32, kind="ExternalOutput").ap()
    build(nc, I, O)
    r = run_bass_kernel_spmd(nc, [arrays], core_ids=[0]).results[0]
    y = r["out_yT"].reshape(P, NC, T).transpose(2, 1, 0).reshape(T, D)
    s = r["out_st"].reshape(P, 2, PAIRS, ROWS).transpose(3, 1, 2, 0).reshape(ROWS, 2, G64, SN)
    k = r["out_qk"].reshape(P, NG, 2, HP, T)[:, :, 1].transpose(1, 3, 2, 0).reshape(NG, T, H, E)
    vv = np.concatenate([r["out_v"].transpose(2, 1, 0, 3).reshape(NG, 256, H, E),
                         r["out_v_s"].transpose(1, 0, 2).reshape(NG, 32, H, E)], 1)
    kvp, kvs = [], []
    for g in range(NG):
        keep = min(WIN[g], 256)
        kvp.append(ca(np.stack([k[g, 256 - keep:256], vv[g, 256 - keep:256]])[None, None]))
        kvs.append(ca(np.stack([k[g, 256:T].reshape(SB, ST, H, E), vv[g, 256:T].reshape(SB, ST, H, E)], 1)[None]))
    return (ca(y[0:256][None]), ca(y[256:].reshape(SB, ST, D)), ca(s[0:1][None]), *kvp, ca(s[1:][None]), *kvs)
```
